# Optimizing a Trainium2 kernel written in Bass

```python
import jax, jax.numpy as jnp
from jax import lax
import numpy as np
import jax
import jax.numpy as jnp

D_MODEL = 1024
BATCH = 1
SEQ = 256
DEPTH = 2

MIX_WIDTH = D_MODEL // 2
N_BRANCH = 3
A_HEAD_DIM = 64
A_HEADS = MIX_WIDTH // A_HEAD_DIM
A_WIDTH = A_HEADS * A_HEAD_DIM
A_RANK_W = 64
A_RANK_A = 64
A_RANK_G = 128
A_GN_EPS = 64e-5
B_KEY_DIM = 128
B_VAL_DIM = 128
B_HEADS = MIX_WIDTH // B_VAL_DIM
B_WIDTH = B_HEADS * B_VAL_DIM
B_CHUNK = 64
C_HEAD_DIM = 64
C_HEADS = MIX_WIDTH // C_HEAD_DIM
C_KV_HEADS = 2
C_WIDTH = C_HEADS * C_HEAD_DIM
IDX_HEADS = 4
IDX_DIM = C_HEAD_DIM
TOPK_MAX = 256
Q_BLOCK = 128
ROPE_THETA = 10000.0
D_FF = 2816
CONV_WIDTH = 3
NORM_EPS = 1e-6

A_COLS = 3 * A_WIDTH + A_RANK_W + A_RANK_A + A_RANK_G
B_COLS = 4 * B_WIDTH
C_COLS = C_WIDTH + 2 * C_KV_HEADS * C_HEAD_DIM + IDX_HEADS * IDX_DIM + IDX_DIM + IDX_HEADS
GATE_COLS = N_BRANCH * D_MODEL
IN_COLS = A_COLS + B_COLS + C_COLS + GATE_COLS


F32 = jnp.float32

def _split(t, sizes):
    out, start = [], 0
    for s in sizes:
        out.append(t[..., start:start + s])
        start += s
    return out

def rms_norm(x, g):
    xf = x.astype(F32)
    y = xf * lax.rsqrt(jnp.mean(xf * xf, axis=-1, keepdims=True) + NORM_EPS)
    return (y * g.astype(F32)).astype(x.dtype)

def token_shift(p):
    return jnp.pad(p, ((0, 0), (1, 0), (0, 0)))[:, :-1]

def rope_tables(seq, dim):
    half = dim // 2
    inv_freq = ROPE_THETA ** (-jnp.arange(half, dtype=F32) * (2.0 / dim))
    ang = jnp.arange(seq, dtype=F32)[:, None] * inv_freq[None, :]
    return jnp.cos(ang), jnp.sin(ang)

def apply_rope(t, cos, sin):
    half = t.shape[-1] // 2
    tf = t.astype(F32)
    t1, t2 = tf[..., :half], tf[..., half:]
    c, s = cos[None, :, None, :], sin[None, :, None, :]
    return jnp.concatenate([t1 * c - t2 * s, t2 * c + t1 * s], axis=-1).astype(t.dtype)

def rwkv7_scan(r, w, k, v, a, b):
    bsz, _, heads, n = r.shape

    def step(state, inp):
        r_t, w_t, k_t, v_t, a_t, b_t = inp
        sa = jnp.einsum('bhij,bhj->bhi', state, a_t)
        state = (state * w_t[:, :, None, :] + sa[..., None] * b_t[:, :, None, :]
                 + v_t[..., None] * k_t[:, :, None, :])
        return state, jnp.einsum('bhij,bhj->bhi', state, r_t)

    xs = tuple(jnp.moveaxis(t, 1, 0) for t in (r, w, k, v, a, b))
    _, ys = lax.scan(step, jnp.zeros((bsz, heads, n, n), F32), xs)
    return jnp.moveaxis(ys, 0, 1)

def rwkv7_branch(p, mu, w0, w_up, a0, a_up, g_up, k_k, k_a, r_k, gn_g, gn_b):
    bsz, seq, _ = p.shape
    p = p + (token_shift(p) - p) * mu
    r, k, v, wd, ad, gd = _split(p, (A_WIDTH, A_WIDTH, A_WIDTH, A_RANK_W, A_RANK_A, A_RANK_G))
    w_log = -jax.nn.softplus(-(w0 + jnp.tanh(wd) @ w_up).astype(F32)) - 0.5
    decay = jnp.exp(-jnp.exp(w_log))
    a = jax.nn.sigmoid((a0 + ad @ a_up).astype(F32))
    g = jax.nn.sigmoid(gd) @ g_up

    def hd(t):
        return t.astype(F32).reshape(bsz, seq, A_HEADS, A_HEAD_DIM)

    kk = hd(k * k_k)
    kk = kk * lax.rsqrt(jnp.maximum(jnp.sum(kk * kk, axis=-1, keepdims=True), 1e-24))
    k_mod = hd(k.astype(F32) * (1.0 + (a - 1.0) * k_a.astype(F32)))
    r_h, v_h, a_h = hd(r), hd(v), hd(a)
    y = rwkv7_scan(r_h, hd(decay), k_mod, v_h, -kk, kk * a_h)
    mean = jnp.mean(y, axis=-1, keepdims=True)
    var = jnp.mean(jnp.square(y - mean), axis=-1, keepdims=True)
    y = ((y - mean) * lax.rsqrt(var + A_GN_EPS)).reshape(bsz, seq, A_WIDTH)
    y = y * gn_g.astype(F32) + gn_b.astype(F32)
    bonus = jnp.sum(r_h * k_mod * r_k.astype(F32), axis=-1, keepdims=True) * v_h
    y = y + bonus.reshape(bsz, seq, A_WIDTH)
    return (y * g.astype(F32)).astype(p.dtype)

def hgrn2_chunk_step(state, inp):
    q, k, g, v = inp
    b = jnp.cumsum(g, axis=2)
    causal = jnp.tril(jnp.ones((B_CHUNK, B_CHUNK), dtype=bool))
    diff = b[:, :, :, None, :] - b[:, :, None, :, :]
    decay = jnp.exp(jnp.where(causal[:, :, None], diff, -jnp.inf))
    scores = jnp.einsum('bhtd,bhsd,bhtsd->bhts', q, k, decay)
    o = (jnp.einsum('bhts,bhsv->bhtv', scores, v)
         + jnp.einsum('bhtd,bhdv->bhtv', q * jnp.exp(b), state))
    b_end = b[:, :, -1:, :]
    state = (state * jnp.exp(b_end)[:, :, 0, :, None]
             + jnp.einsum('bhsd,bhsv->bhdv', k * jnp.exp(b_end - b), v))
    return state, o

def hgrn2_branch(p, lb, gn_g):
    bsz, seq, _ = p.shape
    q, f, i, g = _split(p, (B_WIDTH, B_WIDTH, B_WIDTH, B_WIDTH))
    f = f.astype(F32)
    lb = lb.astype(F32)
    log_f = jnp.logaddexp(jnp.log(lb), jnp.log1p(-lb) + jax.nn.log_sigmoid(f))
    k_in = (1.0 - lb) * jax.nn.sigmoid(-f)
    n_chunk = seq // B_CHUNK

    def chunks(t, d):
        return t.astype(F32).reshape(bsz, n_chunk, B_CHUNK, B_HEADS, d).transpose(1, 0, 3, 2, 4)

    s0 = jnp.zeros((bsz, B_HEADS, B_KEY_DIM, B_VAL_DIM), F32)
    _, o = lax.scan(hgrn2_chunk_step, s0,
                    (chunks(q, B_KEY_DIM), chunks(k_in, B_KEY_DIM),
                     chunks(log_f, B_KEY_DIM), chunks(i, B_VAL_DIM)))
    o = o.transpose(1, 0, 3, 2, 4).reshape(bsz, seq, B_HEADS, B_VAL_DIM)
    o = o * lax.rsqrt(jnp.mean(o * o, axis=-1, keepdims=True) + NORM_EPS)
    o = o.reshape(bsz, seq, B_WIDTH) * gn_g.astype(F32) * jax.nn.silu(g.astype(F32))
    return o.astype(p.dtype)

def dsa_branch(p, cos, sin):
    bsz, seq, _ = p.shape
    kv_w = C_KV_HEADS * C_HEAD_DIM
    q, k, v, qi, ki, wi = _split(p, (C_WIDTH, kv_w, kv_w, IDX_HEADS * IDX_DIM, IDX_DIM, IDX_HEADS))
    q = apply_rope(q.reshape(bsz, seq, C_HEADS, C_HEAD_DIM), cos, sin)
    k = apply_rope(k.reshape(bsz, seq, C_KV_HEADS, C_HEAD_DIM), cos, sin)
    v = v.reshape(bsz, seq, C_KV_HEADS, C_HEAD_DIM)
    qi = apply_rope(qi.reshape(bsz, seq, IDX_HEADS, IDX_DIM), cos, sin)
    ki = apply_rope(ki[:, :, None, :], cos, sin)[:, :, 0, :].astype(F32)
    wi = wi.astype(F32) * (IDX_HEADS ** -0.5) * (IDX_DIM ** -0.5)
    n_blk = seq // Q_BLOCK
    k_sel = min(TOPK_MAX, seq // 4)
    group = C_HEADS // C_KV_HEADS
    s_pos = jnp.arange(seq)

    def blockify(t):
        return jnp.moveaxis(t.reshape(bsz, n_blk, Q_BLOCK, *t.shape[2:]), 1, 0)

    def attend(args):
        qb, qib, wib, t0 = args
        t_pos = t0 + jnp.arange(Q_BLOCK)
        causal = s_pos[None, :] <= t_pos[:, None]
        dots = jnp.einsum('bqhd,bsd->bqhs', qib.astype(F32), ki)
        score = jnp.einsum('bqhs,bqh->bqs', jax.nn.relu(dots), wib)
        score = jnp.where(causal[None], score, -jnp.inf)
        _, idx = lax.top_k(score, k_sel)
        kg = jax.vmap(lambda kb, ib: kb[ib])(k, idx)
        vg = jax.vmap(lambda vb, ib: vb[ib])(v, idx)
        valid = idx <= t_pos[None, :, None]
        qg = qb.reshape(bsz, Q_BLOCK, C_KV_HEADS, group, C_HEAD_DIM)
        logits = jnp.einsum('bqcgd,bqkcd->bqcgk', qg, kg).astype(F32) * (C_HEAD_DIM ** -0.5)
        logits = jnp.where(valid[:, :, None, None, :], logits, -jnp.inf)
        prob = jax.nn.softmax(logits, axis=-1).astype(vg.dtype)
        out = jnp.einsum('bqcgk,bqkcd->bqcgd', prob, vg)
        return out.reshape(bsz, Q_BLOCK, C_WIDTH)

    outs = lax.map(attend, (blockify(q), blockify(qi), blockify(wi),
                            jnp.arange(n_blk, dtype=jnp.int32) * Q_BLOCK))
    return jnp.moveaxis(outs, 0, 1).reshape(bsz, seq, C_WIDTH).astype(p.dtype)

def conv_glu(h, w_up, conv_w, conv_b, w_down):
    seq = h.shape[1]
    up = h @ w_up
    up_pad = jnp.pad(up, ((0, 0), (CONV_WIDTH - 1, 0), (0, 0)))
    c = conv_b
    for j in range(CONV_WIDTH):
        c = c + conv_w[j] * up_pad[:, j:j + seq]
    gate, val = _split(c, (D_FF, D_FF))
    return (jax.nn.silu(gate) * val) @ w_down

def first_inputs(seed: int = 0) -> dict:
    key = jax.random.key(seed)
    ks = iter(jax.random.split(key, 32))

    def nrm(shape, scale):
        return jax.random.normal(next(ks), shape, F32) * scale

    def uni(shape, lo, hi):
        return jax.random.uniform(next(ks), shape, F32, lo, hi)

    f2 = 2 * D_FF
    return {
        'x': nrm((BATCH, SEQ, D_MODEL), 1.0),
        'norm_mix_g': 1.0 + nrm((DEPTH, D_MODEL), 0.02),
        'w_in': nrm((DEPTH, D_MODEL, IN_COLS), D_MODEL ** -0.5),
        'a_mu': uni((DEPTH, A_COLS), 0.0, 1.0),
        'a_w0': uni((DEPTH, A_WIDTH), -5.0, 0.0),
        'a_w_up': nrm((DEPTH, A_RANK_W, A_WIDTH), 0.5 * A_RANK_W ** -0.5),
        'a_a0': nrm((DEPTH, A_WIDTH), 0.5),
        'a_a_up': nrm((DEPTH, A_RANK_A, A_WIDTH), 0.5 * A_RANK_A ** -0.5),
        'a_g_up': nrm((DEPTH, A_RANK_G, A_WIDTH), A_RANK_G ** -0.5),
        'a_k_k': 0.85 + nrm((DEPTH, A_WIDTH), 0.05),
        'a_k_a': 1.0 + nrm((DEPTH, A_WIDTH), 0.05),
        'a_r_k': nrm((DEPTH, A_HEADS, A_HEAD_DIM), 0.1),
        'a_gn_g': 1.0 + nrm((DEPTH, A_WIDTH), 0.02),
        'a_gn_b': nrm((DEPTH, A_WIDTH), 0.02),
        'b_lb_logits': nrm((DEPTH, B_HEADS * B_KEY_DIM), 1.0),
        'b_gn_g': 1.0 + nrm((DEPTH, B_WIDTH), 0.02),
        'w_branch': nrm((DEPTH, N_BRANCH, MIX_WIDTH, D_MODEL), MIX_WIDTH ** -0.5),
        'w_o': nrm((DEPTH, D_MODEL, D_MODEL), D_MODEL ** -0.5),
        'norm_ffn_g': 1.0 + nrm((DEPTH, D_MODEL), 0.02),
        'w_up': nrm((DEPTH, D_MODEL, f2), D_MODEL ** -0.5),
        'conv_w': nrm((DEPTH, CONV_WIDTH, f2), CONV_WIDTH ** -0.5),
        'conv_b': nrm((DEPTH, f2), 0.02),
        'w_down': nrm((DEPTH, D_FF, D_MODEL), D_FF ** -0.5),
        'norm_final_g': 1.0 + nrm((D_MODEL,), 0.02),
    }

def first_block(x, norm_mix_g, w_in, a_mu, a_w0, a_w_up, a_a0, a_a_up, a_g_up, a_k_k, a_k_a,
              a_r_k, a_gn_g, a_gn_b, b_lb_logits, b_gn_g, w_branch, w_o, norm_ffn_g,
              w_up, conv_w, conv_b, w_down, norm_final_g):
    bsz, seq, _ = x.shape
    cos, sin = rope_tables(seq, C_HEAD_DIM)
    lb_cum = jnp.cumsum(jax.nn.softmax(b_lb_logits.astype(F32), axis=0), axis=0)
    lower_bounds = lb_cum - lb_cum[0]
    h = x
    for layer in range(DEPTH):
        u = rms_norm(h, norm_mix_g[layer])
        p = u @ w_in[layer]
        p_a, p_b, p_c, p_gate = _split(p, (A_COLS, B_COLS, C_COLS, GATE_COLS))
        y_a = rwkv7_branch(p_a, a_mu[layer], a_w0[layer], a_w_up[layer], a_a0[layer],
                           a_a_up[layer], a_g_up[layer], a_k_k[layer], a_k_a[layer],
                           a_r_k[layer], a_gn_g[layer], a_gn_b[layer])
        y_b = hgrn2_branch(p_b, lower_bounds[layer], b_gn_g[layer])
        y_c = dsa_branch(p_c, cos, sin)
        ys = jnp.stack([y_a, y_b, y_c], axis=2)
        branch = jnp.einsum('bsnc,ncd->bsnd', ys, w_branch[layer])
        gates = jax.nn.sigmoid(p_gate.reshape(bsz, seq, N_BRANCH, D_MODEL))
        merged = jnp.sum(gates * branch, axis=2)
        h = h + merged @ w_o[layer]
        u = rms_norm(h, norm_ffn_g[layer])
        h = h + conv_glu(u, w_up[layer], conv_w[layer], conv_b[layer], w_down[layer])
    return rms_norm(h, norm_final_g)


FOX_HEADS = 8
FOX_HEAD_DIM = 64
MLA_HEADS = 8
MLA_Q_RANK = 256
MLA_KV_RANK = 128
MLA_NOPE_DIM = 64
MLA_ROPE_DIM = 32
MLA_V_DIM = 64
DN_HEADS = 8
DN_HEAD_DIM = 64
DN_CONV_WIDTH = 4
DN_CHUNK = 64

FOX_WIDTH = FOX_HEADS * FOX_HEAD_DIM
MLA_QK_DIM = MLA_NOPE_DIM + MLA_ROPE_DIM
MLA_WIDTH = MLA_HEADS * MLA_V_DIM
DN_WIDTH = DN_HEADS * DN_HEAD_DIM
IN_WIDTHS = (FOX_WIDTH, FOX_WIDTH, FOX_WIDTH, FOX_HEADS,
             MLA_Q_RANK, MLA_KV_RANK, MLA_ROPE_DIM,
             DN_WIDTH, DN_WIDTH, DN_WIDTH, DN_WIDTH, DN_HEADS, DN_HEADS,
             N_BRANCH * D_MODEL)
N_IN = sum(IN_WIDTHS)


def rmsnorm(x, gain):
    xf = x.astype(jnp.float32)
    y = xf * lax.rsqrt(jnp.mean(xf * xf, axis=-1, keepdims=True) + NORM_EPS)
    return (y * gain.astype(jnp.float32)).astype(x.dtype)

def l2norm(x):
    xf = x.astype(jnp.float32)
    return xf * lax.rsqrt(jnp.sum(xf * xf, axis=-1, keepdims=True) + NORM_EPS)

def swiglu(h, w_gu, w_down):
    gate, up = jnp.split(h @ w_gu, 2, axis=-1)
    return (jax.nn.silu(gate) * up) @ w_down

def rope_tables_2(positions):
    half = MLA_ROPE_DIM // 2
    inv_freq = ROPE_THETA ** (-jnp.arange(half, dtype=jnp.float32) / half)
    ang = positions.astype(jnp.float32)[..., None] * inv_freq
    return jnp.cos(ang)[:, :, None, :], jnp.sin(ang)[:, :, None, :]

def apply_rope_2(x, cos, sin):
    x1, x2 = jnp.split(x.astype(jnp.float32), 2, axis=-1)
    return jnp.concatenate([x1 * cos - x2 * sin, x2 * cos + x1 * sin], axis=-1).astype(x.dtype)

def causal_short_conv(x, w):
    width = w.shape[0]
    s = x.shape[1]
    xp = jnp.pad(x, ((0, 0), (width - 1, 0), (0, 0)))
    return sum(xp[:, i:i + s] * w[i] for i in range(width))

def block_causal_attention(q, k, v, scale, log_decay_cum=None):
    b, s, h, dqk = q.shape
    dv = v.shape[-1]
    nb = s // Q_BLOCK
    q_blocks = q.reshape(b, nb, Q_BLOCK, h, dqk).transpose(1, 0, 3, 2, 4)
    k_pos = jnp.arange(s)
    xs = (jnp.arange(nb), q_blocks)
    if log_decay_cum is not None:
        c = log_decay_cum.astype(jnp.float32).transpose(0, 2, 1)
        c_blocks = c.reshape(b, h, nb, Q_BLOCK).transpose(2, 0, 1, 3)
        xs = (jnp.arange(nb), q_blocks, c_blocks)

    def one_block(args):
        idx, q_blk = args[0], args[1]
        logits = jnp.einsum('bhqd,bkhd->bhqk', q_blk, k).astype(jnp.float32) * scale
        if log_decay_cum is not None:
            logits = logits + args[2][..., :, None] - c[:, :, None, :]
        q_pos = idx * Q_BLOCK + jnp.arange(Q_BLOCK)
        logits = jnp.where(k_pos[None, :] <= q_pos[:, None], logits, -jnp.inf)
        p = jax.nn.softmax(logits, axis=-1).astype(v.dtype)
        return jnp.einsum('bhqk,bkhd->bqhd', p, v)

    out = lax.map(one_block, xs)
    return out.transpose(1, 0, 2, 3, 4).reshape(b, s, h, dv)

def chunk_gated_delta_rule(q, k, v, g, beta):
    b, s, h, dk = q.shape
    dv = v.shape[-1]
    nc = s // DN_CHUNK

    def to_chunks(t):
        return jnp.moveaxis(t.reshape((b, nc, DN_CHUNK, h) + t.shape[3:]), 3, 2)

    q, k, v, g, beta = (to_chunks(t) for t in (q, k, v, g, beta))
    gc = jnp.cumsum(g, axis=-1)
    idx = jnp.arange(DN_CHUNK)
    causal = idx[:, None] >= idx[None, :]
    strict = idx[:, None] > idx[None, :]
    decay_mat = jnp.exp(jnp.where(causal, gc[..., :, None] - gc[..., None, :], -jnp.inf))
    k_beta = k * beta[..., None]
    v_beta = v * beta[..., None]
    m = jnp.where(strict, jnp.einsum('bnhid,bnhjd->bnhij', k_beta, k) * decay_mat, 0.0)
    eye = jnp.eye(DN_CHUNK, dtype=jnp.float32)
    t_inv = lax.linalg.triangular_solve(eye + m, jnp.broadcast_to(eye, m.shape),
                                        left_side=True, lower=True, unit_diagonal=True)
    w = t_inv @ (k_beta * jnp.exp(gc)[..., None])
    u = t_inv @ v_beta
    qk = jnp.einsum('bnhid,bnhjd->bnhij', q, k) * decay_mat
    q_dec = q * jnp.exp(gc)[..., None]
    k_dec = k * jnp.exp(gc[..., -1:] - gc)[..., None]
    g_last = jnp.exp(gc[..., -1])

    def step(state, xs_c):
        w_c, u_c, qk_c, q_c, k_c, gl = xs_c
        v_new = u_c - w_c @ state
        o_c = q_c @ state + qk_c @ v_new
        state = state * gl[..., None, None] + jnp.einsum('bhcd,bhce->bhde', k_c, v_new)
        return state, o_c

    xs = tuple(jnp.moveaxis(t, 1, 0) for t in (w, u, qk, q_dec, k_dec, g_last))
    state0 = jnp.zeros((b, h, dk, dv), jnp.float32)
    _, o = lax.scan(step, state0, xs)
    return o.transpose(1, 0, 3, 2, 4).reshape(b, s, h, dv)

def hybrid_mixer(h, cos, sin, w_in, b_gate, fox_b_f, mla_q_norm, mla_w_uq, mla_kv_norm, mla_w_ukv,
                 dn_conv_w, dn_a_log, dn_dt_bias, dn_o_norm, w_br_fox, w_br_mla, w_br_dn, w_out):
    b, s, _ = h.shape
    f32 = jnp.float32
    splits = np.cumsum(IN_WIDTHS)[:-1]
    (fox_q, fox_k, fox_v, fox_f, mla_cq, mla_ckv, mla_kr,
     dn_q, dn_k, dn_v, dn_z, dn_b, dn_a, gate_logits) = jnp.split(h @ w_in, splits, axis=-1)

    fox_shape = (b, s, FOX_HEADS, FOX_HEAD_DIM)
    log_f = jax.nn.log_sigmoid(fox_f.astype(f32) + fox_b_f.astype(f32))
    fox_out = block_causal_attention(fox_q.reshape(fox_shape), fox_k.reshape(fox_shape),
                                     fox_v.reshape(fox_shape), FOX_HEAD_DIM ** -0.5,
                                     jnp.cumsum(log_f, axis=1))
    y_fox = fox_out.reshape(b, s, FOX_WIDTH) @ w_br_fox

    q = (rmsnorm(mla_cq, mla_q_norm) @ mla_w_uq).reshape(b, s, MLA_HEADS, MLA_QK_DIM)
    q_nope, q_rope = jnp.split(q, [MLA_NOPE_DIM], axis=-1)
    kv = (rmsnorm(mla_ckv, mla_kv_norm) @ mla_w_ukv).reshape(b, s, MLA_HEADS, MLA_NOPE_DIM + MLA_V_DIM)
    k_nope, mla_v = jnp.split(kv, [MLA_NOPE_DIM], axis=-1)
    k_rope = apply_rope_2(mla_kr[:, :, None, :], cos, sin)
    q_full = jnp.concatenate([q_nope, apply_rope_2(q_rope, cos, sin)], axis=-1)
    k_full = jnp.concatenate([k_nope, jnp.broadcast_to(k_rope, (b, s, MLA_HEADS, MLA_ROPE_DIM))], axis=-1)
    mla_out = block_causal_attention(q_full, k_full, mla_v, MLA_QK_DIM ** -0.5)
    y_mla = mla_out.reshape(b, s, MLA_WIDTH) @ w_br_mla

    qkv = jax.nn.silu(causal_short_conv(jnp.concatenate([dn_q, dn_k, dn_v], axis=-1), dn_conv_w))
    cq, ck, cv = jnp.split(qkv, 3, axis=-1)
    dn_shape = (b, s, DN_HEADS, DN_HEAD_DIM)
    q_dn = l2norm(cq.reshape(dn_shape)) * (DN_HEAD_DIM ** -0.5)
    k_dn = l2norm(ck.reshape(dn_shape))
    v_dn = cv.reshape(dn_shape).astype(f32)
    beta = jax.nn.sigmoid(dn_b.astype(f32))
    g = -jnp.exp(dn_a_log.astype(f32)) * jax.nn.softplus(dn_a.astype(f32) + dn_dt_bias.astype(f32))
    o = chunk_gated_delta_rule(q_dn, k_dn, v_dn, g, beta)
    o = rmsnorm(o, dn_o_norm).astype(h.dtype) * jax.nn.silu(dn_z.reshape(dn_shape))
    y_dn = o.reshape(b, s, DN_WIDTH) @ w_br_dn

    g_fox, g_mla, g_dn = jnp.split(jax.nn.sigmoid(gate_logits + b_gate), N_BRANCH, axis=-1)
    return (g_fox * y_fox + g_mla * y_mla + g_dn * y_dn) @ w_out

def second_inputs(seed: int = 0) -> dict:
    key = jax.random.key(seed)
    ks = iter(list(jax.random.split(key, 32)))
    f32 = jnp.float32
    L = DEPTH

    def nrm(shape, scale):
        return jax.random.normal(next(ks), shape, f32) * scale

    def gain(shape):
        return 1.0 + nrm(shape, 0.1)

    x = jax.random.normal(next(ks), (BATCH, SEQ, D_MODEL), f32)
    positions = (jnp.arange(SEQ, dtype=jnp.int32)[None, :]
                 + jax.random.randint(next(ks), (BATCH, 1), 0, 1024, dtype=jnp.int32))
    ffn1_norm = gain((L, D_MODEL))
    ffn1_w_gu = nrm((L, D_MODEL, 2 * D_FF), D_MODEL ** -0.5)
    ffn1_w_down = nrm((L, D_FF, D_MODEL), D_FF ** -0.5)
    mix_norm = gain((L, D_MODEL))
    w_in = nrm((L, D_MODEL, N_IN), D_MODEL ** -0.5)
    b_gate = nrm((L, N_BRANCH * D_MODEL), 0.1)
    fox_b_f = 4.0 + nrm((L, FOX_HEADS), 0.5)
    mla_q_norm = gain((L, MLA_Q_RANK))
    mla_w_uq = nrm((L, MLA_Q_RANK, MLA_HEADS * MLA_QK_DIM), MLA_Q_RANK ** -0.5)
    mla_kv_norm = gain((L, MLA_KV_RANK))
    mla_w_ukv = nrm((L, MLA_KV_RANK, MLA_HEADS * (MLA_NOPE_DIM + MLA_V_DIM)), MLA_KV_RANK ** -0.5)
    dn_conv_w = nrm((L, DN_CONV_WIDTH, 3 * DN_WIDTH), DN_CONV_WIDTH ** -0.5)
    dn_a_log = jnp.log(jax.random.uniform(next(ks), (L, DN_HEADS), f32, 1.0, 16.0))
    dt = jnp.exp(jax.random.uniform(next(ks), (L, DN_HEADS), f32,
                                    float(np.log(1e-3)), float(np.log(1e-1))))
    dn_dt_bias = dt + jnp.log(-jnp.expm1(-dt))
    dn_o_norm = gain((L, DN_HEAD_DIM))
    w_br_fox = nrm((L, FOX_WIDTH, D_MODEL), FOX_WIDTH ** -0.5)
    w_br_mla = nrm((L, MLA_WIDTH, D_MODEL), MLA_WIDTH ** -0.5)
    w_br_dn = nrm((L, DN_WIDTH, D_MODEL), DN_WIDTH ** -0.5)
    w_out = nrm((L, D_MODEL, D_MODEL), D_MODEL ** -0.5)
    ffn2_norm = gain((L, D_MODEL))
    ffn2_w_gu = nrm((L, D_MODEL, 2 * D_FF), D_MODEL ** -0.5)
    ffn2_w_down = nrm((L, D_FF, D_MODEL), D_FF ** -0.5)
    final_norm = gain((D_MODEL,))
    return {'x': x, 'positions': positions,
            'ffn1_norm': ffn1_norm, 'ffn1_w_gu': ffn1_w_gu, 'ffn1_w_down': ffn1_w_down,
            'mix_norm': mix_norm, 'w_in': w_in, 'b_gate': b_gate, 'fox_b_f': fox_b_f,
            'mla_q_norm': mla_q_norm, 'mla_w_uq': mla_w_uq, 'mla_kv_norm': mla_kv_norm, 'mla_w_ukv': mla_w_ukv,
            'dn_conv_w': dn_conv_w, 'dn_a_log': dn_a_log, 'dn_dt_bias': dn_dt_bias, 'dn_o_norm': dn_o_norm,
            'w_br_fox': w_br_fox, 'w_br_mla': w_br_mla, 'w_br_dn': w_br_dn, 'w_out': w_out,
            'ffn2_norm': ffn2_norm, 'ffn2_w_gu': ffn2_w_gu, 'ffn2_w_down': ffn2_w_down,
            'final_norm': final_norm}

def second_block(x, positions, ffn1_norm, ffn1_w_gu, ffn1_w_down, mix_norm, w_in, b_gate, fox_b_f,
              mla_q_norm, mla_w_uq, mla_kv_norm, mla_w_ukv, dn_conv_w, dn_a_log, dn_dt_bias, dn_o_norm,
              w_br_fox, w_br_mla, w_br_dn, w_out, ffn2_norm, ffn2_w_gu, ffn2_w_down, final_norm):
    cos, sin = rope_tables_2(positions)
    for l in range(DEPTH):
        x = x + 0.5 * swiglu(rmsnorm(x, ffn1_norm[l]), ffn1_w_gu[l], ffn1_w_down[l])
        x = x + hybrid_mixer(rmsnorm(x, mix_norm[l]), cos, sin, w_in[l], b_gate[l], fox_b_f[l],
                             mla_q_norm[l], mla_w_uq[l], mla_kv_norm[l], mla_w_ukv[l],
                             dn_conv_w[l], dn_a_log[l], dn_dt_bias[l], dn_o_norm[l],
                             w_br_fox[l], w_br_mla[l], w_br_dn[l], w_out[l])
        x = x + 0.5 * swiglu(rmsnorm(x, ffn2_norm[l]), ffn2_w_gu[l], ffn2_w_down[l])
    return rmsnorm(x, final_norm)


def setup_inputs(seed=0):
    out = dict(first_inputs(seed))
    for name, value in second_inputs(seed + 1).items():
        if name != "x":
            out[name + "_2"] = value
    return out


def reference(
    x, norm_mix_g, w_in, a_mu, a_w0, a_w_up, a_a0, a_a_up, a_g_up, a_k_k, a_k_a, a_r_k, a_gn_g,
    a_gn_b, b_lb_logits, b_gn_g, w_branch, w_o, norm_ffn_g, w_up, conv_w, conv_b, w_down,
    norm_final_g, positions_2, ffn1_norm_2, ffn1_w_gu_2, ffn1_w_down_2, mix_norm_2, w_in_2,
    b_gate_2, fox_b_f_2, mla_q_norm_2, mla_w_uq_2, mla_kv_norm_2, mla_w_ukv_2, dn_conv_w_2,
    dn_a_log_2, dn_dt_bias_2, dn_o_norm_2, w_br_fox_2, w_br_mla_2, w_br_dn_2, w_out_2,
    ffn2_norm_2, ffn2_w_gu_2, ffn2_w_down_2, final_norm_2,
):
    x = first_block(
        x, norm_mix_g, w_in, a_mu, a_w0, a_w_up, a_a0, a_a_up, a_g_up, a_k_k, a_k_a, a_r_k,
        a_gn_g, a_gn_b, b_lb_logits, b_gn_g, w_branch, w_o, norm_ffn_g, w_up, conv_w, conv_b,
        w_down, norm_final_g,
    )
    return second_block(
        x, positions_2, ffn1_norm_2, ffn1_w_gu_2, ffn1_w_down_2, mix_norm_2, w_in_2, b_gate_2,
        fox_b_f_2, mla_q_norm_2, mla_w_uq_2, mla_kv_norm_2, mla_w_ukv_2, dn_conv_w_2,
        dn_a_log_2, dn_dt_bias_2, dn_o_norm_2, w_br_fox_2, w_br_mla_2, w_br_dn_2, w_out_2,
        ffn2_norm_2, ffn2_w_gu_2, ffn2_w_down_2, final_norm_2,
    )


_drawn_inputs = setup_inputs


def setup_inputs(seed=0):
    import zlib

    import numpy as np

    out = dict(_drawn_inputs(seed))
    spreads = {}
    factors = {'a_gn_g': 3.747,
     'a_gn_b': 3.289,
     'b_gn_g': 3.392,
     'b_gate_2': 2.734,
     'mla_q_norm_2': 4.513}
    for name, (base, spread) in spreads.items():
        noise = np.random.default_rng([zlib.crc32(name.encode()), seed]).standard_normal(out[name].shape)
        drawn = base * np.exp(spread * noise) if base else spread * noise
        out[name] = jnp.asarray(drawn.astype(out[name].dtype))
    for name, factor in factors.items():
        out[name] = (out[name] * factor).astype(out[name].dtype)
    return out
```

```python
from contextlib import ExitStack

import numpy as np
import concourse.bass as bass
from concourse import mybir

F32 = mybir.dt.float32
I32 = mybir.dt.int32
ALU = mybir.AluOpType
ACT = mybir.ActivationFunctionType
AX_X = mybir.AxisListType.X

P = 128
T = 256
NBLK = T // P
D = 1024
KT = D // P
DEPTH = 2
D_FF = 2816
MIX = 512
MT_ = MIX // P
HEADS = 8
HD = 64
RING = 3
SLOT = 4096
LEVELS = (1, 2, 4, 8, 16, 32, 64)
NEG = -1e30
TAKEN = -3e38
TOPK = min(256, T // 4)
EPS = 1e-6
GN_EPS = 64e-5
KAPPA = float(np.exp(-0.5))

A_R, A_K, A_V, A_WA, A_G = 0, 4, 8, 12, 13
B_Q, B_F, B_I, B_G = 14, 18, 22, 26
C_Q, C_K, C_QI, C_KI, C_V, C_WI = 30, 34, 36, 38, 39, 40
X_Q, X_K, X_V, X_F, X_CQ, X_CKV, X_KR, X_B, X_A, X_DQ, X_DK, X_DV, X_DZ = (
    0, 4, 8, 12, 13, 15, 16, 17, 18, 19, 23, 27, 31)
P_TILES = 41

PAR1 = [("mix_g", 8), ("mu", 14), ("w0", 4), ("a0", 4), ("k_k", 4), ("k_a", 4), ("r_k", 4),
        ("gn_g", 4), ("gn_b", 4), ("lb0", 4), ("lb1", 4), ("b_gn_g", 4), ("ffn_g", 8),
        ("conv_w", 132), ("conv_b", 44), ("layer", 1), ("fin_g", 8)]
PAR2 = [("ffn1_g", 8), ("mix_g", 8), ("ffn2_g", 8), ("fin_g", 8), ("b_gate", 24), ("q_norm", 2),
        ("kv_norm", 1), ("dn_conv", 48), ("o_norm", 1), ("fox_b", 1), ("a_log", 1), ("dt_bias", 1)]


def columns(table):
    at, out = 0, {}
    for name, n in table:
        out[name] = at
        at += n
    return out, at


C1, N_PAR1 = columns(PAR1)
C2, N_PAR2 = columns(PAR2)
N_PAR = max(N_PAR1, N_PAR2)

CONSTS = [("ident", P), ("ones", T), ("bones", P), ("rot", P), ("rotm", P), ("cbias", P),
          ("cbiasT", P), ("strict", P), ("incl", P), ("levels", len(LEVELS) * P),
          ("cos", T), ("sin", T), ("hsel", MT_ * P), ("invf", 1)]
CC, N_CONST = columns(CONSTS)

JOBS1 = ([(8, 512)] * 3 + [(8, 256)] + [(8, 512)] * 4 + [(8, 512)] * 2 + [(8, 260)]
         + [(8, 512)] * 6 + [(4, 1024)] * 3 + [(4, 1024)] * 2 + [(8, 512)] * 11
         + [(4, 1024)] * 5 + [(2, 1024)])
JOBS2 = ([(8, 512)] * 11 + [(4, 1024)] * 5 + [(2, 1024)] + [(8, 512)] * 3 + [(8, 440)]
         + [(8, 512)] * 4 + [(8, 512)] * 6 + [(4, 1024)] * 3 + [(4, 1024)] * 2
         + [(8, 512)] * 11 + [(4, 1024)] * 5 + [(2, 1024)])


def const_array():
    c = np.zeros((P, N_CONST), np.float32)
    i = np.arange(P)
    c[:, CC["ident"]:][:, :P] = np.eye(P)
    c[:, CC["ones"]:][:, :T] = 1.0
    c[:, CC["bones"]:][:, :P] = (i[:, None] // HD == i[None, :] // HD)
    rot = np.zeros((P, P))
    rotm = np.zeros((P, P))
    for m in range(P):
        if m % HD < HD // 2:
            rot[m + HD // 2, m] = -1.0
        else:
            rot[m - HD // 2, m] = 1.0
    for m in range(16):
        rotm[HD + 16 + m, HD + m] = -1.0
        rotm[HD + m, HD + 16 + m] = 1.0
    c[:, CC["rot"]:][:, :P] = rot
    c[:, CC["rotm"]:][:, :P] = rotm
    c[:, CC["cbias"]:][:, :P] = np.where(i[None, :] > i[:, None], NEG, 0.0)
    c[:, CC["cbiasT"]:][:, :P] = np.where(i[:, None] > i[None, :], NEG, 0.0)
    c[:, CC["strict"]:][:, :P] = i[:, None] < i[None, :]
    c[:, CC["incl"]:][:, :P] = i[:, None] <= i[None, :]
    for n, b in enumerate(LEVELS):
        s, t = i[:, None], i[None, :]
        m = (s // (2 * b) == t // (2 * b)) & (s % (2 * b) < b) & (t % (2 * b) >= b)
        c[:, CC["levels"] + n * P:][:, :P] = m
    freq = np.float32(10000.0) ** (-np.arange(HD // 2, dtype=np.float32) * np.float32(2.0 / HD))
    ang = np.arange(T, dtype=np.float32)[None, :] * freq[i % (HD // 2)][:, None]
    c[:, CC["cos"]:][:, :T] = np.cos(ang)
    c[:, CC["sin"]:][:, :T] = np.sin(ang)
    for n in range(MT_):
        for h in range(HEADS):
            c[h, CC["hsel"] + n * P:][:P] = (i // HD + 2 * n == h)
    invf = np.float32(10000.0) ** (-np.arange(16, dtype=np.float32) / np.float32(16))
    c[HD:HD + 32, CC["invf"]] = np.concatenate([invf, invf])
    return c


class Signals:

    def __init__(self, nc):
        self.nc, self.by_name, self.stack = nc, {}, ExitStack()

    def __call__(self, name):
        if name not in self.by_name:
            self.by_name[name] = self.stack.enter_context(self.nc.semaphore(name))
        return self.by_name[name]

    def end(self):
        nums = sorted(s.num for s in self.by_name.values())
        assert nums == list(range(nums[0], nums[-1] + 1)), nums
        self.nc.all_engine_barrier(sems_to_clear=range(nums[0], nums[-1] + 1))
        self.stack.close()


def linker(eng, sig, own):
    count = {}

    def say(ins, name):
        count[name] = count.get(name, 0) + 1
        ins.then_inc(sig(name), 1)
        eng.wait_ge(sig(name), count[name])

    def link(ins):
        say(ins, own)

    def need(name, n=1):
        eng.wait_ge(sig(name), n)

    return link, say, need


class Memory:

    def __init__(self, nc, ctx):
        def sb(name, shape):
            return ctx.enter_context(nc.sbuf_tensor(name, shape, F32))

        self.ring = sb("weight_ring", [P, RING, SLOT])
        self.proj = sb("projected", [P, P_TILES, T])
        self.scratch = sb("scratch", [P, 64 * 256])
        self.h = sb("residual", [P, KT, T])
        self.u = sb("normed", [P, KT, T])
        self.y = sb("branch_out", [P, 3 * MT_, T])
        self.par = sb("parameters", [P, N_PAR])
        self.small_w = sb("small_weights", [P, 2560])
        self.const = sb("constants", [P, N_CONST])
        self.mla_cos = sb("mla_cos", [P, T])
        self.mla_sin = sb("mla_sin", [P, T])
        self.ps = ctx.enter_context(nc.psum_tensor("banks", [P, 8, 512], F32))

    def c(self, name, width=P):
        return self.const[:, CC[name]:CC[name] + width]


class Cutter:

    def __init__(self, buffer):
        self.buffer, self.at = buffer, 0

    def __call__(self, *shape):
        n = int(np.prod(shape))
        part = self.buffer[:, self.at:self.at + n]
        self.at += n
        assert self.at <= self.buffer.shape[1]
        if len(shape) == 1:
            return part
        names = "abcd"[:len(shape)]
        return part.rearrange("p (%s) -> p %s" % (" ".join(names), " ".join(names)),
                              **dict(zip(names, shape)))


class Stream:

    def __init__(self, mem, dram, jobs, full):
        self.mem, self.dram, self.jobs, self.full = mem, dram, jobs, full

    def load(self, sp, layer, g):
        nk, n = self.jobs[g]
        sp.dma_start(self.mem.ring[:, g % RING, 0:nk * n],
                     self.dram[bass.ds(layer, 1), g, :, 0:nk * n].rearrange("a p n -> (a p) n")
                     ).then_inc(self.full[g % RING], 16)

    def load_behind(self, sp, sig, layer, done):
        for g, value in done:
            if g + RING < len(self.jobs):
                sp.wait_ge(sig("tiles_done"), value)
                self.load(sp, layer, g + RING)

    def arrived(self, pe, g):
        pe.wait_ge(self.full[g % RING], 16 * (g // RING + 1))

    def weight(self, g, k, c0, m):
        n = self.jobs[g][1]
        return self.mem.ring[:, g % RING, k * n + c0:k * n + c0 + m]



def norm_squares(dve, nc, mem, sq, say):
    say(nc.vector.tensor_tensor(sq, mem.h[:], mem.h[:], ALU.mult), "squares")


def norm_sum(pe, mem, sq, sig, bank):
    pe.wait_ge(sig("squares"), 1)
    for k in range(KT):
        mm = pe.matmul(mem.ps[:, bank, 0:T], mem.c("ones"), sq[:, k, :],
                       start=(k == 0), stop=(k == KT - 1))
    mm.then_inc(sig("square_sum"), 1)


def norm_mean(dve, nc, mem, rstd, sig, say, bank):
    dve.wait_ge(sig("square_sum"), 1)
    say(nc.vector.tensor_scalar(rstd, mem.ps[:, bank, 0:T], 1.0 / D, EPS, ALU.mult, ALU.add),
        "mean_square")


def norm_root(act, nc, rstd, sig, say):
    act.wait_ge(sig("mean_square"), 1)
    say(nc.scalar.activation(rstd, rstd, ACT.Sqrt), "root")


def norm_scale(dve, nc, mem, rstd, gain, out, sig, link):
    dve.wait_ge(sig("root"), 1)
    link(nc.vector.reciprocal(rstd, rstd))
    for k in range(KT):
        ins = nc.vector.scalar_tensor_tensor(out=out[:, k, :], in0=mem.h[:, k, :],
                                             scalar=mem.par[:, gain + k:gain + k + 1], in1=rstd,
                                             op0=ALU.mult, op1=ALU.mult)
        ins.then_inc(sig("normed"), 1)



def project_stage(nc, mem, sig, stream, layer, groups, first, gain, loads):
    cut = Cutter(mem.scratch)
    sq, rstd = cut(KT, T), cut(T)
    BANKS = 4
    done = [(g, 1 + max(i for i, grp in enumerate(groups) if any(t[0] == g for t in grp)))
            for g in sorted({t[0] for grp in groups for t in grp})]

    with nc.Block() as block:
        @block.sync
        def _(sp):
            for n, load in enumerate(loads):
                load(sp).then_inc(sig("params"), 16)
            for g in range(first, first + RING):
                if first == 0 or g >= first + RING:
                    stream.load(sp, layer, g)
            stream.load_behind(sp, sig, layer, done)

        @block.vector
        def _(dve):
            link, say, need = linker(dve, sig, "dve_ops")
            norm_squares(dve, nc, mem, sq, say)
            norm_mean(dve, nc, mem, rstd, sig, say, 7)
            if loads:
                need("params", 16 * len(loads))
            norm_scale(dve, nc, mem, rstd, gain, mem.u, sig, link)

        @block.scalar
        def _(act):
            link, say, need = linker(act, sig, "act_ops")
            norm_root(act, nc, rstd, sig, say)
            for i, grp in enumerate(groups):
                act.wait_ge(sig("tiles_done"), i + 1)
                bank = i % BANKS
                for n, (g, c0, m, part, tile) in enumerate(grp):
                    ins = nc.scalar.copy(mem.proj[part:part + m, tile, :],
                                         mem.ps[part:part + m, bank, n * T:(n + 1) * T])
                ins.then_inc(sig("bank_free"), 1)

        @block.tensor
        def _(pe):
            norm_sum(pe, mem, sq, sig, 7)
            pe.wait_ge(sig("normed"), KT)
            seen = set()
            for i, grp in enumerate(groups):
                if i >= BANKS:
                    pe.wait_ge(sig("bank_free"), i - BANKS + 1)
                bank = i % BANKS
                for n, (g, c0, m, part, tile) in enumerate(grp):
                    if g not in seen:
                        seen.add(g)
                        stream.arrived(pe, g)
                    for k in range(KT):
                        mm = pe.matmul(mem.ps[part:part + m, bank, n * T:(n + 1) * T],
                                       stream.weight(g, k, c0, m), mem.u[:, k, :],
                                       start=(k == 0), stop=(k == KT - 1))
                mm.then_inc(sig("tiles_done"), 1)
    sig.end()


def tile_groups(spec):
    return [spec[i:i + 2] for i in range(0, len(spec), 2)]



def accumulate(pe, mem, stream, sig, jobs, rhs, ready=None):
    k0 = 0
    for n, g in enumerate(jobs):
        nk = stream.jobs[g][0]
        stream.arrived(pe, g)
        for k in range(nk):
            if ready:
                ready(k0 + k)
        for o in range(KT):
            for k in range(nk):
                last = n == len(jobs) - 1 and k == nk - 1
                mm = pe.matmul(mem.ps[:, 4 + o // 2, (o % 2) * T:(o % 2 + 1) * T],
                               stream.weight(g, k, o * P, P), rhs[:, k0 + k, :],
                               start=(n == 0 and k == 0 and o % 2 == 0), stop=last,
                               skip_group_check=True)
        mm.then_inc(sig("tiles_done"), 1)
        k0 += nk


def add_residual(dve, nc, mem, sig, value, factor, say):
    dve.wait_ge(sig("tiles_done"), value)
    for b in range(4):
        say(nc.vector.scalar_tensor_tensor(
            out=mem.h[:, 2 * b:2 * b + 2, :].rearrange("p a t -> p (a t)"),
            in0=mem.ps[:, 4 + b, :], scalar=factor,
            in1=mem.h[:, 2 * b:2 * b + 2, :].rearrange("p a t -> p (a t)"),
            op0=ALU.mult, op1=ALU.add), "residual")



def merge_stage(nc, mem, sig, stream, layer, first, bias):
    cut = Cutter(mem.scratch)
    gates, merged, part = cut(3 * KT, T), cut(KT, T), cut(2, 2, T)
    GATE_BANKS = 12
    gate_jobs = list(range(first, first + 6))
    br_jobs = list(range(first + 6, first + 9))
    out_jobs = [first + 9, first + 10]
    done = [(g, 2 * n + 2) for n, g in enumerate(gate_jobs)]
    done += [(g, GATE_BANKS + 4 * n + 4) for n, g in enumerate(br_jobs)]
    done += [(g, GATE_BANKS + 12 + n + 1) for n, g in enumerate(out_jobs)]

    with nc.Block() as block:
        @block.sync
        def _(sp):
            stream.load_behind(sp, sig, layer, done)

        @block.scalar
        def _(act):
            link, say, need = linker(act, sig, "act_ops")
            for i in range(GATE_BANKS):
                need("tiles_done", i + 1)
                out = gates[:, 2 * i:2 * i + 2, :]
                if bias is None:
                    nc.scalar.activation(out.rearrange("p a t -> p (a t)"), mem.ps[:, i % 4, :],
                                         ACT.Sigmoid).then_inc(sig("gates"), 1)
                else:
                    for n in range(2):
                        col = bias + 2 * i + n
                        ins = nc.scalar.activation(out[:, n, :], mem.ps[:, i % 4, n * T:(n + 1) * T],
                                                   ACT.Sigmoid, bias=mem.par[:, col:col + 1])
                    ins.then_inc(sig("gates"), 1)

        @block.vector
        def _(dve):
            link, say, need = linker(dve, sig, "dve_ops")
            need("gates", GATE_BANKS)
            for br in range(3):
                for j in range(4):
                    i = 4 * br + j
                    need("tiles_done", GATE_BANKS + i + 1)
                    g = gates[:, KT * br + 2 * j:KT * br + 2 * j + 2, :].rearrange("p a t -> p (a t)")
                    m = merged[:, 2 * j:2 * j + 2, :].rearrange("p a t -> p (a t)")
                    if br == 0:
                        say(nc.vector.tensor_tensor(m, mem.ps[:, i % 4, :], g, ALU.mult), "merged")
                    else:
                        q = part[:, 0, :, :].rearrange("p a t -> p (a t)")
                        link(nc.vector.tensor_tensor(q, mem.ps[:, i % 4, :], g, ALU.mult))
                        say(nc.vector.tensor_tensor(m, m, q, ALU.add), "merged")
            add_residual(dve, nc, mem, sig, GATE_BANKS + 12 + 2, 1.0, say)

        @block.tensor
        def _(pe):
            for i in range(GATE_BANKS):
                if i >= 4:
                    pe.wait_ge(sig("gates"), i - 3)
                if i % 2 == 0:
                    stream.arrived(pe, gate_jobs[i // 2])
                for n in range(2):
                    for k in range(KT):
                        mm = pe.matmul(mem.ps[:, i % 4, n * T:(n + 1) * T],
                                       stream.weight(gate_jobs[i // 2], k, ((2 * i + n) % 4) * P, P),
                                       mem.u[:, k, :], start=(k == 0), stop=(k == KT - 1))
                mm.then_inc(sig("tiles_done"), 1)
            for i in range(12):
                br, j = divmod(i, 4)
                if i < 4:
                    pe.wait_ge(sig("gates"), GATE_BANKS - 3 + i)
                else:
                    pe.wait_ge(sig("merged"), i - 3)
                if j == 0:
                    stream.arrived(pe, br_jobs[br])
                for n in range(2):
                    for k in range(MT_):
                        mm = pe.matmul(mem.ps[:, i % 4, n * T:(n + 1) * T],
                                       stream.weight(br_jobs[br], k, (2 * j + n) * P, P),
                                       mem.y[:, MT_ * br + k, :], start=(k == 0), stop=(k == MT_ - 1))
                mm.then_inc(sig("tiles_done"), 1)
            pe.wait_ge(sig("merged"), 12)
            accumulate(pe, mem, stream, sig, out_jobs, merged)
    sig.end()



def ffn_stage(nc, mem, sig, stream, layer, first, gain, conv, factor, loads=()):
    cut = Cutter(mem.scratch)
    sq, rstd = cut(KT, T), cut(T)
    RB = 3
    c, sg = cut(RB, 2, T), cut(RB, T)
    hidden = mem.proj[:, 0:D_FF // P, :]
    PAIRS = D_FF // P
    up_jobs = list(range(first, first + 11))
    down_jobs = list(range(first + 11, first + 17))
    done = [(g, 2 * n + 2) for n, g in enumerate(up_jobs)]
    done += [(g, PAIRS + n + 1) for n, g in enumerate(down_jobs)]

    def half(j, n, a=0, b=T):
        return mem.ps[:, j % 4, n * T + a:n * T + b]

    with nc.Block() as block:
        @block.sync
        def _(sp):
            for load in loads:
                load(sp).then_inc(sig("params"), 16)
            if first == 0:
                for g in range(RING):
                    stream.load(sp, layer, g)
            stream.load_behind(sp, sig, layer, done)

        @block.scalar
        def _(act):
            link, say, need = linker(act, sig, "act_ops")
            norm_root(act, nc, rstd, sig, say)
            for j in range(PAIRS):
                need("tiles_done", j + 1)
                if j >= RB:
                    need("hidden", j - RB + 1)
                if conv:
                    taps, cb = conv
                    for n in range(2):
                        col = 2 * 44 + j + 22 * n
                        b = cb + j + 22 * n
                        ins = nc.scalar.activation(c[:, j % RB, n, :], half(j, n), ACT.Identity,
                                                   bias=mem.par[:, b:b + 1],
                                                   scale=mem.par[:, taps + col:taps + col + 1])
                    ins.then_inc(sig("tap_now"), 1)
                    need("convolved", j + 1)
                    say(nc.scalar.activation(sg[:, j % RB, :], c[:, j % RB, 0, :], ACT.Sigmoid),
                        "gate_sigmoid")
                else:
                    say(nc.scalar.activation(sg[:, j % RB, :], half(j, 0), ACT.Sigmoid),
                        "gate_sigmoid")

        @block.vector
        def _(dve):
            link, say, need = linker(dve, sig, "dve_ops")
            norm_squares(dve, nc, mem, sq, say)
            norm_mean(dve, nc, mem, rstd, sig, say, 7)
            if loads:
                need("params", 16 * len(loads))
            norm_scale(dve, nc, mem, rstd, gain, mem.u, sig, link)
            for j in range(PAIRS):
                if conv:
                    taps, cb = conv
                    need("tap_now", j + 1)
                    for lag in (1, 2):
                        for n in range(2):
                            col = taps + (2 - lag) * 44 + j + 22 * n
                            ins = nc.vector.scalar_tensor_tensor(
                                out=c[:, j % RB, n, lag:T], in0=half(j, n, 0, T - lag),
                                scalar=mem.par[:, col:col + 1], in1=c[:, j % RB, n, lag:T],
                                op0=ALU.mult, op1=ALU.add)
                            if (lag, n) == (2, 1):
                                say(ins, "convolved")
                            else:
                                link(ins)
                    gate, val = c[:, j % RB, 0, :], c[:, j % RB, 1, :]
                else:
                    gate, val = half(j, 0), half(j, 1)
                need("gate_sigmoid", j + 1)
                s = sg[:, j % RB, :]
                link(nc.vector.tensor_tensor(s, gate, s, ALU.mult))
                say(nc.vector.tensor_tensor(hidden[:, j, :], s, val, ALU.mult), "hidden")
            add_residual(dve, nc, mem, sig, PAIRS + 6, factor, say)

        @block.tensor
        def _(pe):
            norm_sum(pe, mem, sq, sig, 7)
            pe.wait_ge(sig("normed"), KT)
            for j in range(PAIRS):
                if j >= 4:
                    pe.wait_ge(sig("convolved" if conv else "hidden"), j - 3)
                if j % 2 == 0:
                    stream.arrived(pe, up_jobs[j // 2])
                for n in range(2):
                    for k in range(KT):
                        mm = pe.matmul(half(j, n), stream.weight(up_jobs[j // 2], k,
                                                                 (2 * (j % 2) + n) * P, P),
                                       mem.u[:, k, :], start=(k == 0), stop=(k == KT - 1))
                mm.then_inc(sig("tiles_done"), 1)
            accumulate(pe, mem, stream, sig, down_jobs, hidden,
                       ready=lambda k: pe.wait_ge(sig("hidden"), k + 1))
    sig.end()



def final_norm_stage(nc, mem, sig, gain, store=None):
    cut = Cutter(mem.scratch)
    sq, rstd = cut(KT, T), cut(T)
    with nc.Block() as block:
        @block.vector
        def _(dve):
            link, say, need = linker(dve, sig, "dve_ops")
            norm_squares(dve, nc, mem, sq, say)
            norm_mean(dve, nc, mem, rstd, sig, say, 7)
            norm_scale(dve, nc, mem, rstd, gain, mem.h, sig, link)

        @block.scalar
        def _(act):
            link, say, need = linker(act, sig, "act_ops")
            norm_root(act, nc, rstd, sig, say)

        @block.tensor
        def _(pe):
            norm_sum(pe, mem, sq, sig, 7)

        if store is not None:
            @block.sync
            def _(sp):
                sp.wait_ge(sig("normed"), KT)
                sp.dma_start(store, mem.h[:]).then_inc(sig("stored"), 16)
                sp.wait_ge(sig("stored"), 16)
    sig.end()



class Solver:
    def __init__(self, mem, mt, t, tt, x, c):
        self.mem, self.mt, self.t, self.tt, self.x, self.c = mem, mt, t, tt, x, c

    def pool(self, pool, nc, sig, n):
        mem, LV = self.mem, len(LEVELS)
        pool.wait_ge(sig("masked"), n + 1)
        for lv in range(LV):
            if n or lv:
                pool.wait_ge(sig("c_used"), n * LV + lv)
            if lv == 1:
                pool.wait_ge(sig("t_ready"), 2 * (n * LV + 1))
            mask = mem.c("levels", LV * P)[:, lv * P:(lv + 1) * P]
            for g in range(2):
                hs = slice(4 * g, 4 * g + 4)
                ins = nc.gpsimd.tensor_tensor(self.c[:, hs, :], self.mt[:, hs, :],
                                              mask.unsqueeze(1).to_broadcast([P, 4, P]), ALU.mult)
                ins.then_inc(sig("c_ready"), 1)

    def tensor(self, pe, sig, n):
        mem, LV = self.mem, len(LEVELS)
        pe.wait_ge(sig("c_ready"), 2 * (n * LV + 1))
        for h in range(HEADS):
            mm = pe.transpose(mem.ps[:, h // 4, (h % 4) * P:(h % 4 + 1) * P], self.c[:, h, :],
                              mem.c("ident"))
        mm.then_inc(sig("c_used"), 1)
        for lv in range(1, LV):
            pe.wait_ge(sig("c_ready"), 2 * (n * LV + lv + 1))
            for g in range(2):
                pe.wait_ge(sig("t_ready"), 2 * (n * (LV) + lv - 1) + g + 1)
                for h in range(4 * g, 4 * g + 4):
                    mm = pe.matmul(mem.ps[:, g, (h % 4) * P:(h % 4 + 1) * P], self.c[:, h, :],
                                   self.t[:, h, :], start=True, stop=True)
                mm.then_inc(sig("x_summed" if g == 0 else "c_used"), 1)
            for g in range(2):
                pe.wait_ge(sig("x_ready"), 2 * (n * (LV - 1) + lv - 1) + g + 1)
                for h in range(4 * g, 4 * g + 4):
                    at = slice((h % 4) * P, (h % 4 + 1) * P)
                    mm = pe.matmul(mem.ps[:, 2 + g, at], self.x[:, h, :], self.tt[:, h, :],
                                   start=True, stop=True)
                    if lv < LV - 1:
                        mm = pe.matmul(mem.ps[:, 4 + g, at], self.tt[:, h, :], self.x[:, h, :],
                                       start=True, stop=True)
                mm.then_inc(sig("growth_summed"), 1)

    def scalar(self, act, nc, sig, n):
        mem, LV = self.mem, len(LEVELS)
        for lv in range(1, LV):
            for g in range(2):
                if g == 0:
                    act.wait_ge(sig("x_summed"), n * (LV - 1) + lv)
                else:
                    act.wait_ge(sig("c_used"), n * LV + lv + 1)
                nc.scalar.copy(self.x[:, 4 * g:4 * g + 4, :].rearrange("p h t -> p (h t)"),
                               mem.ps[:, g, :]).then_inc(sig("x_ready"), 1)

    def vector(self, dve, nc, sig, n, link, say):
        mem, LV = self.mem, len(LEVELS)
        eye = mem.c("ident").unsqueeze(1).to_broadcast([P, 4, P])

        def four(buffer, g):
            return buffer[:, 4 * g:4 * g + 4, :]

        def bank(b):
            return mem.ps[:, b, :].rearrange("p (h t) -> p h t", h=4)

        dve.wait_ge(sig("c_used"), n * LV + 1)
        for g in range(2):
            link(nc.vector.tensor_tensor(four(self.t, g), bank(g), eye, ALU.add))
            say(nc.vector.tensor_tensor(four(self.tt, g), four(self.c, g), eye, ALU.add), "t_ready")
        for lv in range(1, LV):
            for g in range(2):
                dve.wait_ge(sig("growth_summed"), 2 * (n * (LV - 1) + lv - 1) + g + 1)
                if lv < LV - 1:
                    link(nc.vector.tensor_tensor(four(self.t, g), four(self.t, g), bank(4 + g),
                                                 ALU.add))
                say(nc.vector.tensor_tensor(four(self.tt, g), four(self.tt, g), bank(2 + g),
                                            ALU.add), "t_ready")



def rwkv_stage(nc, mem, sig):
    cut = Cutter(mem.scratch)
    z = [cut(MT_, T) for _ in range(8)]
    ar = cut(MT_, 4, 2, HD)
    bt, kt, btp, ktp = cut(MT_, T), cut(MT_, T), cut(MT_, T), cut(MT_, T)
    rhs, sa, state, kh_t = cut(MIX), cut(MIX), cut(MT_, HD), cut(MIX)
    jump, one_ka, mids = cut(MT_, 2), cut(MT_), cut(MT_, 4)
    ps, par = mem.ps, mem.par
    p_r, p_k, p_v = (mem.proj[:, i:i + 4, :] for i in (A_R, A_K, A_V))
    wa, gd = mem.proj[:, A_WA, :], mem.proj[:, A_G, :]
    bonus, gate, out = mem.y[:, 4:8, :], mem.y[:, 8:12, :], mem.y[:, 0:4, :]
    w_up_a_up = mem.small_w[:, 0:MIX]
    g_up = mem.small_w[:, MIX:2 * MIX]
    mixed = cut.buffer[:, 0:14 * T].rearrange("p (a t) -> p a t", a=14)
    a_all = mem.proj[:, 0:14, :]
    b0, b1 = slice(0, P), slice(P, T)
    bh_t = mem.proj[:, A_WA:A_WA + 2, :].rearrange("p a t -> p (a t)")
    mt, t_, tt, x, c, qb, ak, qk = (
        zi.rearrange("p a t -> p (a t)").rearrange("p (h t) -> p h t", h=HEADS) for zi in z)
    solver = Solver(mem, mt, t_, tt, x, c)

    def flat(ap):
        return ap.rearrange("p a t -> p (a t)")

    def q64(ap):
        return flat(ap).rearrange("p (q t) -> p q t", t=HD)

    def two(b):
        return ps[:, b:b + 2, :].rearrange("p a (b t) -> p (a b) t", t=T)

    def col(name, i):
        return par[:, C1[name] + i:C1[name] + i + 1]

    def hp(s):
        return slice(HD * (s // 4), HD * (s // 4) + HD)

    with nc.Block() as block:
        @block.vector
        def _(dve):
            link, say, need = linker(dve, sig, "dve_ops")
            V = nc.vector
            link(V.tensor_tensor(mixed[:, :, 1:T], a_all[:, :, 0:T - 1], a_all[:, :, 1:T], ALU.subtract))
            link(V.tensor_scalar(mixed[:, :, 0:1], a_all[:, :, 0:1], -1.0, None, ALU.mult))
            for i in [12, 13] + list(range(12)):
                ins = V.scalar_tensor_tensor(out=a_all[:, i, :], in0=mixed[:, i, :], scalar=col("mu", i),
                                             in1=a_all[:, i, :], op0=ALU.mult, op1=ALU.add)
                say(ins, "shifted")
            for i in range(MT_):
                link(V.tensor_scalar(z[2][:, i, :], p_k[:, i, :], col("k_k", i), None, ALU.mult))
            say(V.tensor_tensor(flat(z[3]), flat(z[2]), flat(z[2]), ALU.mult), "kk_squares")
            need("kk_sum", 1)
            say(V.tensor_scalar(z[3], two(6), 1e-24, None, ALU.max), "kk_guarded")
            need("kk_root", 1)
            link(V.reciprocal(flat(z[3]), flat(z[3])))
            link(V.tensor_tensor(flat(z[2]), flat(z[2]), flat(z[3]), ALU.mult))
            need("decay_sigmoid", 4)
            for i in range(MT_):
                link(V.tensor_tensor_scan(z[4][:, i, :], mem.c("ones", T), z[0][:, i, :], 0.0,
                                          ALU.mult, ALU.add))
            link(V.tensor_copy(mids[:], q64(z[4]).rearrange("p (a q) t -> p a q t", q=4)[:, :, :, 31]))
            mid = flat(mids).unsqueeze(2).to_broadcast([P, 16, HD])
            link(V.tensor_tensor(q64(z[5]), q64(z[4]), mid, ALU.subtract))
            say(V.tensor_tensor(flat(z[6]), flat(z[5]), flat(z[0]), ALU.subtract), "sums_centred")
            m2 = mids.rearrange("p a (b q) -> p a b q", q=2)
            say(V.tensor_tensor(jump[:], m2[:, :, :, 1], m2[:, :, :, 0], ALU.subtract), "jump_sums")
            link(V.tensor_tensor(z[3], z[4], z[4][:, :, P - 1:P].to_broadcast([P, MT_, T]), ALU.subtract))
            say(V.tensor_tensor(z[4][:, :, b1], z[3][:, :, b1], z[0][:, :, b1], ALU.subtract), "sums_from_half")
            need("a_sigmoid", 4)
            link(V.tensor_scalar(one_ka, par[:, C1["k_a"]:C1["k_a"] + 4], -1.0, 1.0, ALU.mult, ALU.add))
            for i in range(MT_):
                link(V.tensor_scalar(z[7][:, i, :], z[1][:, i, :], col("k_a", i), one_ka[:, i:i + 1],
                                     ALU.mult, ALU.add))
            link(V.tensor_tensor(flat(p_k), flat(p_k), flat(z[7]), ALU.mult))
            for i in range(MT_):
                ins = V.scalar_tensor_tensor(out=z[7][:, i, :], in0=p_r[:, i, :], scalar=col("r_k", i),
                                             in1=p_k[:, i, :], op0=ALU.mult, op1=ALU.mult)
                say(ins, "rk")
            link(V.tensor_tensor(flat(z[1]), flat(z[1]), flat(z[2]), ALU.mult))
            need("bonus_sum", 1)
            say(V.tensor_tensor(bonus, two(0), p_v, ALU.mult), "bonus")
            need("exps", 3)
            link(V.scalar_tensor_tensor(out=ar.rearrange("p a q r t -> p (a q) r t")[:, :, 0, :],
                                        in0=q64(z[2]), scalar=-1.0, in1=q64(z[6]),
                                        op0=ALU.mult, op1=ALU.mult))
            link(V.tensor_tensor(ar.rearrange("p a q r t -> p (a q) r t")[:, :, 1, :],
                                 q64(p_r), q64(z[7]), ALU.mult))
            link(V.tensor_tensor(flat(bt), flat(z[1]), flat(z[5]), ALU.mult))
            link(V.tensor_tensor(flat(kt), flat(p_k), flat(z[5]), ALU.mult))
            need("exps", 7)
            for near, far in ((bt, btp), (kt, ktp)):
                n4, f4 = (v.rearrange("p a (b q t) -> p (a b) q t", b=2, q=2) for v in (near, far))
                link(V.tensor_copy(f4[:, :, 1, :], n4[:, :, 1, :]))
                link(V.tensor_tensor(f4[:, :, 0, :], n4[:, :, 0, :],
                                     flat(jump).unsqueeze(2).to_broadcast([P, 8, HD]), ALU.mult))
            link(V.tensor_tensor(p_r[:, :, b0], z[1][:, :, b0], z[3][:, :, b0], ALU.mult))
            link(V.tensor_tensor(p_r[:, :, b1], p_r[:, :, b1], z[3][:, :, b1], ALU.mult))
            link(V.tensor_tensor(p_k[:, :, b0], p_k[:, :, b0], z[3][:, :, b0], ALU.mult))
            say(V.scalar_tensor_tensor(out=p_k[:, :, b1], in0=z[2][:, :, b1], scalar=-1.0,
                                       in1=z[4][:, :, b1], op0=ALU.mult, op1=ALU.mult), "operands")
            need("turned", 1)
            say(V.tensor_copy(p_v, two(4)), "by_token")
            say(V.tensor_copy(bh_t, ps[:, 6, :]), "by_token")
            say(V.tensor_copy(kh_t, ps[:, 7, :]), "by_token")
            for n in range(NBLK):
                for kind, (seen_a, seen_r) in enumerate(((mt, qb), (ak, qk))):
                    for j in range(4):
                        need("pairs_summed", n * 8 + kind * 4 + j + 1)
                        src = ps[:, 4 * kind + j, :].rearrange("p (h q r t) -> p h q r t", h=2, q=2, r=2)
                        for r, (dst, mask) in enumerate(((seen_a, "strict"), (seen_r, "incl"))):
                            m = mem.c(mask).rearrange("p (q t) -> p q t", q=2).unsqueeze(1)
                            ins = V.tensor_tensor(
                                dst[:, 2 * j:2 * j + 2, :].rearrange("p h (q t) -> p h q t", q=2),
                                src[:, :, :, r, :], m.to_broadcast([P, 2, 2, HD]), ALU.mult)
                            if (kind, j, r) == (1, 3, 1):
                                say(ins, "masked")
                            else:
                                link(ins)
                solver.vector(dve, nc, sig, n, link, say)
                need("rhs_summed", n + 1)
                say(V.tensor_copy(rhs.rearrange("p (b a) -> p b a", b=2), ps[:, 6:8, 0:T]), "rhs")
                need("sa_summed", n + 1)
                say(V.tensor_copy(sa, ps[:, 4, :]), "sa")
                need("y_summed", n + 1)
                say(V.tensor_copy(out[:, :, n * P:n * P + P],
                                  ps[:, 0, :].rearrange("p (a t) -> p a t", a=MT_)), "y_out")
                if n == 0:
                    need("state_summed", 1)
                    say(V.tensor_copy(flat(state), ps[:, 1, 0:MT_ * HD]), "state")
            need("mean_sum", 1)
            link(V.scalar_tensor_tensor(out=z[0], in0=two(2), scalar=-1.0 / HD, in1=out,
                                        op0=ALU.mult, op1=ALU.add))
            say(V.tensor_tensor(flat(z[1]), flat(z[0]), flat(z[0]), ALU.mult), "deviations")
            need("var_sum", 1)
            say(V.tensor_scalar(z[1], two(4), 1.0 / HD, GN_EPS, ALU.mult, ALU.add), "variance")
            need("std", 1)
            link(V.reciprocal(flat(z[1]), flat(z[1])))
            link(V.tensor_tensor(flat(z[0]), flat(z[0]), flat(z[1]), ALU.mult))
            for i in range(MT_):
                link(V.tensor_scalar(z[0][:, i, :], z[0][:, i, :], col("gn_g", i), col("gn_b", i),
                                     ALU.mult, ALU.add))
            link(V.tensor_tensor(z[0], z[0], bonus, ALU.add))
            need("low_rank_gate", 1)
            link(V.tensor_tensor(out, z[0], gate, ALU.mult))

        @block.scalar
        def _(act):
            link, say, need = linker(act, sig, "act_ops")
            A = nc.scalar.activation
            need("shifted", 2)
            link(A(wa[0:HD, :], wa[0:HD, :], ACT.Tanh))
            say(A(gd, gd, ACT.Sigmoid), "low_rank_in")
            need("shifted", 14)
            need("up_summed", 3)
            for i in range(MT_):
                say(A(z[0][:, i, :], two(0)[:, i, :], ACT.Sigmoid, bias=col("w0", i)), "decay_sigmoid")
            for i in range(MT_):
                say(A(z[1][:, i, :], two(2)[:, i, :], ACT.Sigmoid, bias=col("a0", i)), "a_sigmoid")
            say(nc.scalar.copy(gate, two(4)), "low_rank_gate")
            need("kk_guarded", 1)
            say(A(flat(z[3]), flat(z[3]), ACT.Sqrt), "kk_root")
            need("sums_centred", 1)
            say(A(flat(z[6]), flat(z[6]), ACT.Exp, scale=-KAPPA), "exps")
            need("bonus", 1)
            say(A(flat(z[7]), flat(z[5]), ACT.Exp, scale=-KAPPA), "exps")
            say(A(flat(z[5]), flat(z[5]), ACT.Exp, scale=KAPPA), "exps")
            need("jump_sums", 1)
            say(A(jump[:], jump[:], ACT.Exp, scale=-KAPPA), "exps")
            need("sums_from_half", 1)
            say(A(z[4][:, :, b1], z[4][:, :, b1], ACT.Exp, scale=-KAPPA), "exps")
            say(A(z[3][:, :, b1], z[3][:, :, b1], ACT.Exp, scale=-KAPPA), "exps")
            say(A(z[3][:, :, b0], z[3][:, :, b0], ACT.Exp, scale=KAPPA), "exps")
            for n in range(NBLK):
                solver.scalar(act, nc, sig, n)
            need("variance", 1)
            say(A(flat(z[1]), flat(z[1]), ACT.Sqrt), "std")

        @block.gpsimd
        def _(pool):
            for n in range(NBLK):
                solver.pool(pool, nc, sig, n)

        @block.tensor
        def _(pe):
            def need(name, n=1):
                pe.wait_ge(sig(name), n)

            need("low_rank_in", 1)
            for w, (rows, src, b) in enumerate(((slice(0, HD), wa, 0), (slice(HD, P), wa, 2),
                                                (slice(0, P), gd, 4))):
                weight = g_up if w == 2 else w_up_a_up
                for i in range(MT_):
                    mm = pe.matmul(two(b)[:, i, :], weight[rows, i * P:(i + 1) * P], src[rows, :],
                                   start=True, stop=True)
                mm.then_inc(sig("up_summed"), 1)

            def head_sums(b, src, name):
                for i in range(2):
                    mm = pe.matmul(ps[:, b + i, :], mem.c("bones"), flat(src[:, 2 * i:2 * i + 2, :]),
                                   start=True, stop=True)
                mm.then_inc(sig(name), 1)

            need("kk_squares", 1)
            head_sums(6, z[3], "kk_sum")
            need("decay_sigmoid", 4)
            need("rk", 4)
            head_sums(0, z[7], "bonus_sum")
            need("operands", 1)
            need("low_rank_gate", 1)
            for i in range(MT_):
                for n in range(NBLK):
                    pe.transpose(ps[:, 4 + n, i * P:(i + 1) * P], p_v[:, i, n * P:(n + 1) * P],
                                 mem.c("ident"))
                pe.transpose(ps[:, 6, i * P:(i + 1) * P], p_r[:, i, b0], mem.c("ident"))
                mm = pe.transpose(ps[:, 7, i * P:(i + 1) * P], p_k[:, i, b0], mem.c("ident"))
            mm.then_inc(sig("turned"), 1)
            need("by_token", 3)

            def of_head(by_token, s, n=0):
                at = n * MIX + (2 * (s % 4) + s // 4) * HD
                return by_token[:, at:at + HD]

            def v_t(n, s):
                return of_head(flat(p_v), s, n)

            for n in range(NBLK):
                if n:
                    need("state", 1)
                for kind, (near, far) in enumerate(((bt, btp), (kt, ktp))):
                    for h in range(HEADS):
                        o = ps[:, 4 * kind + h // 2, (h % 2) * T:(h % 2 + 1) * T]
                        for q, left in enumerate((near, far)):
                            mm = pe.matmul(o[:, q * P:(q + 1) * P],
                                           left[hp(h), h % 4, n * P:(n + 1) * P],
                                           ar[hp(h), h % 4, 2 * n + q, :, :].rearrange("p r t -> p (r t)"),
                                           start=True, stop=True)
                        if h % 2:
                            mm.then_inc(sig("pairs_summed"), 1)
                need("masked", n + 1)
                solver.tensor(pe, sig, n)
                for h in range(HEADS):
                    o = ps[:, 6 + h // 4, (h % 4) * HD:(h % 4 + 1) * HD]
                    mm = pe.matmul(o, ak[:, h, :], v_t(n, h), start=True, stop=(n == 0))
                    if n:
                        mm = pe.matmul(o, p_k[hp(h), h % 4, b1], state[hp(h), h % 4, :],
                                       start=False, stop=True)
                mm.then_inc(sig("rhs_summed"), 1)
                need("rhs", n + 1)
                need("t_ready", 2 * len(LEVELS) * (n + 1))
                for h in range(HEADS):
                    mm = pe.matmul(ps[:, 4, h * HD:(h + 1) * HD], tt[:, h, :],
                                   rhs[:, h * HD:(h + 1) * HD], start=True, stop=True)
                mm.then_inc(sig("sa_summed"), 1)
                need("sa", n + 1)
                for h in range(HEADS):
                    o = ps[hp(h), 0, (h % 4) * P:(h % 4 + 1) * P]
                    pe.matmul(o, sa[:, h * HD:(h + 1) * HD], qb[:, h, :], start=True, stop=False)
                    mm = pe.matmul(o, v_t(n, h), qk[:, h, :], start=False, stop=(n == 0))
                    if n:
                        mm = pe.matmul(o, state[hp(h), h % 4, :], p_r[hp(h), h % 4, b1],
                                       start=False, stop=True)
                mm.then_inc(sig("y_summed"), 1)
                if n == 0:
                    for h in range(HEADS):
                        o = ps[hp(h), 1, (h % 4) * HD:(h % 4 + 1) * HD]
                        pe.matmul(o, of_head(bh_t, h), sa[:, h * HD:(h + 1) * HD],
                                  start=True, stop=False)
                        mm = pe.matmul(o, of_head(kh_t, h), v_t(n, h),
                                       start=False, stop=True)
                    mm.then_inc(sig("state_summed"), 1)
            need("y_out", 2)
            head_sums(2, out, "mean_sum")
            need("deviations", 1)
            head_sums(4, z[1], "var_sum")
    sig.end()



def hgrn_stage(nc, mem, sig):
    NH = MIX // P
    cut = Cutter(mem.scratch)
    key, cs, acc, vt = (cut(NH, T) for _ in range(4))
    diff = [cut(NH, T) for _ in range(2)]
    fac = [cut(NH, T) for _ in range(2)]
    far = cut(NH, P)
    t1, t2 = cut(NH, T), cut(NH, T)
    lb, lb_inv, lbt = cut(NH), cut(NH), cut(3, NH)
    ps, par = mem.ps, mem.par
    q, f, v, g = (mem.proj[:, i:i + 4, :] for i in (B_Q, B_F, B_I, B_G))
    out = mem.y[:, 4:8, :]
    ALL = (P,) + tuple(reversed(LEVELS))
    accs = acc.rearrange("p h t -> p (h t)").rearrange("p (g t) -> p g t", t=P)

    def flat(ap):
        return ap.rearrange("p a t -> p (a t)")

    def halves(ap, b):
        return flat(ap).rearrange("p (m h b) -> p m h b", h=2, b=b)

    def cols(name):
        return par[:, C1[name]:C1[name] + NH]

    def two(b):
        return ps[:, b:b + 2, :].rearrange("p a (b t) -> p (a b) t", t=T)

    with nc.Block() as block:
        @block.vector
        def _(dve):
            link, say, need = linker(dve, sig, "dve_ops")
            V = nc.vector
            link(V.tensor_tensor(lbt[:, 0, :], cols("lb0"), cols("lb1"), ALU.max))
            link(V.tensor_tensor(lbt[:, 1, :], cols("lb0"), lbt[:, 0, :], ALU.subtract))
            say(V.tensor_tensor(lbt[:, 2, :], cols("lb1"), lbt[:, 0, :], ALU.subtract), "lb_logits")
            link(V.scalar_tensor_tensor(out=flat(t1), in0=flat(f), scalar=-1.0, in1=flat(f),
                                        op0=ALU.mult, op1=ALU.max))
            say(V.tensor_scalar(flat(t2), flat(f), -40.0, None, ALU.max), "f_sizes")
            need("lb_exp", 1)
            link(V.tensor_tensor(lbt[:, 0, :], lbt[:, 1, :], lbt[:, 2, :], ALU.add))
            link(V.reciprocal(lbt[:, 0, :], lbt[:, 0, :]))
            link(V.scalar_tensor_tensor(out=lb, in0=lbt[:, 2, :],
                                        scalar=par[:, C1["layer"]:C1["layer"] + 1],
                                        in1=lbt[:, 0, :], op0=ALU.mult, op1=ALU.mult))
            say(V.tensor_scalar(lb_inv, lb, -1.0, 1.0, ALU.mult, ALU.add), "lower_bound")
            need("log_terms", 1 + NH)
            link(V.scalar_tensor_tensor(out=flat(t1), in0=flat(f), scalar=0.0, in1=flat(t1),
                                        op0=ALU.min, op1=ALU.subtract))
            link(V.tensor_tensor(flat(t1), flat(t1), flat(t2), ALU.add))
            for h in range(NH):
                link(V.tensor_tensor_scan(cs[:, h, :], mem.c("ones", T), t1[:, h, :], 0.0,
                                          ALU.mult, ALU.add))
            need("forget_inverse", 1)
            for h in range(NH):
                ins = V.tensor_scalar(key[:, h, :], key[:, h, :], lb_inv[:, h:h + 1], None, ALU.mult)
                say(ins, "keys")
            say(V.memset(flat(acc), 0.0), "cleared")
            need("values_turned", 1)
            say(V.tensor_copy(vt, two(0)), "values_by_token")

            def exponents(n):
                b = ALL[n]
                d, c = halves(diff[n % 2], b), halves(cs, b)
                r = c[:, :, 0, b - 1:b].to_broadcast([P, NH * T // (2 * b), b])
                link(V.tensor_tensor(d[:, :, 0, :], r, c[:, :, 0, :], ALU.subtract))
                say(V.tensor_tensor(d[:, :, 1, :], c[:, :, 1, :], r, ALU.subtract), "exponents")

            def gather(n):
                need("scores_summed", n + 1)
                if n == 0:
                    say(V.tensor_copy(flat(far), ps[:, 4, :]), "gathered")
                else:
                    src = ps[:, 4 + 2 * (n % 2):6 + 2 * (n % 2), :].rearrange("p a (b t) -> p (a b) t", t=P)
                    if n <= len(LEVELS):
                        lv = len(LEVELS) - n
                        m = mem.c("levels", len(LEVELS) * P)[:, lv * P:(lv + 1) * P]
                    else:
                        m = mem.c("ident")
                    say(V.copy_predicated(accs, m.unsqueeze(1).to_broadcast([P, 8, P]).bitcast(I32),
                                          src), "gathered")

            exponents(0)
            for n in range(len(ALL)):
                if n + 1 < len(ALL):
                    exponents(n + 1)
                need("decays", n + 1)
                d, o, b = halves(diff[n % 2], ALL[n]), halves(fac[n % 2], ALL[n]), ALL[n]
                if n >= 2:
                    need("scores_summed", n - 1)
                link(V.tensor_tensor(o[:, :, 0, :], halves(key, b)[:, :, 0, :], d[:, :, 0, :], ALU.mult))
                say(V.tensor_tensor(o[:, :, 1, :], halves(q, b)[:, :, 1, :], d[:, :, 1, :], ALU.mult),
                    "factors")
                if n:
                    gather(n - 1)
            gather(len(ALL) - 1)
            gather(len(ALL))
            need("out_summed", 1)
            link(V.tensor_copy(t1, two(0)))
            say(V.tensor_tensor(flat(t2), flat(t1), flat(t1), ALU.mult), "out_squares")
            need("out_square_sum", 1)
            say(V.tensor_scalar(t2, two(2), 1.0 / P, EPS, ALU.mult, ALU.add), "out_mean_square")
            need("out_root", 1)
            link(V.reciprocal(flat(t2), flat(t2)))
            link(V.tensor_tensor(flat(t1), flat(t1), flat(t2), ALU.mult))
            need("gate_sigmoid", 1)
            link(V.tensor_tensor(flat(g), flat(g), flat(key), ALU.mult))
            for h in range(NH):
                link(V.scalar_tensor_tensor(out=out[:, h, :], in0=t1[:, h, :],
                                            scalar=par[:, C1["b_gn_g"] + h:C1["b_gn_g"] + h + 1],
                                            in1=g[:, h, :], op0=ALU.mult, op1=ALU.mult))

        @block.scalar
        def _(act):
            link, say, need = linker(act, sig, "act_ops")
            A = nc.scalar.activation
            need("lb_logits", 1)
            say(A(lbt[:, 1:3, :], lbt[:, 1:3, :], ACT.Exp), "lb_exp")
            need("f_sizes", 1)
            link(A(flat(t1), flat(t1), ACT.Exp, scale=-1.0))
            link(A(flat(t2), flat(t2), ACT.Exp, scale=-1.0))
            say(A(flat(t1), flat(t1), ACT.Ln, bias=1.0), "log_terms")
            need("lower_bound", 1)
            for h in range(NH):
                say(A(t2[:, h, :], t2[:, h, :], ACT.Ln, bias=1.0, scale=lb[:, h:h + 1]), "log_terms")
            say(A(flat(key), flat(f), ACT.Sigmoid, scale=-1.0), "forget_inverse")
            for n in range(len(ALL)):
                need("exponents", n + 1)
                say(A(flat(diff[n % 2]), flat(diff[n % 2]), ACT.Exp), "decays")
            need("scores_summed", len(ALL) + 1)
            say(A(flat(key), flat(g), ACT.Sigmoid), "gate_sigmoid")
            need("out_mean_square", 1)
            say(A(flat(t2), flat(t2), ACT.Sqrt), "out_root")

        @block.tensor
        def _(pe):
            def need(name, n=1):
                pe.wait_ge(sig(name), n)

            for n in range(NBLK):
                for h in range(NH):
                    mm = pe.transpose(ps[:, n, h * P:(h + 1) * P], v[:, h, n * P:(n + 1) * P],
                                      mem.c("ident"))
            mm.then_inc(sig("values_turned"), 1)
            for n in range(len(ALL) + 1):
                if n < len(ALL):
                    need("factors", n + 1)
                    left = right = fac[n % 2]
                else:
                    left, right = key, q
                if n >= 2:
                    need("gathered", n - 1)
                for h in range(NH):
                    if n == 0:
                        mm = pe.matmul(ps[:, 4, h * P:(h + 1) * P], left[:, h, 0:P], right[:, h, P:T],
                                       start=True, stop=True)
                        continue
                    for blk in range(NBLK):
                        i = 2 * h + blk
                        mm = pe.matmul(ps[:, 4 + 2 * (n % 2) + i // 4, (i % 4) * P:(i % 4 + 1) * P],
                                       left[:, h, blk * P:(blk + 1) * P],
                                       right[:, h, blk * P:(blk + 1) * P], start=True, stop=True)
                mm.then_inc(sig("scores_summed"), 1)
            need("gathered", len(ALL) + 1)
            need("values_by_token", 1)
            for h in range(NH):
                o = two(0)[:, h, :]
                v0, v1 = (flat(vt)[:, n * MIX + h * P:n * MIX + (h + 1) * P] for n in range(2))
                pe.matmul(o[:, 0:P], v0, accs[:, 2 * h, :], start=True, stop=True)
                pe.matmul(o[:, P:T], v0, far[:, h, :], start=True, stop=False)
                mm = pe.matmul(o[:, P:T], v1, accs[:, 2 * h + 1, :], start=False, stop=True)
            mm.then_inc(sig("out_summed"), 1)
            need("out_squares", 1)
            for i in range(2):
                mm = pe.matmul(ps[:, 2 + i, :], mem.c("ones"), flat(t2[:, 2 * i:2 * i + 2, :]),
                               start=True, stop=True)
            mm.then_inc(sig("out_square_sum"), 1)
    sig.end()



class Attention:

    def __init__(self, mem, cut, q, k, v, scale, bias):
        self.mem, self.q, self.k, self.v, self.scale, self.bias = mem, q, k, v, scale, bias
        self.prob = [cut(T) for _ in range(3)]
        self.turned = [cut(T) for _ in range(3)]
        self.low, self.sums = cut(16), cut(16)
        self.units = [(h, n) for n in range(NBLK) for h in range(HEADS)]

    def vector(self, dve, nc, sig, link, say):
        V = nc.vector
        for i in range(len(self.units) + 1):
            if i < len(self.units):
                w = P * (self.units[i][1] + 1)
                dve.wait_ge(sig("scores"), i + 1)
                link(V.tensor_reduce(self.low[:, i:i + 1], self.mem.ps[:, i % 3, 0:w], AX_X, ALU.max))
                say(V.tensor_scalar(self.low[:, i:i + 1], self.low[:, i:i + 1], -self.scale, None,
                                    ALU.mult), "row_max")
            if i:
                j = i - 1
                w = P * (self.units[j][1] + 1)
                dve.wait_ge(sig("prob"), j + 1)
                link(V.reciprocal(self.sums[:, j:j + 1], self.sums[:, j:j + 1]))
                say(V.tensor_scalar(self.prob[j % 3][:, 0:w], self.prob[j % 3][:, 0:w],
                                    self.sums[:, j:j + 1], None, ALU.mult), "prob_scaled")

    def scalar(self, act, nc, sig, say):
        for i in range(len(self.units) + 2):
            if i < len(self.units):
                w = P * (self.units[i][1] + 1)
                act.wait_ge(sig("row_max"), i + 1)
                if i >= 3:
                    act.wait_ge(sig("prob_turned"), i - 2)
                say(nc.scalar.activation(self.prob[i % 3][:, 0:w], self.mem.ps[:, i % 3, 0:w], ACT.Exp,
                                         bias=self.low[:, i:i + 1], scale=self.scale,
                                         accum_out=self.sums[:, i:i + 1]), "prob")
            if i >= 2:
                j = i - 2
                w = P * (self.units[j][1] + 1)
                act.wait_ge(sig("prob_turned"), j + 1)
                if j >= 3:
                    act.wait_ge(sig("attended"), j - 2)
                say(nc.scalar.copy(self.turned[j % 3][:, 0:w], self.mem.ps[:, 3 + j % 2, 0:w]),
                    "turned_out")

    def tensor(self, pe, sig):
        mem, n_units = self.mem, len(self.units)
        for i in range(n_units + 4):
            if i < n_units:
                h, n = self.units[i]
                w = P * (n + 1)
                if i >= 3:
                    pe.wait_ge(sig("prob"), i - 2)
                o = mem.ps[:, i % 3, 0:w]
                pe.matmul(o, self.q(h)[:, n * P:(n + 1) * P], self.k(h)[:, 0:w], start=True, stop=False)
                self.bias(pe, mem.ps[:, i % 3, :], h, n).then_inc(sig("scores"), 1)
            if 2 <= i < n_units + 2:
                j = i - 2
                n = self.units[j][1]
                pe.wait_ge(sig("prob_scaled"), j + 1)
                if j >= 2:
                    pe.wait_ge(sig("turned_out"), j - 1)
                for b in range(n + 1):
                    mm = pe.transpose(mem.ps[:, 3 + j % 2, b * P:(b + 1) * P],
                                      self.prob[j % 3][:, b * P:(b + 1) * P], mem.c("ident"))
                mm.then_inc(sig("prob_turned"), 1)
            if i >= 4:
                j = i - 4
                h, n = self.units[j]
                pe.wait_ge(sig("turned_out"), j + 1)
                rows = slice(HD * (h % 2), HD * (h % 2) + HD)
                o = mem.ps[rows, 5 + n, (h // 2) * P:(h // 2 + 1) * P]
                for b in range(n + 1):
                    mm = pe.matmul(o, self.v(h, b), self.turned[j % 3][:, b * P:(b + 1) * P],
                                   start=(b == 0), stop=(b == n))
                mm.then_inc(sig("attended"), 1)

    def out_of_psum(self, dve, nc, sig, link, out):
        for n in range(NBLK):
            dve.wait_ge(sig("attended"), HEADS * (n + 1))
            link(nc.vector.tensor_copy(out[:, :, n * P:(n + 1) * P],
                                       self.mem.ps[:, 5 + n, :].rearrange("p (a t) -> p a t", a=MT_)))


def rope(dve_v, link, say, x, turned, cos, sin, name):
    n = x.shape[1]
    r = x.shape[0]
    link(dve_v.tensor_tensor(turned, turned, sin.unsqueeze(1).to_broadcast([r, n, T]), ALU.mult))
    link(dve_v.tensor_tensor(x, x, cos.unsqueeze(1).to_broadcast([r, n, T]), ALU.mult))
    say(dve_v.tensor_tensor(x, x, turned, ALU.add), name)



def dsa_stage(nc, mem, sig):
    cut = Cutter(mem.scratch)
    score = [cut(T) for _ in range(NBLK)]
    bias = [cut(T) for _ in range(NBLK)]
    part, wi, top, vt = cut(T), cut(NBLK, 4), cut(8), cut(NBLK, P)
    ps = mem.ps
    x = mem.proj[:, C_Q:C_KI + 1, :]
    qi, ki = mem.proj[:, C_QI:C_QI + 2, :], mem.proj[:, C_KI, :]
    NT = C_KI + 1 - C_Q

    def rows(h):
        return slice(HD * (h % 2), HD * (h % 2) + HD)

    def tiles(b, n):
        return ps[:, b:b + (n + 1) // 2, :].rearrange("p a (b t) -> p (a b) t", t=T)[:, 0:n, :]

    def add_bias(pe, o, h, n):
        w = P * (n + 1)
        return pe.matmul(o[:, 0:w], mem.c("ident"), bias[n][:, 0:w], start=False, stop=True)

    att = Attention(mem, cut,
                    q=lambda h: mem.proj[rows(h), C_Q + h // 2, :],
                    k=lambda h: mem.proj[rows(h), C_K + h // 4, :],
                    v=lambda h, b: vt[:, b, HD * (h // 4):HD * (h // 4) + HD],
                    scale=HD ** -0.5, bias=add_bias)

    with nc.Block() as block:
        @block.vector
        def _(dve):
            link, say, need = linker(dve, sig, "dve_ops")
            V = nc.vector
            need("halves_swapped", 1)
            rope(V, link, say, x, tiles(0, NT), mem.c("cos", T), mem.c("sin", T), "roped")
            need("by_token", 1)
            say(V.tensor_copy(vt, ps[:, 5, 0:T].rearrange("p (n d) -> p n d", n=NBLK)), "values")
            say(V.tensor_scalar(wi, ps[:, 5, T:T + 8].rearrange("p (n j) -> p n j", n=NBLK),
                                4 ** -0.5 * HD ** -0.5, None, ALU.mult), "values")
            for n in range(NBLK):
                w = P * (n + 1)
                need("dots", n + 1)
                for j in range(4):
                    src = ps[:, 2 * n + j % 2, (j // 2) * T:(j // 2) * T + w]
                    dst = score[n] if j == 0 else part
                    link(V.tensor_scalar(dst[:, 0:w], src, 0.0, wi[:, n, j:j + 1], ALU.max, ALU.mult))
                    if j:
                        link(V.tensor_tensor(score[n][:, 0:w], score[n][:, 0:w], part[:, 0:w], ALU.add))
                diag = slice(n * P, (n + 1) * P)
                link(V.tensor_tensor(score[n][:, diag], score[n][:, diag], mem.c("cbias"), ALU.add))
                for _ in range(TOPK // 8):
                    link(V.max(top, score[n][:, 0:w]))
                    link(V.match_replace(score[n][:, 0:w], top, score[n][:, 0:w], TAKEN))
                link(V.tensor_scalar(bias[n][:, 0:w], score[n][:, 0:w], TAKEN / 2, NEG,
                                     ALU.is_gt, ALU.mult))
                say(V.tensor_tensor(bias[n][:, diag], bias[n][:, diag], mem.c("cbias"), ALU.add),
                    "key_bias")
            att.vector(dve, nc, sig, link, say)
            att.out_of_psum(dve, nc, sig, link, mem.y[:, 8:12, :])

        @block.scalar
        def _(act):
            link, say, need = linker(act, sig, "act_ops")
            att.scalar(act, nc, sig, say)

        @block.tensor
        def _(pe):
            def need(name, n=1):
                pe.wait_ge(sig(name), n)

            for i in range(NT):
                mm = pe.matmul(tiles(0, NT)[:, i, :], mem.c("rot"), x[:, i, :], start=True, stop=True)
            mm.then_inc(sig("halves_swapped"), 1)
            need("roped", 1)
            for n in range(NBLK):
                pe.transpose(ps[:, 5, n * P:(n + 1) * P], mem.proj[:, C_V, n * P:(n + 1) * P],
                             mem.c("ident"))
                mm = pe.transpose(ps[:, 5, T + 4 * n:T + 4 * n + 4],
                                  mem.proj[0:4, C_WI, n * P:(n + 1) * P],
                                  mem.c("ident")[0:4, 0:4])
            mm.then_inc(sig("by_token"), 1)
            for n in range(NBLK):
                w = P * (n + 1)
                for j in range(4):
                    mm = pe.matmul(ps[:, 2 * n + j % 2, (j // 2) * T:(j // 2) * T + w],
                                   qi[rows(j), j // 2, n * P:(n + 1) * P], ki[rows(j), 0:w],
                                   start=True, stop=True)
                mm.then_inc(sig("dots"), 1)
            need("values", 2)
            need("key_bias", NBLK)
            att.tensor(pe, sig)
    sig.end()



def mla_angles_stage(nc, mem, sig, pos):
    cut = Cutter(mem.scratch)
    where, angle, turns = cut(T), cut(T), cut(T)
    whole = cut(T)
    PI2 = 2 * np.pi
    HI = float(np.float32(np.floor(PI2 * 512) / 512))
    MID = float(np.float32(np.floor((PI2 - HI) * 2 ** 21) / 2 ** 21))
    LOW = float(np.float32(PI2 - HI - MID))
    with nc.Block() as block:
        @block.sync
        def _(sp):
            sp.dma_start(where.bitcast(I32), pos.to_broadcast([P, T])).then_inc(sig("positions"), 16)

        @block.vector
        def _(dve):
            link, say, need = linker(dve, sig, "dve_ops")
            V = nc.vector
            need("positions", 16)
            link(V.tensor_copy(angle, where.bitcast(I32)))
            link(V.tensor_scalar(angle, angle, mem.const[:, CC["invf"]:CC["invf"] + 1], None, ALU.mult))
            for out, quarter in ((mem.mla_sin, 0.0), (mem.mla_cos, 0.25)):
                link(V.tensor_scalar(turns, angle, 1.0 / PI2, quarter, ALU.mult, ALU.add))
                link(V.tensor_copy(whole.bitcast(I32), turns))
                link(V.tensor_copy(turns, whole.bitcast(I32)))
                link(V.scalar_tensor_tensor(out=out[:], in0=turns, scalar=-HI, in1=angle,
                                            op0=ALU.mult, op1=ALU.add))
                link(V.scalar_tensor_tensor(out=out[:], in0=turns, scalar=-MID, in1=out[:],
                                            op0=ALU.mult, op1=ALU.add))
                link(V.scalar_tensor_tensor(out=out[:], in0=turns, scalar=-LOW, in1=out[:],
                                            op0=ALU.mult, op1=ALU.add))
                link(V.tensor_scalar(out[:], out[:], quarter * PI2, float(np.float32(3.1415925)),
                                     ALU.add, ALU.min))
                say(V.tensor_scalar(out[:], out[:], -float(np.float32(3.1415925)), None, ALU.max),
                    "reduced")

        @block.scalar
        def _(act):
            link, say, need = linker(act, sig, "act_ops")
            for n, out in enumerate((mem.mla_sin, mem.mla_cos)):
                need("reduced", n + 1)
                link(nc.scalar.activation(out[:], out[:], ACT.Sin))
    sig.end()


def in_groups_2():
    groups = tile_groups([(17 + i // 4, (i % 4) * P, P, 0, X_Q + i) for i in range(12)])
    groups += [[(20, 0, 8, 0, X_F)]]
    groups += tile_groups([(20, 8, P, 0, X_CQ), (20, 8 + P, P, 0, X_CQ + 1)])
    groups += [[(20, 8 + 2 * P, P, 0, X_CKV)], [(20, 392, 32, HD, X_KR)]]
    groups += [[(20, 424, 8, 0, X_B)], [(20, 432, 8, 0, X_A)]]
    groups += tile_groups([(21 + i // 4, (i % 4) * P, P, 0, X_DQ + i) for i in range(16)])
    return groups



def fox_stage(nc, mem, sig):
    cut = Cutter(mem.scratch)
    vt, logf, size, c8 = cut(NBLK, MIX), cut(T), cut(T), cut(T)
    ps, par = mem.ps, mem.par
    f = mem.proj[0:HEADS, X_F, :]
    logf, size, c8 = (b[0:HEADS, :] for b in (logf, size, c8))
    bias = par[0:HEADS, C2["fox_b"]:C2["fox_b"] + 1]

    def rows(h):
        return slice(HD * (h % 2), HD * (h % 2) + HD)

    def add_bias(pe, o, h, n):
        pe.matmul(o[:, 0:P * (n + 1)], mem.c("ident")[0:HEADS, h:h + 1].to_broadcast([HEADS, P]),
                  c8[:, 0:P * (n + 1)], start=False, stop=False)
        return pe.matmul(o[:, n * P:(n + 1) * P], mem.c("ident"), mem.c("cbias"),
                         start=False, stop=True)

    att = Attention(mem, cut,
                    q=lambda h: mem.proj[rows(h), X_Q + h // 2, :],
                    k=lambda h: mem.proj[rows(h), X_K + h // 2, :],
                    v=lambda h, b: vt[:, b, h * HD:(h + 1) * HD],
                    scale=HD ** -0.5, bias=add_bias)

    with nc.Block() as block:
        @block.vector
        def _(dve):
            link, say, need = linker(dve, sig, "dve_ops")
            V = nc.vector
            link(V.tensor_scalar(f, f, bias, None, ALU.add))
            say(V.scalar_tensor_tensor(out=size, in0=f, scalar=-1.0, in1=f, op0=ALU.mult, op1=ALU.max),
                "f_size")
            need("values_turned", 1)
            say(V.tensor_copy(vt, ps[:, 0:2, :]), "values")
            need("log_term", 1)
            link(V.scalar_tensor_tensor(out=logf, in0=f, scalar=0.0, in1=size, op0=ALU.min,
                                        op1=ALU.subtract))
            link(V.tensor_tensor_scan(c8, mem.c("ones", T)[0:HEADS, :], logf, 0.0, ALU.mult, ALU.add))
            say(V.tensor_scalar(c8, c8, -float(HD ** 0.5), None, ALU.mult), "forget_sums")
            att.vector(dve, nc, sig, link, say)
            att.out_of_psum(dve, nc, sig, link, mem.y[:, 0:4, :])

        @block.scalar
        def _(act):
            link, say, need = linker(act, sig, "act_ops")
            need("f_size", 1)
            link(nc.scalar.activation(size, size, ACT.Exp, scale=-1.0))
            say(nc.scalar.activation(size, size, ACT.Ln, bias=1.0), "log_term")
            att.scalar(act, nc, sig, say)

        @block.tensor
        def _(pe):
            for n in range(NBLK):
                for i in range(MT_):
                    mm = pe.transpose(ps[:, n, i * P:(i + 1) * P],
                                      mem.proj[:, X_V + i, n * P:(n + 1) * P], mem.c("ident"))
            mm.then_inc(sig("values_turned"), 1)
            pe.wait_ge(sig("values"), 1)
            pe.wait_ge(sig("forget_sums"), 1)
            att.tensor(pe, sig)
    sig.end()



def mla_stage(nc, mem, sig):
    W = HD + 32
    cut = Cutter(mem.scratch)
    qf, kf, vt = cut(HEADS, T), cut(HEADS, T), cut(NBLK, MIX)
    sq, rstd = cut(3, T), cut(2, T)
    ps, par = mem.ps, mem.par
    c_all = mem.proj[:, X_CQ:X_CKV + 1, :]
    kr = mem.proj[HD:W, X_KR:X_KR + 1, :]
    w_uq = mem.small_w[:, 0:1536].rearrange("p (k n) -> p k n", k=2)
    w_ukv = mem.small_w[:, 1536:2560]

    def tiles(b, n):
        return ps[:, b:b + (n + 1) // 2, :].rearrange("p a (b t) -> p (a b) t", t=T)[:, 0:n, :]

    def add_bias(pe, o, h, n):
        return pe.matmul(o[:, n * P:(n + 1) * P], mem.c("ident"), mem.c("cbias"),
                         start=False, stop=True)

    att = Attention(mem, cut, q=lambda h: qf[0:W, h, :], k=lambda h: kf[0:W, h, :],
                    v=lambda h, b: vt[:, b, h * HD:(h + 1) * HD], scale=W ** -0.5, bias=add_bias)

    with nc.Block() as block:
        @block.vector
        def _(dve):
            link, say, need = linker(dve, sig, "dve_ops")
            V = nc.vector
            say(V.tensor_tensor(sq, c_all, c_all, ALU.mult), "squares")
            need("square_sums", 1)
            link(V.tensor_scalar(rstd[:, 0, :], ps[:, 0, 0:T], 1.0 / 256, EPS, ALU.mult, ALU.add))
            say(V.tensor_scalar(rstd[:, 1, :], ps[:, 1, 0:T], 1.0 / 128, EPS, ALU.mult, ALU.add),
                "mean_squares")
            need("roots", 1)
            link(V.reciprocal(rstd, rstd))
            for i in range(3):
                g = C2["q_norm"] + i
                say(V.scalar_tensor_tensor(out=c_all[:, i, :], in0=c_all[:, i, :],
                                           scalar=par[:, g:g + 1], in1=rstd[:, i // 2, :],
                                           op0=ALU.mult, op1=ALU.mult), "latents")
            need("queries_out", 1)
            need("queries_swapped", 1)
            rope(V, link, say, qf[0:W], tiles(4, HEADS)[0:W], mem.mla_cos[0:W, :],
                 mem.mla_sin[0:W, :], "roped")
            need("key_swapped", 1)
            rope(V, link, say, kr, ps[HD:W, 0:1, 0:T], mem.mla_cos[HD:W, :], mem.mla_sin[HD:W, :],
                 "roped")
            say(V.tensor_copy(kf[HD:W], kr.to_broadcast([32, HEADS, T])), "keys")
            need("keys_summed", 1)
            say(V.tensor_copy(kf[0:HD], tiles(4, HEADS)[0:HD]), "keys")
            need("values_summed", 1)
            say(V.tensor_copy(vt, ps[:, 1:3, :]), "values")
            att.vector(dve, nc, sig, link, say)
            att.out_of_psum(dve, nc, sig, link, mem.y[:, 4:8, :])

        @block.scalar
        def _(act):
            link, say, need = linker(act, sig, "act_ops")
            need("mean_squares", 1)
            say(nc.scalar.activation(rstd, rstd, ACT.Sqrt), "roots")
            need("queries_summed", 1)
            say(nc.scalar.copy(qf[0:W], tiles(0, HEADS)[0:W]), "queries_out")
            att.scalar(act, nc, sig, say)

        @block.tensor
        def _(pe):
            def need(name, n=1):
                pe.wait_ge(sig(name), n)

            need("squares", 1)
            for i in range(3):
                mm = pe.matmul(ps[:, i // 2, 0:T], mem.c("ones"), sq[:, i, :],
                               start=(i != 1), stop=(i != 0))
            mm.then_inc(sig("square_sums"), 1)
            need("latents", 3)
            for h in range(HEADS):
                for k in range(2):
                    mm = pe.matmul(tiles(0, HEADS)[0:W, h, :], w_uq[:, k, h * W:(h + 1) * W],
                                   c_all[:, k, :], start=(k == 0), stop=(k == 1))
            mm.then_inc(sig("queries_summed"), 1)
            need("queries_out", 1)
            for h in range(HEADS):
                mm = pe.matmul(tiles(4, HEADS)[0:W, h, :], mem.c("rotm")[0:W, 0:W], qf[0:W, h, :],
                               start=True, stop=True)
            mm.then_inc(sig("queries_swapped"), 1)
            pe.matmul(ps[HD:W, 0, 0:T], mem.c("rotm")[HD:W, HD:W], kr[:, 0, :], start=True,
                      stop=True).then_inc(sig("key_swapped"), 1)
            for n in range(NBLK):
                mm = pe.matmul(ps[:, 1 + n, :], c_all[:, 2, n * P:(n + 1) * P],
                               w_ukv.rearrange("p (h a d) -> p h a d", h=HEADS, a=2)[:, :, 1, :],
                               start=True, stop=True)
            mm.then_inc(sig("values_summed"), 1)
            need("roped", 1)
            for h in range(HEADS):
                mm = pe.matmul(tiles(4, HEADS)[0:HD, h, :], w_ukv[:, h * P:h * P + HD],
                               c_all[:, 2, :], start=True, stop=True)
            mm.then_inc(sig("keys_summed"), 1)
            need("keys", 2)
            need("values", 1)
            att.tensor(pe, sig)
    sig.end()



def delta_stage(nc, mem, sig):
    cut = Cutter(mem.scratch)
    z = [cut(MT_, T) for _ in range(7)]
    kq = cut(MT_, NBLK, 2, P)
    vt, kt, qh, kh, vnew, rhs = cut(NBLK, MIX), cut(MIX), cut(MT_, P), cut(MT_, P), cut(MIX), cut(MIX)
    state, cols, rows = cut(MT_, HD), cut(2, NBLK, HEADS), cut(4, T)
    ps, par = mem.ps, mem.par
    b0, b1 = slice(0, P), slice(P, T)
    x = mem.proj[:, X_DQ:X_DZ, :]
    q, k, v, dz = (mem.proj[:, i:i + 4, :] for i in (X_DQ, X_DK, X_DV, X_DZ))
    conv = mem.scratch[:, 0:12 * T].rearrange("p (a t) -> p a t", a=12)
    out = mem.y[:, 8:12, :]
    mt, t_, tt, xx, c, qk, dec = (
        zi.rearrange("p a t -> p (a t)").rearrange("p (h t) -> p h t", h=HEADS) for zi in z)
    solver = Solver(mem, mt, t_, tt, xx, c)
    beta, decay = mem.proj[0:HEADS, X_B, :], mem.proj[0:HEADS, X_A, :]
    size, gsum, egsum = (rows[0:HEADS, i, :] for i in range(3))
    ea = rows[0:HEADS, 3, 0:1]

    def flat(ap):
        return ap.rearrange("p a t -> p (a t)")

    def two(b):
        return ps[:, b:b + 2, :].rearrange("p a (b t) -> p (a b) t", t=T)

    def hp(s):
        return slice(HD * (s // 4), HD * (s // 4) + HD)

    def head(s):
        return 2 * (s % 4) + s // 4

    def par8(name):
        return par[0:HEADS, C2[name]:C2[name] + 1]

    with nc.Block() as block:
        @block.vector
        def _(dve):
            link, say, need = linker(dve, sig, "dve_ops")
            V = nc.vector
            link(V.tensor_scalar(decay, decay, par8("dt_bias"), None, ALU.add))
            say(V.scalar_tensor_tensor(out=size, in0=decay, scalar=-1.0, in1=decay,
                                       op0=ALU.mult, op1=ALU.max), "a_size")
            for i in range(12):
                tap = C2["dn_conv"] + i
                link(V.tensor_scalar(conv[:, i, :], x[:, i, :], par[:, tap + 36:tap + 37], None, ALU.mult))
                for lag in (1, 2, 3):
                    w = tap + 12 * (3 - lag)
                    ins = V.scalar_tensor_tensor(out=conv[:, i, lag:T], in0=x[:, i, 0:T - lag],
                                                 scalar=par[:, w:w + 1], in1=conv[:, i, lag:T],
                                                 op0=ALU.mult, op1=ALU.add)
                    if lag == 3:
                        say(ins, "convolved")
                    else:
                        link(ins)
            need("log_term", 1)
            link(V.scalar_tensor_tensor(out=size, in0=decay, scalar=0.0, in1=size, op0=ALU.max,
                                        op1=ALU.add))
            link(V.tensor_scalar(size, size, ea, -1.0, ALU.mult, ALU.mult))
            for n in range(NBLK):
                at = slice(n * P, (n + 1) * P)
                ins = V.tensor_tensor_scan(gsum[:, at], mem.c("ones", T)[0:HEADS, at], size[:, at], 0.0,
                                           ALU.mult, ALU.add)
                say(ins, "gate_sums")
            need("silu_gate", 1)
            link(V.tensor_tensor(x, x, conv, ALU.mult))
            for i in range(2):
                s = mem.scratch[:, i * 4 * T:(i + 1) * 4 * T]
                say(V.tensor_tensor(s, flat(x[:, 4 * i:4 * i + 4, :]), flat(x[:, 4 * i:4 * i + 4, :]),
                                    ALU.mult), "squares")
            for i in range(2):
                need("square_sums", i + 1)
                say(V.tensor_scalar(z[i], two(2 * i), EPS, None, ALU.add), "sums_out")
            for i in range(2):
                need("roots", i + 1)
                link(V.reciprocal(flat(z[i]), flat(z[i])))
                say(V.scalar_tensor_tensor(out=flat(x[:, 4 * i:4 * i + 4, :]),
                                           in0=flat(x[:, 4 * i:4 * i + 4, :]),
                                           scalar=HD ** -0.5 if i == 0 else 1.0,
                                           in1=flat(z[i]), op0=ALU.mult, op1=ALU.mult), "unit")
            need("columns_turned", 1)
            src = ps[:, 0, 0:4 * HEADS].rearrange("p (a n h) -> p a n h", a=2, n=NBLK)
            link(V.tensor_scalar(cols[:, 0, :, :], src[:, 0, :, :], -1.0, None, ALU.mult))
            say(V.tensor_copy(cols[:, 1, :, :], src[:, 1, :, :]), "columns")
            need("beta_spread", 1)
            kq5 = kq.rearrange("p a n w t -> p (a n) w t")
            k3 = flat(k).rearrange("p (a t) -> p a t", t=P)
            link(V.scalar_tensor_tensor(out=kq5[:, :, 0, :], in0=k3, scalar=-1.0,
                                        in1=ps[:, 4:6, :].rearrange("p a (b t) -> p (a b) t", t=P),
                                        op0=ALU.mult, op1=ALU.mult))
            link(V.tensor_copy(kq5[:, :, 1, :], flat(q).rearrange("p (a t) -> p a t", t=P)))
            spread = ps[:, 6, :].rearrange("p (a t) -> p a t", a=MT_)
            link(V.tensor_tensor(kh, kq[:, :, 1, 0, :], spread, ALU.mult))
            say(V.tensor_tensor(qh, q[:, :, b1], spread, ALU.mult), "operands")
            need("turned", 1)
            beta_t = cols[:, 1, :, :].rearrange("p n h -> p (n h)").unsqueeze(2)
            link(V.tensor_tensor(flat(vt).rearrange("p (h d) -> p h d", d=HD),
                                 ps[:, 1:3, :].rearrange("p a (h d) -> p (a h) d", d=HD),
                                 beta_t.to_broadcast([P, 16, HD]), ALU.mult))
            say(V.tensor_copy(kt, ps[:, 3, :]), "by_token")
            for n in range(NBLK):
                need("decay", 8 * (n + 1))
                for j in range(4):
                    need("pairs_summed", 4 * n + j + 1)
                    hs = slice(2 * j, 2 * j + 2)
                    src = ps[:, 4 + j, :].rearrange("p (h w t) -> p h w t", h=2, w=2)
                    link(V.tensor_tensor(mt[:, hs, :], src[:, :, 0, :], dec[:, hs, :], ALU.mult))
                    ins = V.tensor_tensor(qk[:, hs, :], src[:, :, 1, :], dec[:, hs, :], ALU.mult)
                    if j == 3:
                        say(ins, "masked")
                    else:
                        link(ins)
                if n == 0:
                    kt4 = kt.rearrange("p (a b d) -> p b a d", a=4, b=2)
                    for b in range(2):
                        ins = V.tensor_tensor(kt4[:, b, :, :], kt4[:, b, :, :],
                                              dec[:, 4 * b:4 * b + 4, P - 1:P].to_broadcast([P, 4, HD]),
                                              ALU.mult)
                        say(ins, "keys_to_end")
                solver.vector(dve, nc, sig, n, link, say)
                vb = vt[:, n, :].rearrange("p (a b d) -> p b a d", a=4, b=2)
                r4 = rhs.rearrange("p (b a d) -> p b a d", b=2, a=4)
                for b in range(2):
                    if n == 0:
                        say(V.tensor_copy(r4[:, b, :, :], vb[:, b, :, :]), "rhs")
                    else:
                        need("seen_summed", 1)
                        src = ps[:, 6 + b, 0:T].rearrange("p (a d) -> p a d", a=4)
                        say(V.tensor_tensor(r4[:, b, :, :], vb[:, b, :, :], src, ALU.add), "rhs")
                need("new_summed", n + 1)
                say(V.tensor_copy(vnew, ps[:, 4, :]), "new")
                need("out_summed", n + 1)
                say(V.tensor_copy(out[:, :, n * P:n * P + P],
                                  ps[:, 0, :].rearrange("p (a t) -> p a t", a=MT_)), "out")
                if n == 0:
                    need("state_summed", 1)
                    say(V.tensor_copy(flat(state), ps[:, 1, 0:MT_ * HD]), "state")
            say(V.tensor_tensor(z[0], out, out, ALU.mult), "out_squares")
            need("out_square_sums", 1)
            say(V.tensor_scalar(z[0], two(2), 1.0 / HD, EPS, ALU.mult, ALU.add), "out_mean")
            need("out_root", 1)
            link(V.reciprocal(flat(z[0]), flat(z[0])))
            link(V.tensor_tensor(out, out, z[0], ALU.mult))
            link(V.tensor_tensor(flat(z[1]), flat(z[1]), flat(dz), ALU.mult))
            link(V.scalar_tensor_tensor(out=out.rearrange("p a t -> p (a t)"),
                                        in0=out.rearrange("p a t -> p (a t)"),
                                        scalar=par[:, C2["o_norm"]:C2["o_norm"] + 1],
                                        in1=flat(z[1]), op0=ALU.mult, op1=ALU.mult))

        @block.scalar
        def _(act):
            link, say, need = linker(act, sig, "act_ops")
            A = nc.scalar.activation
            link(A(ea, par8("a_log"), ACT.Exp))
            need("a_size", 1)
            link(A(size, size, ACT.Exp, scale=-1.0))
            say(A(size, size, ACT.Ln, bias=1.0), "log_term")
            say(A(beta, beta, ACT.Sigmoid), "beta")
            need("convolved", 12)
            link(nc.scalar.copy(x, conv))
            say(A(conv, conv, ACT.Sigmoid), "silu_gate")
            for i in range(2):
                need("sums_out", i + 1)
                say(A(flat(z[i]), flat(z[i]), ACT.Sqrt), "roots")
            need("gate_sums", NBLK)
            say(A(egsum, gsum, ACT.Exp), "gate_exp")
            for n in range(NBLK):
                if n:
                    need("masked", n)
                    need("keys_to_end", 2)
                for s in range(HEADS):
                    need("rows_spread", n * 2 + s // 4 + 1)
                    say(A(dec[:, s, :], ps[:, 2 + s // 4, (s % 4) * P:(s % 4 + 1) * P], ACT.Exp,
                          bias=cols[:, 0, n, head(s):head(s) + 1]), "decay")
                solver.scalar(act, nc, sig, n)
            need("out_summed", 2)
            link(A(flat(z[1]), flat(dz), ACT.Sigmoid))
            need("out_mean", 1)
            say(A(flat(z[0]), flat(z[0]), ACT.Sqrt), "out_root")

        @block.gpsimd
        def _(pool):
            for n in range(NBLK):
                solver.pool(pool, nc, sig, n)

        @block.tensor
        def _(pe):
            def need(name, n=1):
                pe.wait_ge(sig(name), n)

            def head_sums(b, src, name):
                for i in range(2):
                    mm = pe.matmul(ps[:, b + i, :], mem.c("bones"), src[:, 2 * i * T:2 * (i + 1) * T],
                                   start=True, stop=True)
                mm.then_inc(sig(name), 1)

            for i in range(2):
                need("squares", i + 1)
                head_sums(2 * i, mem.scratch[:, i * 4 * T:(i + 1) * 4 * T], "square_sums")
            hsel = mem.c("hsel", MT_ * P)
            need("beta", 1)
            for i in range(MT_):
                mm = pe.matmul(two(4)[:, i, :], hsel[0:HEADS, i * P:(i + 1) * P], beta,
                               start=True, stop=True)
            mm.then_inc(sig("beta_spread"), 1)
            need("gate_exp", 1)
            for i in range(MT_):
                pe.matmul(ps[:, 6, i * P:(i + 1) * P], hsel[0:HEADS, i * P:(i + 1) * P], egsum[:, b1],
                          start=True, stop=True)
            need("unit", 2)
            eye8 = mem.c("ident")[0:HEADS, 0:HEADS]
            for w, src in enumerate((gsum, beta)):
                for n in range(NBLK):
                    at = (w * NBLK + n) * HEADS
                    mm = pe.transpose(ps[:, 0, at:at + HEADS], src[:, n * P:(n + 1) * P], eye8)
            mm.then_inc(sig("columns_turned"), 1)
            for i in range(MT_):
                for n in range(NBLK):
                    pe.transpose(ps[:, 1 + n, i * P:(i + 1) * P], v[:, i, n * P:(n + 1) * P],
                                 mem.c("ident"))
                mm = pe.transpose(ps[:, 3, i * P:(i + 1) * P], k[:, i, b0], mem.c("ident"))
            mm.then_inc(sig("turned"), 1)
            need("operands", 1)
            need("by_token", 1)
            need("columns", 1)
            for n in range(NBLK):
                if n:
                    need("state", 1)
                for s in range(HEADS):
                    o = ps[:, 2 + s // 4, (s % 4) * P:(s % 4 + 1) * P]
                    h = head(s)
                    pe.matmul(o, mem.c("ident")[0:HEADS, h:h + 1].to_broadcast([HEADS, P]),
                              gsum[:, n * P:(n + 1) * P], start=True, stop=False)
                    mm = pe.matmul(o, mem.c("ident"), mem.c("cbiasT"), start=False, stop=True)
                    if s % 4 == 3:
                        mm.then_inc(sig("rows_spread"), 1)
                for s in range(HEADS):
                    mm = pe.matmul(ps[:, 4 + s // 2, (s % 2) * T:(s % 2 + 1) * T],
                                   k[hp(s), s % 4, n * P:(n + 1) * P],
                                   kq[hp(s), s % 4, n, :, :].rearrange("p w t -> p (w t)"),
                                   start=True, stop=True)
                    if s % 2:
                        mm.then_inc(sig("pairs_summed"), 1)
                need("masked", n + 1)
                solver.tensor(pe, sig, n)
                if n:
                    for s in range(HEADS):
                        mm = pe.matmul(ps[:, 6 + s // 4, (s % 4) * HD:(s % 4 + 1) * HD],
                                       kh[hp(s), s % 4, :], state[hp(s), s % 4, :],
                                       start=True, stop=True)
                    mm.then_inc(sig("seen_summed"), 1)
                need("rhs", 2 * (n + 1))
                need("t_ready", 2 * len(LEVELS) * (n + 1))
                for s in range(HEADS):
                    mm = pe.matmul(ps[:, 4, s * HD:(s + 1) * HD], tt[:, s, :],
                                   rhs[:, s * HD:(s + 1) * HD], start=True, stop=True)
                mm.then_inc(sig("new_summed"), 1)
                need("new", n + 1)
                for s in range(HEADS):
                    o = ps[hp(s), 0, (s % 4) * P:(s % 4 + 1) * P]
                    mm = pe.matmul(o, vnew[:, s * HD:(s + 1) * HD], qk[:, s, :], start=True,
                                   stop=(n == 0))
                    if n:
                        mm = pe.matmul(o, state[hp(s), s % 4, :], qh[hp(s), s % 4, :],
                                       start=False, stop=True)
                mm.then_inc(sig("out_summed"), 1)
                if n == 0:
                    need("keys_to_end", 2)
                    for s in range(HEADS):
                        h = head(s)
                        mm = pe.matmul(ps[hp(s), 1, (s % 4) * HD:(s % 4 + 1) * HD],
                                       kt[:, h * HD:(h + 1) * HD], vnew[:, s * HD:(s + 1) * HD],
                                       start=True, stop=True)
                    mm.then_inc(sig("state_summed"), 1)
            need("out_squares", 1)
            head_sums(2, flat(z[0]), "out_square_sums")
    sig.end()


def in_groups():
    tiles = [(i // 4, (i % 4) * P, P, 0, i) for i in range(14)]
    groups = tile_groups(tiles)
    groups += tile_groups([(4 + i // 4, (i % 4) * P, P, 0, B_Q + i) for i in range(16)])
    groups += tile_groups([(8 + i // 4, (i % 4) * P, P, 0, C_Q + i) for i in range(8)])
    groups += tile_groups([(10, 0, P, 0, C_KI), (10, P, P, 0, C_V)])
    groups += [[(10, 2 * P, 4, 0, C_WI)]]
    return groups


def hybrid_blocks(nc, w1, w2, par1, par2, small1, small2, xt, const, pos, out):
    with ExitStack() as ctx:
        mem = Memory(nc, ctx)
        full = [ctx.enter_context(nc.semaphore("slot_full_%d" % i)) for i in range(RING)]
        sig = Signals(nc)

        def clear_ring():
            nc.all_engine_barrier(sems_to_clear=range(full[0].num, full[-1].num + 1))

        def row(ap, layer):
            return ap[bass.ds(layer, 1)].rearrange("a p n -> (a p) n")

        with nc.Block() as block:
            @block.sync
            def _(sp):
                sp.dma_start(mem.h[:], xt).then_inc(sig("loaded"), 16)
                sp.dma_start(mem.const[:], const).then_inc(sig("loaded"), 16)
                sp.wait_ge(sig("loaded"), 32)
        sig.end()

        with nc.Fori(0, DEPTH) as layer:
            stream = Stream(mem, w1, JOBS1, full)
            loads = [lambda sp: sp.dma_start(mem.par[:, 0:N_PAR1], row(par1, layer)),
                     lambda sp: sp.dma_start(mem.small_w[:, 0:2 * MIX], row(small1, layer))]
            project_stage(nc, mem, sig, stream, layer, in_groups(), 0, C1["mix_g"], loads)
            rwkv_stage(nc, mem, sig)
            hgrn_stage(nc, mem, sig)
            dsa_stage(nc, mem, sig)
            merge_stage(nc, mem, sig, stream, layer, 11, None)
            ffn_stage(nc, mem, sig, stream, layer, 22, C1["ffn_g"],
                      (C1["conv_w"], C1["conv_b"]), 1.0)
            clear_ring()
        final_norm_stage(nc, mem, sig, C1["fin_g"])
        mla_angles_stage(nc, mem, sig, pos)
        with nc.Fori(0, DEPTH) as layer:
            stream = Stream(mem, w2, JOBS2, full)
            loads = [lambda sp: sp.dma_start(mem.par[:, 0:N_PAR2], row(par2, layer)),
                     lambda sp: sp.dma_start(mem.small_w[:], row(small2, layer))]
            ffn_stage(nc, mem, sig, stream, layer, 0, C2["ffn1_g"], None, 0.5, loads)
            project_stage(nc, mem, sig, stream, layer, in_groups_2(), 17, C2["mix_g"], [])
            fox_stage(nc, mem, sig)
            mla_stage(nc, mem, sig)
            delta_stage(nc, mem, sig)
            merge_stage(nc, mem, sig, stream, layer, 25, C2["b_gate"])
            ffn_stage(nc, mem, sig, stream, layer, 36, C2["ffn2_g"], None, 0.5)
            clear_ring()
        final_norm_stage(nc, mem, sig, C2["fin_g"], store=out)
    return mem



def cols_of(v):
    v = np.asarray(v)
    return v.reshape(-1, P).T


def job_block(w, cols=None):
    w = w if cols is None else np.concatenate([w[:, a:b] for a, b in cols], axis=1)
    k, n = w.shape
    return w.reshape(k // P, P, n).transpose(1, 0, 2).reshape(P, -1)


def fill(dst, src):
    dst[:, :src.shape[1]] = src


def pack_block1(i):
    w1 = np.zeros((DEPTH, len(JOBS1), P, SLOT), np.float32)
    par = np.zeros((DEPTH, P, N_PAR1), np.float32)
    small = np.zeros((DEPTH, P, 2 * MIX), np.float32)
    c0, gate0 = 1792 + 2048, 1792 + 2048 + 1092
    for l in range(DEPTH):
        w, jobs = i["w_in"][l], []
        jobs += [job_block(w, [(a, min(a + 512, 1792))]) for a in range(0, 1792, 512)]
        jobs += [job_block(w, [(1792 + a, 1792 + a + 512)]) for a in range(0, 2048, 512)]
        jobs += [job_block(w, [(c0, c0 + 512)])]
        k, v, qi, ki, wi = c0 + 512, c0 + 640, c0 + 768, c0 + 1024, c0 + 1088
        jobs += [job_block(w, [(k, k + 64)] * 2 + [(k + 64, k + 128)] * 2 + [(qi, qi + 256)])]
        jobs += [job_block(w, [(ki, ki + 64)] * 2 + [(v, v + 128), (wi, wi + 4)])]
        jobs += [job_block(w, [(gate0 + a, gate0 + a + 512)]) for a in range(0, 3072, 512)]
        jobs += [job_block(i["w_branch"][l, n]) for n in range(3)]
        jobs += [job_block(i["w_o"][l, a:a + 512]) for a in (0, 512)]
        up = i["w_up"][l]
        for j in range(0, 22, 2):
            jobs += [job_block(up, [(x, x + P) for x in (j * P, D_FF + j * P, (j + 1) * P,
                                                         D_FF + (j + 1) * P)])]
        jobs += [job_block(i["w_down"][l, a:min(a + 512, D_FF)]) for a in range(0, D_FF, 512)]
        for g, job in enumerate(jobs):
            fill(w1[l, g], job)
        table = {"mix_g": i["norm_mix_g"][l], "mu": i["a_mu"][l], "w0": i["a_w0"][l],
                 "a0": i["a_a0"][l], "k_k": i["a_k_k"][l], "k_a": i["a_k_a"][l],
                 "r_k": i["a_r_k"][l].reshape(-1), "gn_g": i["a_gn_g"][l], "gn_b": i["a_gn_b"][l],
                 "lb0": i["b_lb_logits"][0], "lb1": i["b_lb_logits"][1], "b_gn_g": i["b_gn_g"][l],
                 "ffn_g": i["norm_ffn_g"][l], "conv_w": i["conv_w"][l].reshape(-1),
                 "conv_b": i["conv_b"][l], "fin_g": i["norm_final_g"]}
        for name, v in table.items():
            fill(par[l, :, C1[name]:], cols_of(v))
        par[l, :, C1["layer"]] = float(l)
        small[l, 0:HD, 0:MIX] = i["a_w_up"][l]
        small[l, HD:P, 0:MIX] = i["a_a_up"][l]
        small[l, :, MIX:] = i["a_g_up"][l]
    return w1, par, small


def pack_block2(i):
    w2 = np.zeros((DEPTH, len(JOBS2), P, SLOT), np.float32)
    par = np.zeros((DEPTH, P, N_PAR2), np.float32)
    small = np.zeros((DEPTH, P, 2560), np.float32)
    for l in range(DEPTH):
        def ffn(up, down):
            out = []
            for j in range(0, 22, 2):
                out += [job_block(up, [(x, x + P) for x in (j * P, D_FF + j * P, (j + 1) * P,
                                                            D_FF + (j + 1) * P)])]
            return out + [job_block(down[a:min(a + 512, D_FF)]) for a in range(0, D_FF, 512)]

        w = i["w_in_2"][l]
        jobs = ffn(i["ffn1_w_gu_2"][l], i["ffn1_w_down_2"][l])
        jobs += [job_block(w, [(a, a + 512)]) for a in range(0, 1536, 512)]
        jobs += [job_block(w, [(1536, 1960), (4008, 4024)])]
        jobs += [job_block(w, [(a, a + 512)]) for a in range(1960, 4008, 512)]
        jobs += [job_block(w, [(a, a + 512)]) for a in range(4024, 7096, 512)]
        jobs += [job_block(i[n][l]) for n in ("w_br_fox_2", "w_br_mla_2", "w_br_dn_2")]
        jobs += [job_block(i["w_out_2"][l, a:a + 512]) for a in (0, 512)]
        jobs += ffn(i["ffn2_w_gu_2"][l], i["ffn2_w_down_2"][l])
        for g, job in enumerate(jobs):
            fill(w2[l, g], job)
        table = {"ffn1_g": i["ffn1_norm_2"][l], "mix_g": i["mix_norm_2"][l],
                 "ffn2_g": i["ffn2_norm_2"][l], "fin_g": i["final_norm_2"],
                 "b_gate": i["b_gate_2"][l], "q_norm": i["mla_q_norm_2"][l],
                 "kv_norm": i["mla_kv_norm_2"][l], "dn_conv": i["dn_conv_w_2"][l].reshape(-1)}
        for name, v in table.items():
            fill(par[l, :, C2[name]:], cols_of(v))
        par[l, 0:HD, C2["o_norm"]] = i["dn_o_norm_2"][l]
        par[l, HD:P, C2["o_norm"]] = i["dn_o_norm_2"][l]
        par[l, 0:HEADS, C2["fox_b"]] = i["fox_b_f_2"][l]
        par[l, 0:HEADS, C2["a_log"]] = i["dn_a_log_2"][l]
        par[l, 0:HEADS, C2["dt_bias"]] = i["dn_dt_bias_2"][l]
        fill(small[l], job_block(i["mla_w_uq_2"][l]))
        small[l, :, 1536:] = i["mla_w_ukv_2"][l]
    return w2, par, small


def kernel(**inputs):
    import concourse.bacc as bacc
    from concourse.bass_utils import run_bass_kernel_spmd as run

    i = {k: np.asarray(v) for k, v in inputs.items()}
    w1, par1, small1 = pack_block1(i)
    w2, par2, small2 = pack_block2(i)
    xt = np.ascontiguousarray(i["x"][0].T.reshape(KT, P, T).transpose(1, 0, 2))
    pos = np.ascontiguousarray(i["positions_2"].astype(np.int32))
    arrays = {"w1": w1, "w2": w2, "par1": par1, "par2": par2, "small1": small1, "small2": small2,
              "xt": xt, "const": const_array(), "pos": pos}
    nc = bacc.Bacc("TRN2", target_bir_lowering=False, num_devices=1)
    aps = [nc.dram_tensor(n, a.shape, mybir.dt.from_np(a.dtype), kind="ExternalInput").ap()
           for n, a in arrays.items()]
    out = nc.dram_tensor("out", (P, KT, T), F32, kind="ExternalOutput").ap()
    hybrid_blocks(nc, *aps, out)
    got = run(nc, [arrays], core_ids=[0]).results[0]["out"]
    return np.ascontiguousarray(got.transpose(1, 0, 2).reshape(D, T).T)[None]
```

```python
from contextlib import ExitStack

import numpy as np
import concourse.bass as bass
from concourse import mybir

F32 = mybir.dt.float32
I32 = mybir.dt.int32
ALU = mybir.AluOpType
ACT = mybir.ActivationFunctionType
AX_X = mybir.AxisListType.X

P = 128
T = 256
NBLK = T // P
D = 1024
KT = D // P
DEPTH = 2
D_FF = 2816
MIX = 512
MT_ = MIX // P
HEADS = 8
HD = 64
RING = 3
SLOT = 2048
LEVELS = (1, 2, 4, 8, 16, 32, 64)
NEG = -1e30
TAKEN = -3e38
TOPK = min(256, T // 4)
EPS = 1e-6
GN_EPS = 64e-5
KAPPA = float(np.exp(-0.5))

W_SCALE = 256.0
X_SCALE = 8.0
H_SCALE = 4.0
F16 = mybir.dt.float16
PART_X = 1.0 / (W_SCALE * X_SCALE)
PART_H = 1.0 / (W_SCALE * H_SCALE)

A_R, A_K, A_V, A_WA, A_G = 0, 4, 8, 12, 13
B_Q, B_F, B_I, B_G = 14, 18, 22, 26
C_Q, C_K, C_QI, C_KI, C_V, C_WI = 30, 34, 36, 38, 39, 40
X_Q, X_K, X_V, X_F, X_CQ, X_CKV, X_KR, X_B, X_A, X_DQ, X_DK, X_DV, X_DZ = (
    0, 4, 8, 12, 13, 15, 16, 17, 18, 19, 23, 27, 31)
P_TILES = 41

PAR1 = [("mix_g", 8), ("mu", 14), ("w0", 4), ("a0", 4), ("k_k", 4), ("k_a", 4), ("r_k", 4),
        ("gn_g", 4), ("gn_b", 4), ("lb0", 4), ("lb1", 4), ("b_gn_g", 4), ("ffn_g", 8),
        ("conv_w", 132), ("conv_b", 44), ("layer", 1), ("fin_g", 8)]
PAR2 = [("ffn1_g", 8), ("mix_g", 8), ("ffn2_g", 8), ("fin_g", 8), ("b_gate", 24), ("q_norm", 2),
        ("kv_norm", 1), ("dn_conv", 48), ("o_norm", 1), ("fox_b", 1), ("a_log", 1), ("dt_bias", 1)]


def columns(table):
    at, out = 0, {}
    for name, n in table:
        out[name] = at
        at += n
    return out, at


C1, N_PAR1 = columns(PAR1)
C2, N_PAR2 = columns(PAR2)
N_PAR = max(N_PAR1, N_PAR2)

CONSTS = [("ident", P), ("ones", T), ("bones", P), ("rot", P), ("rotm", P), ("cbias", P),
          ("cbiasT", P), ("strict", P), ("incl", P), ("levels", len(LEVELS) * P),
          ("cos", T), ("sin", T), ("hsel", MT_ * P), ("invf", 1)]
CC, N_CONST = columns(CONSTS)

PAIR, BRANCH, ROWS = (8, 256), (4, 512), (2, 1024)
FFN_JOBS = [PAIR] * 22 + [ROWS] * 11
MERGE_JOBS = [BRANCH] * 6 + [PAIR] * 4
JOBS1 = [PAIR] * 20 + [(8, 4)] + [PAIR] * 12 + MERGE_JOBS + FFN_JOBS
JOBS2 = (FFN_JOBS + [PAIR] * 6 + [PAIR, (8, 160), (8, 24)] + [PAIR] * 8 + [PAIR] * 12
         + MERGE_JOBS + FFN_JOBS)
GATE_JOBS = 12
GATES_AT1 = 21
FFN_AT1 = len(JOBS1) - len(FFN_JOBS)
GATES_AT2 = len(FFN_JOBS) + 17
FFN_AT2 = len(JOBS2) - len(FFN_JOBS)


def const_array():
    c = np.zeros((P, N_CONST), np.float32)
    i = np.arange(P)
    c[:, CC["ident"]:][:, :P] = np.eye(P)
    c[:, CC["ones"]:][:, :T] = 1.0
    c[:, CC["bones"]:][:, :P] = (i[:, None] // HD == i[None, :] // HD)
    rot = np.zeros((P, P))
    rotm = np.zeros((P, P))
    for m in range(P):
        if m % HD < HD // 2:
            rot[m + HD // 2, m] = -1.0
        else:
            rot[m - HD // 2, m] = 1.0
    for m in range(16):
        rotm[HD + 16 + m, HD + m] = -1.0
        rotm[HD + m, HD + 16 + m] = 1.0
    c[:, CC["rot"]:][:, :P] = rot
    c[:, CC["rotm"]:][:, :P] = rotm
    c[:, CC["cbias"]:][:, :P] = np.where(i[None, :] > i[:, None], NEG, 0.0)
    c[:, CC["cbiasT"]:][:, :P] = np.where(i[:, None] > i[None, :], NEG, 0.0)
    c[:, CC["strict"]:][:, :P] = i[:, None] < i[None, :]
    c[:, CC["incl"]:][:, :P] = i[:, None] <= i[None, :]
    for n, b in enumerate(LEVELS):
        s, t = i[:, None], i[None, :]
        m = (s // (2 * b) == t // (2 * b)) & (s % (2 * b) < b) & (t % (2 * b) >= b)
        c[:, CC["levels"] + n * P:][:, :P] = m
    freq = np.float32(10000.0) ** (-np.arange(HD // 2, dtype=np.float32) * np.float32(2.0 / HD))
    ang = np.arange(T, dtype=np.float32)[None, :] * freq[i % (HD // 2)][:, None]
    c[:, CC["cos"]:][:, :T] = np.cos(ang)
    c[:, CC["sin"]:][:, :T] = np.sin(ang)
    for n in range(MT_):
        for h in range(HEADS):
            c[h, CC["hsel"] + n * P:][:P] = (i // HD + 2 * n == h)
    invf = np.float32(10000.0) ** (-np.arange(16, dtype=np.float32) / np.float32(16))
    c[HD:HD + 32, CC["invf"]] = np.concatenate([invf, invf])
    return c


class Signals:

    def __init__(self, nc):
        self.nc, self.by_name, self.stack = nc, {}, ExitStack()

    def __call__(self, name):
        if name not in self.by_name:
            self.by_name[name] = self.stack.enter_context(self.nc.semaphore(name))
        return self.by_name[name]

    def end(self):
        nums = sorted(s.num for s in self.by_name.values())
        assert nums == list(range(nums[0], nums[-1] + 1)), nums
        self.nc.all_engine_barrier(sems_to_clear=range(nums[0], nums[-1] + 1))
        self.stack.close()


def linker(eng, sig, own):
    count = {}

    def say(ins, name):
        count[name] = count.get(name, 0) + 1
        ins.then_inc(sig(name), 1)
        eng.wait_ge(sig(name), count[name])

    def link(ins):
        say(ins, own)

    def need(name, n=1):
        eng.wait_ge(sig(name), n)

    return link, say, need


class Memory:

    def __init__(self, nc, ctx):
        def sb(name, shape, dt=F32):
            return ctx.enter_context(nc.sbuf_tensor(name, shape, dt))

        self.ring = sb("weight_ring", [P, RING, SLOT])
        self.w_high = sb("weights_high", [P, RING, SLOT], F16)
        self.w_low = sb("weights_low", [P, RING, SLOT], F16)
        self.proj = sb("projected", [P, P_TILES, T])
        self.scratch = sb("scratch", [P, 64 * 256])
        self.h = sb("residual", [P, KT, T])
        self.u_high = sb("normed_high", [P, KT, T], F16)
        self.u_low = sb("normed_low", [P, KT, T], F16)
        self.y = sb("branch_out", [P, 3 * MT_, T])
        self.par = sb("parameters", [P, N_PAR])
        self.small_w = sb("small_weights", [P, 2560])
        self.const = sb("constants", [P, N_CONST])
        self.mla_cos = sb("mla_cos", [P, T])
        self.mla_sin = sb("mla_sin", [P, T])
        self.ps = ctx.enter_context(nc.psum_tensor("banks", [P, 8, 512], F32))
        self.gates = self.scratch[:, 40 * 256:64 * 256].rearrange("p (a t) -> p a t", t=T)

    def c(self, name, width=P):
        return self.const[:, CC[name]:CC[name] + width]


class Cutter:

    def __init__(self, buffer):
        self.buffer, self.at = buffer, 0

    def __call__(self, *shape):
        n = int(np.prod(shape))
        part = self.buffer[:, self.at:self.at + n]
        self.at += n
        assert self.at <= self.buffer.shape[1]
        if len(shape) == 1:
            return part
        names = "abcd"[:len(shape)]
        return part.rearrange("p (%s) -> p %s" % (" ".join(names), " ".join(names)),
                              **dict(zip(names, shape)))


class Stream:

    def __init__(self, mem, dram, jobs, full):
        self.mem, self.dram, self.jobs, self.full = mem, dram, jobs, full

    def load(self, sp, layer, g):
        nk, n = self.jobs[g]
        sp.dma_start(self.mem.ring[:, g % RING, 0:nk * n],
                     self.dram[bass.ds(layer, 1), g, :, 0:nk * n].rearrange("a p n -> (a p) n")
                     ).then_inc(self.full[g % RING], 16)

    def load_behind(self, sp, sig, layer, first, count):
        for n in range(count):
            if first + n + RING < len(self.jobs):
                sp.wait_ge(sig("lows"), n + 1)
                self.load(sp, layer, first + n + RING)

    def part(self, buffer, g):
        nk, n = self.jobs[g]
        return buffer[:, g % RING, 0:nk * n]

    def arrived(self, eng, g):
        eng.wait_ge(self.full[g % RING], 16 * (g // RING + 1))

    def high(self, act, nc, sig, g, used):
        self.arrived(act, g)
        if used:
            act.wait_ge(sig(used[0]), used[1])
        nc.scalar.activation(self.part(self.mem.w_high, g), self.part(self.mem.ring, g), ACT.Copy,
                             scale=W_SCALE).then_inc(sig("highs"), 1)

    def low(self, dve, nc, sig, g, n):
        dve.wait_ge(sig("highs"), n + 1)
        nc.vector.scalar_tensor_tensor(out=self.part(self.mem.w_low, g),
                                       in0=self.part(self.mem.ring, g), scalar=W_SCALE,
                                       in1=self.part(self.mem.w_high, g), op0=ALU.mult,
                                       op1=ALU.subtract).then_inc(sig("lows"), 1)

    def weight(self, g, k, c0, m):
        n = self.jobs[g][1]
        at = slice(k * n + c0, k * n + c0 + m)
        return self.mem.w_high[:, g % RING, at], self.mem.w_low[:, g % RING, at]


def product(pe, out, weight, high, low, start, stop, skip=False):
    w_high, w_low = weight
    pe.matmul(out, w_high, high, start=start, stop=False, skip_group_check=skip)
    pe.matmul(out, w_high, low, start=False, stop=False, skip_group_check=skip)
    return pe.matmul(out, w_low, high, start=False, stop=stop, skip_group_check=skip)


def split(nc, act, dve, sig, x, high, low, scale, name, n):
    if act is not None:
        nc.scalar.activation(high, x, ACT.Copy, scale=scale).then_inc(sig(name + "_high"), 1)
    else:
        dve.wait_ge(sig(name + "_high"), n)
        nc.vector.scalar_tensor_tensor(out=low, in0=x, scalar=scale, in1=high, op0=ALU.mult,
                                       op1=ALU.subtract).then_inc(sig(name + "_low"), 1)


def flat(ap):
    return ap.rearrange("p a t -> p (a t)")



class Norm:

    def __init__(self, mem, cut, gain):
        self.mem, self.gain = mem, gain
        self.sq, self.rstd, self.u = cut(KT, T), cut(T), cut(KT, T)

    def squares(self, nc, say):
        say(nc.vector.tensor_tensor(self.sq, self.mem.h[:], self.mem.h[:], ALU.mult), "squares")

    def sum(self, pe, sig):
        pe.wait_ge(sig("squares"), 1)
        for k in range(KT):
            mm = pe.matmul(self.mem.ps[:, 7, 0:T], self.mem.c("ones"), self.sq[:, k, :],
                           start=(k == 0), stop=(k == KT - 1))
        mm.then_inc(sig("square_sum"), 1)

    def mean(self, dve, nc, sig, say):
        dve.wait_ge(sig("square_sum"), 1)
        say(nc.vector.tensor_scalar(self.rstd, self.mem.ps[:, 7, 0:T], 1.0 / D, EPS,
                                    ALU.mult, ALU.add), "mean_square")

    def root(self, act, nc, sig, say):
        act.wait_ge(sig("mean_square"), 1)
        say(nc.scalar.activation(self.rstd, self.rstd, ACT.Sqrt), "root")

    def scale(self, dve, nc, sig, link, say, out=None):
        dve.wait_ge(sig("root"), 1)
        link(nc.vector.reciprocal(self.rstd, self.rstd))
        dst = self.u if out is None else out
        for k in range(KT):
            gain = self.mem.par[:, self.gain + k:self.gain + k + 1]
            say(nc.vector.scalar_tensor_tensor(out=dst[:, k, :], in0=self.mem.h[:, k, :],
                                               scalar=gain, in1=self.rstd, op0=ALU.mult,
                                               op1=ALU.mult), "normed")
            if out is None and k:
                self.pair(nc, sig, k - 1, dve=dve)
        if out is None:
            self.pair(nc, sig, KT - 1, dve=dve)

    def pair(self, nc, sig, k, act=None, dve=None):
        mem = self.mem
        split(nc, act, dve, sig, self.u[:, k, :], mem.u_high[:, k, :], mem.u_low[:, k, :],
              X_SCALE, "u", k + 1)

    def highs(self, act, nc, sig):
        for k in range(KT):
            act.wait_ge(sig("normed"), k + 1)
            self.pair(nc, sig, k, act=act)



def project_stage(nc, mem, sig, stream, layer, groups, first, gain, loads):
    norm = Norm(mem, Cutter(mem.scratch), gain)
    BANKS = 4
    jobs = sorted({t[0] for grp in groups for t in grp})
    used = {g: 1 + max(i for i, grp in enumerate(groups) if any(t[0] == g for t in grp))
            for g in jobs}

    def after(g):
        return ("tiles_done", used[g - RING]) if g - RING >= first else None

    with nc.Block() as block:
        @block.sync
        def _(sp):
            if first == 0:
                for g in range(RING):
                    stream.load(sp, layer, g)
            for load in loads:
                load(sp).then_inc(sig("params"), 16)
            stream.load_behind(sp, sig, layer, first, len(jobs))

        @block.vector
        def _(dve):
            link, say, need = linker(dve, sig, "dve_ops")
            norm.squares(nc, say)
            stream.low(dve, nc, sig, first, 0)
            norm.mean(dve, nc, sig, say)
            stream.low(dve, nc, sig, first + 1, 1)
            if loads:
                need("params", 16 * len(loads))
            norm.scale(dve, nc, sig, link, say)
            for n, g in enumerate(jobs[2:]):
                stream.low(dve, nc, sig, g, n + 2)

        @block.scalar
        def _(act):
            link, say, need = linker(act, sig, "act_ops")
            split_jobs = iter(jobs)
            for _ in range(2):
                stream.high(act, nc, sig, next(split_jobs), None)
            norm.root(act, nc, sig, say)
            norm.highs(act, nc, sig)
            stream.high(act, nc, sig, next(split_jobs), None)
            split_up_to = first + 2
            for i, grp in enumerate(groups):
                act.wait_ge(sig("tiles_done"), i + 1)
                for n, (g, c0, m, part, tile) in enumerate(grp):
                    ins = nc.scalar.activation(mem.proj[part:part + m, tile, :],
                                               mem.ps[part:part + m, i % BANKS, n * T:(n + 1) * T],
                                               ACT.Copy, scale=PART_X)
                ins.then_inc(sig("bank_free"), 1)
                while split_up_to < jobs[-1] and used[split_up_to + 1 - RING] <= i + 1:
                    split_up_to += 1
                    stream.high(act, nc, sig, split_up_to, after(split_up_to))

        @block.tensor
        def _(pe):
            norm.sum(pe, sig)
            seen = 0
            for i, grp in enumerate(groups):
                if i >= BANKS:
                    pe.wait_ge(sig("bank_free"), i - BANKS + 1)
                for n, (g, c0, m, part, tile) in enumerate(grp):
                    if g - first + 1 > seen:
                        seen = g - first + 1
                        pe.wait_ge(sig("lows"), seen)
                    for k in range(KT):
                        if i == 0 and n == 0:
                            pe.wait_ge(sig("u_low"), k + 1)
                        mm = product(pe, mem.ps[part:part + m, i % BANKS, n * T:(n + 1) * T],
                                     stream.weight(g, k, c0, m), mem.u_high[:, k, :],
                                     mem.u_low[:, k, :], k == 0, k == KT - 1)
                mm.then_inc(sig("tiles_done"), 1)
    sig.end()


def tile_groups(spec):
    return [spec[i:i + 2] for i in range(0, len(spec), 2)]



class Gates:

    def __init__(self, mem, stream, layer, first, a, b, banks, bias):
        self.mem, self.stream, self.layer, self.bias = mem, stream, layer, bias
        self.jobs = list(range(a, b))
        self.first, self.banks = first, banks

    def bank(self, n):
        return self.mem.ps[:, self.banks[n % len(self.banks)], :]

    def sync(self, sp, sig):
        self.stream.load_behind(sp, sig, self.layer, self.first + self.jobs[0], len(self.jobs))

    def high(self, act, nc, sig, n):
        st, g = self.stream, self.first + self.jobs[n]
        st.arrived(act, g)
        raw = st.part(self.mem.ring, g)
        nc.scalar.activation(raw, raw, ACT.Copy, scale=W_SCALE).then_inc(sig("scaled"), 1)
        act.wait_ge(sig("scaled"), n + 1)
        if n >= RING:
            act.wait_ge(sig("gate_done"), n - RING + 1)
        nc.scalar.copy(st.part(self.mem.w_high, g), raw).then_inc(sig("highs"), 1)

    def lows(self, pool, nc, sig):
        for n, j in enumerate(self.jobs):
            st, g = self.stream, self.first + j
            pool.wait_ge(sig("highs"), n + 1)
            nc.gpsimd.tensor_tensor(st.part(self.mem.w_low, g), st.part(self.mem.ring, g),
                                    st.part(self.mem.w_high, g), ALU.subtract
                                    ).then_inc(sig("lows"), 1)

    def fill(self, pe, sig, n):
        mem, g = self.mem, self.first + self.jobs[n]
        pe.wait_ge(sig("lows"), n + 1)
        if n >= len(self.banks):
            pe.wait_ge(sig("gates_out"), n - len(self.banks) + 1)
        for i in range(2):
            for k in range(KT):
                mm = product(pe, self.bank(n)[:, i * T:(i + 1) * T],
                             self.stream.weight(g, k, i * P, P), mem.u_high[:, k, :],
                             mem.u_low[:, k, :], k == 0, k == KT - 1)
        mm.then_inc(sig("gate_done"), 1)

    def out(self, act, nc, sig, n):
        act.wait_ge(sig("gate_done"), n + 1)
        j = self.jobs[n]
        if self.bias is None:
            ins = nc.scalar.activation(flat(self.mem.gates[:, 2 * j:2 * j + 2, :]), self.bank(n),
                                       ACT.Sigmoid, scale=PART_X)
        else:
            for i in range(2):
                at = self.bias + 2 * j + i
                ins = nc.scalar.activation(self.mem.gates[:, 2 * j + i, :],
                                           self.bank(n)[:, i * T:(i + 1) * T], ACT.Sigmoid,
                                           bias=self.mem.par[:, at:at + 1], scale=PART_X)
        ins.then_inc(sig("gates_out"), 1)

    def begin(self, act, nc, sig):
        for n in range(min(2, len(self.jobs))):
            self.high(act, nc, sig, n)

    def step(self, act, nc, sig, n):
        if n:
            self.out(act, nc, sig, n - 1)
        if n + 2 < len(self.jobs):
            self.high(act, nc, sig, n + 2)

    def end(self, act, nc, sig):
        self.out(act, nc, sig, len(self.jobs) - 1)


def gates_stage(nc, mem, sig, stream, layer, first, bias):
    gates = Gates(mem, stream, layer, first, 0, GATE_JOBS, (0, 1, 2, 3), bias)
    with nc.Block() as block:
        @block.sync
        def _(sp):
            gates.sync(sp, sig)

        @block.scalar
        def _(act):
            gates.begin(act, nc, sig)
            for n in range(GATE_JOBS):
                gates.step(act, nc, sig, n)
            gates.end(act, nc, sig)

        @block.gpsimd
        def _(pool):
            gates.lows(pool, nc, sig)

        @block.tensor
        def _(pe):
            for n in range(GATE_JOBS):
                gates.fill(pe, sig, n)
    sig.end()



def merge_stage(nc, mem, sig, stream, layer, first):
    y_pair = mem.proj[:, 0:3 * MT_, :].bitcast(F16)
    m_pair = mem.proj[:, 3 * MT_:3 * MT_ + KT, :].bitcast(F16)
    cut = Cutter(mem.scratch)
    merged, part = cut(KT, T), cut(2 * T)
    BR, WO = 12, 4
    jobs = list(range(first, first + 10))
    done = [2 * (n + 1) if n < 6 else BR + n - 5 for n in range(10)]

    def high(act, n):
        stream.high(act, nc, sig, jobs[n], ("tiles_done", done[n - RING]) if n >= RING else None)

    def pair(buffer, k):
        return buffer[:, k, 0:T], buffer[:, k, T:2 * T]

    with nc.Block() as block:
        @block.sync
        def _(sp):
            stream.load_behind(sp, sig, layer, first, len(jobs))

        @block.scalar
        def _(act):
            high(act, 0)
            for br in range(3):
                split(nc, act, None, sig, mem.y[:, MT_ * br:MT_ * (br + 1), :],
                      y_pair[:, MT_ * br:MT_ * (br + 1), 0:T], None, X_SCALE, "y", br + 1)
            high(act, 1)
            high(act, 2)
            for n in range(3, 9):
                high(act, n)
            for j in range(4):
                act.wait_ge(sig("merged"), 9 + j)
                split(nc, act, None, sig, merged[:, 2 * j:2 * j + 2, :],
                      m_pair[:, 2 * j:2 * j + 2, 0:T], None, X_SCALE, "m", j + 1)
            high(act, 9)

        @block.vector
        def _(dve):
            link, say, need = linker(dve, sig, "dve_ops")

            def low(n):
                stream.low(dve, nc, sig, jobs[n], n)

            low(0)
            for br in range(3):
                split(nc, None, dve, sig, mem.y[:, MT_ * br:MT_ * (br + 1), :],
                      y_pair[:, MT_ * br:MT_ * (br + 1), 0:T],
                      y_pair[:, MT_ * br:MT_ * (br + 1), T:2 * T], X_SCALE, "y", br + 1)
            low(1)
            low(2)
            for i in range(BR):
                br, j = divmod(i, 4)
                need("tiles_done", i + 1)
                g = flat(mem.gates[:, KT * br + 2 * j:KT * br + 2 * j + 2, :])
                m = flat(merged[:, 2 * j:2 * j + 2, :])
                dst = m if br == 0 else part
                ins = nc.vector.scalar_tensor_tensor(out=dst, in0=mem.ps[:, i % 4, :], scalar=PART_X,
                                                     in1=g, op0=ALU.mult, op1=ALU.mult)
                if br == 0:
                    say(ins, "merged")
                else:
                    link(ins)
                    say(nc.vector.tensor_tensor(m, m, part, ALU.add), "merged")
                if i % 2 and i // 2 + 3 < 9:
                    low(i // 2 + 3)
                if br == 2:
                    split(nc, None, dve, sig, merged[:, 2 * j:2 * j + 2, :],
                          m_pair[:, 2 * j:2 * j + 2, 0:T], m_pair[:, 2 * j:2 * j + 2, T:2 * T],
                          X_SCALE, "m", j + 1)
            low(9)
            for j in range(WO):
                need("tiles_done", BR + j + 1)
                h = flat(mem.h[:, 2 * j:2 * j + 2, :])
                say(nc.vector.scalar_tensor_tensor(out=h, in0=mem.ps[:, j, :], scalar=PART_X,
                                                   in1=h, op0=ALU.mult, op1=ALU.add), "residual")

        @block.tensor
        def _(pe):
            for i in range(BR):
                br, j = divmod(i, 4)
                if i >= 4:
                    pe.wait_ge(sig("merged"), i - 3)
                if i % 2 == 0:
                    pe.wait_ge(sig("lows"), i // 2 + 1)
                if j == 0:
                    pe.wait_ge(sig("y_low"), br + 1)
                for n in range(2):
                    for k in range(MT_):
                        mm = product(pe, mem.ps[:, i % 4, n * T:(n + 1) * T],
                                     stream.weight(jobs[i // 2], k, (2 * (j % 2) + n) * P, P),
                                     *pair(y_pair, MT_ * br + k), k == 0, k == MT_ - 1)
                mm.then_inc(sig("tiles_done"), 1)
            for j in range(WO):
                pe.wait_ge(sig("merged"), 9 + j)
                pe.wait_ge(sig("lows"), 6 + j + 1)
                for n in range(2):
                    for k in range(KT):
                        if j == 0 and n == 0 and k % 2 == 0:
                            pe.wait_ge(sig("m_low"), k // 2 + 1)
                        mm = product(pe, mem.ps[:, j, n * T:(n + 1) * T],
                                     stream.weight(jobs[6 + j], k, n * P, P), *pair(m_pair, k),
                                     k == 0, k == KT - 1)
                mm.then_inc(sig("tiles_done"), 1)
    sig.end()



def ffn_stage(nc, mem, sig, stream, layer, first, gain, conv, factor, loads=()):
    cut = Cutter(mem.scratch)
    norm = Norm(mem, cut, gain)
    RB = 3
    c, sg, hid, taps = cut(RB, 2, T), cut(RB, T), cut(RB, T), cut(132)
    PAIRS = D_FF // P
    hidden = mem.proj[:, 0:PAIRS, :].bitcast(F16)
    DOWN = PAIRS // 2
    jobs = list(range(first, first + PAIRS + DOWN))

    def high(act, n):
        stream.high(act, nc, sig, jobs[n], ("tiles_done", n - RING + 1) if n >= RING else None)

    def low(dve, n):
        stream.low(dve, nc, sig, jobs[n], n)

    def half(j, n, a=0, b=T):
        return mem.ps[:, j % 4, n * T + a:n * T + b]

    with nc.Block() as block:
        @block.sync
        def _(sp):
            if first == 0:
                for g in range(RING):
                    stream.load(sp, layer, g)
            for load in loads:
                load(sp).then_inc(sig("params"), 16)
            stream.load_behind(sp, sig, layer, first, len(jobs))

        @block.scalar
        def _(act):
            link, say, need = linker(act, sig, "act_ops")
            high(act, 0)
            high(act, 1)
            norm.root(act, nc, sig, say)
            norm.highs(act, nc, sig)
            high(act, 2)
            for j in range(PAIRS):
                need("tiles_done", j + 1)
                if j >= RB:
                    need("hidden_low", j - RB + 1)
                if conv:
                    for n in range(2):
                        col = 2 * 44 + j + 22 * n
                        b = conv[1] + j + 22 * n
                        ins = nc.scalar.activation(c[:, j % RB, n, :], half(j, n), ACT.Identity,
                                                   bias=mem.par[:, b:b + 1],
                                                   scale=taps[:, col:col + 1])
                    ins.then_inc(sig("tap_now"), 1)
                    high(act, j + 3)
                    need("convolved", j + 1)
                    say(nc.scalar.activation(sg[:, j % RB, :], c[:, j % RB, 0, :], ACT.Sigmoid),
                        "gate_sigmoid")
                else:
                    say(nc.scalar.activation(sg[:, j % RB, :], half(j, 0), ACT.Sigmoid,
                                             scale=PART_X), "gate_sigmoid")
                    high(act, j + 3)
                need("hidden", j + 1)
                split(nc, act, None, sig, hid[:, j % RB, :], hidden[:, j, 0:T], None, H_SCALE,
                      "hidden", j + 1)
            for n in range(PAIRS + 3, len(jobs)):
                high(act, n)

        @block.vector
        def _(dve):
            link, say, need = linker(dve, sig, "dve_ops")
            norm.squares(nc, say)
            low(dve, 0)
            norm.mean(dve, nc, sig, say)
            low(dve, 1)
            if loads:
                need("params", 16 * len(loads))
            if conv:
                link(nc.vector.tensor_scalar(taps, mem.par[:, conv[0]:conv[0] + 132], PART_X, None,
                                             ALU.mult))
            norm.scale(dve, nc, sig, link, say)
            low(dve, 2)
            for j in range(PAIRS):
                if conv:
                    need("tap_now", j + 1)
                    for lag in (1, 2):
                        for n in range(2):
                            col = (2 - lag) * 44 + j + 22 * n
                            ins = nc.vector.scalar_tensor_tensor(
                                out=c[:, j % RB, n, lag:T], in0=half(j, n, 0, T - lag),
                                scalar=taps[:, col:col + 1], in1=c[:, j % RB, n, lag:T],
                                op0=ALU.mult, op1=ALU.add)
                            if (lag, n) == (2, 1):
                                say(ins, "convolved")
                            else:
                                link(ins)
                    low(dve, j + 3)
                    need("gate_sigmoid", j + 1)
                    s, gate, val = sg[:, j % RB, :], c[:, j % RB, 0, :], c[:, j % RB, 1, :]
                    link(nc.vector.tensor_tensor(s, gate, s, ALU.mult))
                    say(nc.vector.tensor_tensor(hid[:, j % RB, :], s, val, ALU.mult), "hidden")
                else:
                    need("gate_sigmoid", j + 1)
                    s = sg[:, j % RB, :]
                    link(nc.vector.scalar_tensor_tensor(out=s, in0=half(j, 0), scalar=PART_X, in1=s,
                                                        op0=ALU.mult, op1=ALU.mult))
                    say(nc.vector.scalar_tensor_tensor(out=hid[:, j % RB, :], in0=half(j, 1),
                                                       scalar=PART_X, in1=s, op0=ALU.mult,
                                                       op1=ALU.mult), "hidden")
                    low(dve, j + 3)
                split(nc, None, dve, sig, hid[:, j % RB, :], hidden[:, j, 0:T],
                      hidden[:, j, T:2 * T], H_SCALE, "hidden", j + 1)
            for n in range(PAIRS + 3, len(jobs)):
                low(dve, n)
            need("tiles_done", len(jobs))
            for b in range(4):
                h = flat(mem.h[:, 2 * b:2 * b + 2, :])
                say(nc.vector.scalar_tensor_tensor(out=h, in0=mem.ps[:, 4 + b, :],
                                                   scalar=factor * PART_H, in1=h, op0=ALU.mult,
                                                   op1=ALU.add), "residual")

        @block.tensor
        def _(pe):
            norm.sum(pe, sig)
            for j in range(PAIRS):
                if j >= 4:
                    pe.wait_ge(sig("convolved" if conv else "hidden"), j - 3)
                pe.wait_ge(sig("lows"), j + 1)
                for n in range(2):
                    for k in range(KT):
                        if j == 0 and n == 0:
                            pe.wait_ge(sig("u_low"), k + 1)
                        mm = product(pe, half(j, n), stream.weight(jobs[j], k, n * P, P),
                                     mem.u_high[:, k, :], mem.u_low[:, k, :], k == 0, k == KT - 1)
                mm.then_inc(sig("tiles_done"), 1)
            for i in range(DOWN):
                n = PAIRS + i
                pe.wait_ge(sig("lows"), n + 1)
                pe.wait_ge(sig("hidden_low"), 2 * (i + 1))
                for o in range(KT):
                    for k in range(2):
                        x = hidden[:, 2 * i + k, :]
                        mm = product(pe, mem.ps[:, 4 + o // 2, (o % 2) * T:(o % 2 + 1) * T],
                                     stream.weight(jobs[n], k, o * P, P), x[:, 0:T], x[:, T:2 * T],
                                     i == 0 and k == 0 and o % 2 == 0,
                                     i == DOWN - 1 and k == 1, skip=True)
                mm.then_inc(sig("tiles_done"), 1)
    sig.end()



def final_norm_stage(nc, mem, sig, gain, store=None):
    norm = Norm(mem, Cutter(mem.scratch), gain)
    with nc.Block() as block:
        @block.vector
        def _(dve):
            link, say, need = linker(dve, sig, "dve_ops")
            norm.squares(nc, say)
            norm.mean(dve, nc, sig, say)
            norm.scale(dve, nc, sig, link, say, out=mem.h)

        @block.scalar
        def _(act):
            link, say, need = linker(act, sig, "act_ops")
            norm.root(act, nc, sig, say)

        @block.tensor
        def _(pe):
            norm.sum(pe, sig)

        if store is not None:
            @block.sync
            def _(sp):
                sp.wait_ge(sig("normed"), KT)
                sp.dma_start(store, mem.h[:]).then_inc(sig("stored"), 16)
                sp.wait_ge(sig("stored"), 16)
    sig.end()



class Solver:
    def __init__(self, mem, mt, t, tt, x, c):
        self.mem, self.mt, self.t, self.tt, self.x, self.c = mem, mt, t, tt, x, c

    def pool(self, pool, nc, sig, n):
        mem, LV = self.mem, len(LEVELS)
        pool.wait_ge(sig("masked"), n + 1)
        for lv in range(LV):
            if n or lv:
                pool.wait_ge(sig("c_used"), n * LV + lv)
            if lv == 1:
                pool.wait_ge(sig("t_ready"), 2 * (n * LV + 1))
            mask = mem.c("levels", LV * P)[:, lv * P:(lv + 1) * P]
            for g in range(2):
                hs = slice(4 * g, 4 * g + 4)
                ins = nc.gpsimd.tensor_tensor(self.c[:, hs, :], self.mt[:, hs, :],
                                              mask.unsqueeze(1).to_broadcast([P, 4, P]), ALU.mult)
                ins.then_inc(sig("c_ready"), 1)

    def tensor(self, pe, sig, n):
        mem, LV = self.mem, len(LEVELS)
        pe.wait_ge(sig("c_ready"), 2 * (n * LV + 1))
        for h in range(HEADS):
            mm = pe.transpose(mem.ps[:, h // 4, (h % 4) * P:(h % 4 + 1) * P], self.c[:, h, :],
                              mem.c("ident"))
        mm.then_inc(sig("c_used"), 1)
        for lv in range(1, LV):
            pe.wait_ge(sig("c_ready"), 2 * (n * LV + lv + 1))
            for g in range(2):
                pe.wait_ge(sig("t_ready"), 2 * (n * (LV) + lv - 1) + g + 1)
                for h in range(4 * g, 4 * g + 4):
                    mm = pe.matmul(mem.ps[:, g, (h % 4) * P:(h % 4 + 1) * P], self.c[:, h, :],
                                   self.t[:, h, :], start=True, stop=True)
                mm.then_inc(sig("x_summed" if g == 0 else "c_used"), 1)
            for g in range(2):
                pe.wait_ge(sig("x_ready"), 2 * (n * (LV - 1) + lv - 1) + g + 1)
                for h in range(4 * g, 4 * g + 4):
                    at = slice((h % 4) * P, (h % 4 + 1) * P)
                    mm = pe.matmul(mem.ps[:, 2 + g, at], self.x[:, h, :], self.tt[:, h, :],
                                   start=True, stop=True)
                    if lv < LV - 1:
                        mm = pe.matmul(mem.ps[:, 4 + g, at], self.tt[:, h, :], self.x[:, h, :],
                                       start=True, stop=True)
                mm.then_inc(sig("growth_summed"), 1)

    def scalar(self, act, nc, sig, n):
        mem, LV = self.mem, len(LEVELS)
        for lv in range(1, LV):
            for g in range(2):
                if g == 0:
                    act.wait_ge(sig("x_summed"), n * (LV - 1) + lv)
                else:
                    act.wait_ge(sig("c_used"), n * LV + lv + 1)
                nc.scalar.copy(self.x[:, 4 * g:4 * g + 4, :].rearrange("p h t -> p (h t)"),
                               mem.ps[:, g, :]).then_inc(sig("x_ready"), 1)

    def vector(self, dve, nc, sig, n, link, say):
        mem, LV = self.mem, len(LEVELS)
        eye = mem.c("ident").unsqueeze(1).to_broadcast([P, 4, P])

        def four(buffer, g):
            return buffer[:, 4 * g:4 * g + 4, :]

        def bank(b):
            return mem.ps[:, b, :].rearrange("p (h t) -> p h t", h=4)

        dve.wait_ge(sig("c_used"), n * LV + 1)
        for g in range(2):
            link(nc.vector.tensor_tensor(four(self.t, g), bank(g), eye, ALU.add))
            say(nc.vector.tensor_tensor(four(self.tt, g), four(self.c, g), eye, ALU.add), "t_ready")
        for lv in range(1, LV):
            for g in range(2):
                dve.wait_ge(sig("growth_summed"), 2 * (n * (LV - 1) + lv - 1) + g + 1)
                if lv < LV - 1:
                    link(nc.vector.tensor_tensor(four(self.t, g), four(self.t, g), bank(4 + g),
                                                 ALU.add))
                say(nc.vector.tensor_tensor(four(self.tt, g), four(self.tt, g), bank(2 + g),
                                            ALU.add), "t_ready")



def rwkv_stage(nc, mem, sig):
    cut = Cutter(mem.scratch)
    z = [cut(MT_, T) for _ in range(8)]
    ar = cut(MT_, 4, 2, HD)
    bt, kt, btp, ktp = cut(MT_, T), cut(MT_, T), cut(MT_, T), cut(MT_, T)
    rhs, sa, state, kh_t = cut(MIX), cut(MIX), cut(MT_, HD), cut(MIX)
    jump, one_ka, mids = cut(MT_, 2), cut(MT_), cut(MT_, 4)
    ps, par = mem.ps, mem.par
    p_r, p_k, p_v = (mem.proj[:, i:i + 4, :] for i in (A_R, A_K, A_V))
    wa, gd = mem.proj[:, A_WA, :], mem.proj[:, A_G, :]
    bonus, gate, out = mem.y[:, 4:8, :], mem.y[:, 8:12, :], mem.y[:, 0:4, :]
    w_up_a_up = mem.small_w[:, 0:MIX]
    g_up = mem.small_w[:, MIX:2 * MIX]
    mixed = cut.buffer[:, 0:14 * T].rearrange("p (a t) -> p a t", a=14)
    a_all = mem.proj[:, 0:14, :]
    b0, b1 = slice(0, P), slice(P, T)
    bh_t = mem.proj[:, A_WA:A_WA + 2, :].rearrange("p a t -> p (a t)")
    mt, t_, tt, x, c, qb, ak, qk = (
        zi.rearrange("p a t -> p (a t)").rearrange("p (h t) -> p h t", h=HEADS) for zi in z)
    solver = Solver(mem, mt, t_, tt, x, c)

    def flat(ap):
        return ap.rearrange("p a t -> p (a t)")

    def q64(ap):
        return flat(ap).rearrange("p (q t) -> p q t", t=HD)

    def two(b):
        return ps[:, b:b + 2, :].rearrange("p a (b t) -> p (a b) t", t=T)

    def col(name, i):
        return par[:, C1[name] + i:C1[name] + i + 1]

    def hp(s):
        return slice(HD * (s // 4), HD * (s // 4) + HD)

    with nc.Block() as block:
        @block.vector
        def _(dve):
            link, say, need = linker(dve, sig, "dve_ops")
            V = nc.vector
            link(V.tensor_tensor(mixed[:, :, 1:T], a_all[:, :, 0:T - 1], a_all[:, :, 1:T], ALU.subtract))
            link(V.tensor_scalar(mixed[:, :, 0:1], a_all[:, :, 0:1], -1.0, None, ALU.mult))
            for i in [12, 13] + list(range(12)):
                ins = V.scalar_tensor_tensor(out=a_all[:, i, :], in0=mixed[:, i, :], scalar=col("mu", i),
                                             in1=a_all[:, i, :], op0=ALU.mult, op1=ALU.add)
                say(ins, "shifted")
            for i in range(MT_):
                link(V.tensor_scalar(z[2][:, i, :], p_k[:, i, :], col("k_k", i), None, ALU.mult))
            say(V.tensor_tensor(flat(z[3]), flat(z[2]), flat(z[2]), ALU.mult), "kk_squares")
            need("kk_sum", 1)
            say(V.tensor_scalar(z[3], two(6), 1e-24, None, ALU.max), "kk_guarded")
            need("kk_root", 1)
            link(V.reciprocal(flat(z[3]), flat(z[3])))
            link(V.tensor_tensor(flat(z[2]), flat(z[2]), flat(z[3]), ALU.mult))
            need("decay_sigmoid", 4)
            for i in range(MT_):
                link(V.tensor_tensor_scan(z[4][:, i, :], mem.c("ones", T), z[0][:, i, :], 0.0,
                                          ALU.mult, ALU.add))
            link(V.tensor_copy(mids[:], q64(z[4]).rearrange("p (a q) t -> p a q t", q=4)[:, :, :, 31]))
            mid = flat(mids).unsqueeze(2).to_broadcast([P, 16, HD])
            link(V.tensor_tensor(q64(z[5]), q64(z[4]), mid, ALU.subtract))
            say(V.tensor_tensor(flat(z[6]), flat(z[5]), flat(z[0]), ALU.subtract), "sums_centred")
            m2 = mids.rearrange("p a (b q) -> p a b q", q=2)
            say(V.tensor_tensor(jump[:], m2[:, :, :, 1], m2[:, :, :, 0], ALU.subtract), "jump_sums")
            link(V.tensor_tensor(z[3], z[4], z[4][:, :, P - 1:P].to_broadcast([P, MT_, T]), ALU.subtract))
            say(V.tensor_tensor(z[4][:, :, b1], z[3][:, :, b1], z[0][:, :, b1], ALU.subtract), "sums_from_half")
            need("a_sigmoid", 4)
            link(V.tensor_scalar(one_ka, par[:, C1["k_a"]:C1["k_a"] + 4], -1.0, 1.0, ALU.mult, ALU.add))
            for i in range(MT_):
                link(V.tensor_scalar(z[7][:, i, :], z[1][:, i, :], col("k_a", i), one_ka[:, i:i + 1],
                                     ALU.mult, ALU.add))
            link(V.tensor_tensor(flat(p_k), flat(p_k), flat(z[7]), ALU.mult))
            for i in range(MT_):
                ins = V.scalar_tensor_tensor(out=z[7][:, i, :], in0=p_r[:, i, :], scalar=col("r_k", i),
                                             in1=p_k[:, i, :], op0=ALU.mult, op1=ALU.mult)
                say(ins, "rk")
            link(V.tensor_tensor(flat(z[1]), flat(z[1]), flat(z[2]), ALU.mult))
            need("bonus_sum", 1)
            say(V.tensor_tensor(bonus, two(0), p_v, ALU.mult), "bonus")
            need("exps", 3)
            link(V.scalar_tensor_tensor(out=ar.rearrange("p a q r t -> p (a q) r t")[:, :, 0, :],
                                        in0=q64(z[2]), scalar=-1.0, in1=q64(z[6]),
                                        op0=ALU.mult, op1=ALU.mult))
            link(V.tensor_tensor(ar.rearrange("p a q r t -> p (a q) r t")[:, :, 1, :],
                                 q64(p_r), q64(z[7]), ALU.mult))
            link(V.tensor_tensor(flat(bt), flat(z[1]), flat(z[5]), ALU.mult))
            link(V.tensor_tensor(flat(kt), flat(p_k), flat(z[5]), ALU.mult))
            need("exps", 7)
            for near, far in ((bt, btp), (kt, ktp)):
                n4, f4 = (v.rearrange("p a (b q t) -> p (a b) q t", b=2, q=2) for v in (near, far))
                link(V.tensor_copy(f4[:, :, 1, :], n4[:, :, 1, :]))
                link(V.tensor_tensor(f4[:, :, 0, :], n4[:, :, 0, :],
                                     flat(jump).unsqueeze(2).to_broadcast([P, 8, HD]), ALU.mult))
            link(V.tensor_tensor(p_r[:, :, b0], z[1][:, :, b0], z[3][:, :, b0], ALU.mult))
            link(V.tensor_tensor(p_r[:, :, b1], p_r[:, :, b1], z[3][:, :, b1], ALU.mult))
            link(V.tensor_tensor(p_k[:, :, b0], p_k[:, :, b0], z[3][:, :, b0], ALU.mult))
            say(V.scalar_tensor_tensor(out=p_k[:, :, b1], in0=z[2][:, :, b1], scalar=-1.0,
                                       in1=z[4][:, :, b1], op0=ALU.mult, op1=ALU.mult), "operands")
            need("turned", 1)
            say(V.tensor_copy(p_v, two(4)), "by_token")
            say(V.tensor_copy(bh_t, ps[:, 6, :]), "by_token")
            say(V.tensor_copy(kh_t, ps[:, 7, :]), "by_token")
            for n in range(NBLK):
                for kind, (seen_a, seen_r) in enumerate(((mt, qb), (ak, qk))):
                    for j in range(4):
                        need("pairs_summed", n * 8 + kind * 4 + j + 1)
                        src = ps[:, 4 * kind + j, :].rearrange("p (h q r t) -> p h q r t", h=2, q=2, r=2)
                        for r, (dst, mask) in enumerate(((seen_a, "strict"), (seen_r, "incl"))):
                            m = mem.c(mask).rearrange("p (q t) -> p q t", q=2).unsqueeze(1)
                            ins = V.tensor_tensor(
                                dst[:, 2 * j:2 * j + 2, :].rearrange("p h (q t) -> p h q t", q=2),
                                src[:, :, :, r, :], m.to_broadcast([P, 2, 2, HD]), ALU.mult)
                            if (kind, j, r) == (1, 3, 1):
                                say(ins, "masked")
                            else:
                                link(ins)
                solver.vector(dve, nc, sig, n, link, say)
                need("rhs_summed", n + 1)
                say(V.tensor_copy(rhs.rearrange("p (b a) -> p b a", b=2), ps[:, 6:8, 0:T]), "rhs")
                need("sa_summed", n + 1)
                say(V.tensor_copy(sa, ps[:, 4, :]), "sa")
                need("y_summed", n + 1)
                say(V.tensor_copy(out[:, :, n * P:n * P + P],
                                  ps[:, 0, :].rearrange("p (a t) -> p a t", a=MT_)), "y_out")
                if n == 0:
                    need("state_summed", 1)
                    say(V.tensor_copy(flat(state), ps[:, 1, 0:MT_ * HD]), "state")
            need("mean_sum", 1)
            link(V.scalar_tensor_tensor(out=z[0], in0=two(2), scalar=-1.0 / HD, in1=out,
                                        op0=ALU.mult, op1=ALU.add))
            say(V.tensor_tensor(flat(z[1]), flat(z[0]), flat(z[0]), ALU.mult), "deviations")
            need("var_sum", 1)
            say(V.tensor_scalar(z[1], two(4), 1.0 / HD, GN_EPS, ALU.mult, ALU.add), "variance")
            need("std", 1)
            link(V.reciprocal(flat(z[1]), flat(z[1])))
            link(V.tensor_tensor(flat(z[0]), flat(z[0]), flat(z[1]), ALU.mult))
            for i in range(MT_):
                link(V.tensor_scalar(z[0][:, i, :], z[0][:, i, :], col("gn_g", i), col("gn_b", i),
                                     ALU.mult, ALU.add))
            link(V.tensor_tensor(z[0], z[0], bonus, ALU.add))
            need("low_rank_gate", 1)
            link(V.tensor_tensor(out, z[0], gate, ALU.mult))

        @block.scalar
        def _(act):
            link, say, need = linker(act, sig, "act_ops")
            A = nc.scalar.activation
            need("shifted", 2)
            link(A(wa[0:HD, :], wa[0:HD, :], ACT.Tanh))
            say(A(gd, gd, ACT.Sigmoid), "low_rank_in")
            need("shifted", 14)
            need("up_summed", 3)
            for i in range(MT_):
                say(A(z[0][:, i, :], two(0)[:, i, :], ACT.Sigmoid, bias=col("w0", i)), "decay_sigmoid")
            for i in range(MT_):
                say(A(z[1][:, i, :], two(2)[:, i, :], ACT.Sigmoid, bias=col("a0", i)), "a_sigmoid")
            say(nc.scalar.copy(gate, two(4)), "low_rank_gate")
            need("kk_guarded", 1)
            say(A(flat(z[3]), flat(z[3]), ACT.Sqrt), "kk_root")
            need("sums_centred", 1)
            say(A(flat(z[6]), flat(z[6]), ACT.Exp, scale=-KAPPA), "exps")
            need("bonus", 1)
            say(A(flat(z[7]), flat(z[5]), ACT.Exp, scale=-KAPPA), "exps")
            say(A(flat(z[5]), flat(z[5]), ACT.Exp, scale=KAPPA), "exps")
            need("jump_sums", 1)
            say(A(jump[:], jump[:], ACT.Exp, scale=-KAPPA), "exps")
            need("sums_from_half", 1)
            say(A(z[4][:, :, b1], z[4][:, :, b1], ACT.Exp, scale=-KAPPA), "exps")
            say(A(z[3][:, :, b1], z[3][:, :, b1], ACT.Exp, scale=-KAPPA), "exps")
            say(A(z[3][:, :, b0], z[3][:, :, b0], ACT.Exp, scale=KAPPA), "exps")
            for n in range(NBLK):
                solver.scalar(act, nc, sig, n)
            need("variance", 1)
            say(A(flat(z[1]), flat(z[1]), ACT.Sqrt), "std")

        @block.gpsimd
        def _(pool):
            for n in range(NBLK):
                solver.pool(pool, nc, sig, n)

        @block.tensor
        def _(pe):
            def need(name, n=1):
                pe.wait_ge(sig(name), n)

            need("low_rank_in", 1)
            for w, (rows, src, b) in enumerate(((slice(0, HD), wa, 0), (slice(HD, P), wa, 2),
                                                (slice(0, P), gd, 4))):
                weight = g_up if w == 2 else w_up_a_up
                for i in range(MT_):
                    mm = pe.matmul(two(b)[:, i, :], weight[rows, i * P:(i + 1) * P], src[rows, :],
                                   start=True, stop=True)
                mm.then_inc(sig("up_summed"), 1)

            def head_sums(b, src, name):
                for i in range(2):
                    mm = pe.matmul(ps[:, b + i, :], mem.c("bones"), flat(src[:, 2 * i:2 * i + 2, :]),
                                   start=True, stop=True)
                mm.then_inc(sig(name), 1)

            need("kk_squares", 1)
            head_sums(6, z[3], "kk_sum")
            need("decay_sigmoid", 4)
            need("rk", 4)
            head_sums(0, z[7], "bonus_sum")
            need("operands", 1)
            need("low_rank_gate", 1)
            for i in range(MT_):
                for n in range(NBLK):
                    pe.transpose(ps[:, 4 + n, i * P:(i + 1) * P], p_v[:, i, n * P:(n + 1) * P],
                                 mem.c("ident"))
                pe.transpose(ps[:, 6, i * P:(i + 1) * P], p_r[:, i, b0], mem.c("ident"))
                mm = pe.transpose(ps[:, 7, i * P:(i + 1) * P], p_k[:, i, b0], mem.c("ident"))
            mm.then_inc(sig("turned"), 1)
            need("by_token", 3)

            def of_head(by_token, s, n=0):
                at = n * MIX + (2 * (s % 4) + s // 4) * HD
                return by_token[:, at:at + HD]

            def v_t(n, s):
                return of_head(flat(p_v), s, n)

            for n in range(NBLK):
                if n:
                    need("state", 1)
                for kind, (near, far) in enumerate(((bt, btp), (kt, ktp))):
                    for h in range(HEADS):
                        o = ps[:, 4 * kind + h // 2, (h % 2) * T:(h % 2 + 1) * T]
                        for q, left in enumerate((near, far)):
                            mm = pe.matmul(o[:, q * P:(q + 1) * P],
                                           left[hp(h), h % 4, n * P:(n + 1) * P],
                                           ar[hp(h), h % 4, 2 * n + q, :, :].rearrange("p r t -> p (r t)"),
                                           start=True, stop=True)
                        if h % 2:
                            mm.then_inc(sig("pairs_summed"), 1)
                need("masked", n + 1)
                solver.tensor(pe, sig, n)
                for h in range(HEADS):
                    o = ps[:, 6 + h // 4, (h % 4) * HD:(h % 4 + 1) * HD]
                    mm = pe.matmul(o, ak[:, h, :], v_t(n, h), start=True, stop=(n == 0))
                    if n:
                        mm = pe.matmul(o, p_k[hp(h), h % 4, b1], state[hp(h), h % 4, :],
                                       start=False, stop=True)
                mm.then_inc(sig("rhs_summed"), 1)
                need("rhs", n + 1)
                need("t_ready", 2 * len(LEVELS) * (n + 1))
                for h in range(HEADS):
                    mm = pe.matmul(ps[:, 4, h * HD:(h + 1) * HD], tt[:, h, :],
                                   rhs[:, h * HD:(h + 1) * HD], start=True, stop=True)
                mm.then_inc(sig("sa_summed"), 1)
                need("sa", n + 1)
                for h in range(HEADS):
                    o = ps[hp(h), 0, (h % 4) * P:(h % 4 + 1) * P]
                    pe.matmul(o, sa[:, h * HD:(h + 1) * HD], qb[:, h, :], start=True, stop=False)
                    mm = pe.matmul(o, v_t(n, h), qk[:, h, :], start=False, stop=(n == 0))
                    if n:
                        mm = pe.matmul(o, state[hp(h), h % 4, :], p_r[hp(h), h % 4, b1],
                                       start=False, stop=True)
                mm.then_inc(sig("y_summed"), 1)
                if n == 0:
                    for h in range(HEADS):
                        o = ps[hp(h), 1, (h % 4) * HD:(h % 4 + 1) * HD]
                        pe.matmul(o, of_head(bh_t, h), sa[:, h * HD:(h + 1) * HD],
                                  start=True, stop=False)
                        mm = pe.matmul(o, of_head(kh_t, h), v_t(n, h),
                                       start=False, stop=True)
                    mm.then_inc(sig("state_summed"), 1)
            need("y_out", 2)
            head_sums(2, out, "mean_sum")
            need("deviations", 1)
            head_sums(4, z[1], "var_sum")
    sig.end()



def hgrn_stage(nc, mem, sig):
    NH = MIX // P
    cut = Cutter(mem.scratch)
    key, cs, acc, vt = (cut(NH, T) for _ in range(4))
    diff = [cut(NH, T) for _ in range(2)]
    fac = [cut(NH, T) for _ in range(2)]
    far = cut(NH, P)
    t1, t2 = cut(NH, T), cut(NH, T)
    lb, lb_inv, lbt = cut(NH), cut(NH), cut(3, NH)
    ps, par = mem.ps, mem.par
    q, f, v, g = (mem.proj[:, i:i + 4, :] for i in (B_Q, B_F, B_I, B_G))
    out = mem.y[:, 4:8, :]
    ALL = (P,) + tuple(reversed(LEVELS))
    accs = acc.rearrange("p h t -> p (h t)").rearrange("p (g t) -> p g t", t=P)

    def flat(ap):
        return ap.rearrange("p a t -> p (a t)")

    def halves(ap, b):
        return flat(ap).rearrange("p (m h b) -> p m h b", h=2, b=b)

    def cols(name):
        return par[:, C1[name]:C1[name] + NH]

    def two(b):
        return ps[:, b:b + 2, :].rearrange("p a (b t) -> p (a b) t", t=T)

    with nc.Block() as block:
        @block.vector
        def _(dve):
            link, say, need = linker(dve, sig, "dve_ops")
            V = nc.vector
            link(V.tensor_tensor(lbt[:, 0, :], cols("lb0"), cols("lb1"), ALU.max))
            link(V.tensor_tensor(lbt[:, 1, :], cols("lb0"), lbt[:, 0, :], ALU.subtract))
            say(V.tensor_tensor(lbt[:, 2, :], cols("lb1"), lbt[:, 0, :], ALU.subtract), "lb_logits")
            link(V.scalar_tensor_tensor(out=flat(t1), in0=flat(f), scalar=-1.0, in1=flat(f),
                                        op0=ALU.mult, op1=ALU.max))
            say(V.tensor_scalar(flat(t2), flat(f), -40.0, None, ALU.max), "f_sizes")
            need("lb_exp", 1)
            link(V.tensor_tensor(lbt[:, 0, :], lbt[:, 1, :], lbt[:, 2, :], ALU.add))
            link(V.reciprocal(lbt[:, 0, :], lbt[:, 0, :]))
            link(V.scalar_tensor_tensor(out=lb, in0=lbt[:, 2, :],
                                        scalar=par[:, C1["layer"]:C1["layer"] + 1],
                                        in1=lbt[:, 0, :], op0=ALU.mult, op1=ALU.mult))
            say(V.tensor_scalar(lb_inv, lb, -1.0, 1.0, ALU.mult, ALU.add), "lower_bound")
            need("log_terms", 1 + NH)
            link(V.scalar_tensor_tensor(out=flat(t1), in0=flat(f), scalar=0.0, in1=flat(t1),
                                        op0=ALU.min, op1=ALU.subtract))
            link(V.tensor_tensor(flat(t1), flat(t1), flat(t2), ALU.add))
            for h in range(NH):
                link(V.tensor_tensor_scan(cs[:, h, :], mem.c("ones", T), t1[:, h, :], 0.0,
                                          ALU.mult, ALU.add))
            need("forget_inverse", 1)
            for h in range(NH):
                ins = V.tensor_scalar(key[:, h, :], key[:, h, :], lb_inv[:, h:h + 1], None, ALU.mult)
                say(ins, "keys")
            say(V.memset(flat(acc), 0.0), "cleared")
            need("values_turned", 1)
            say(V.tensor_copy(vt, two(0)), "values_by_token")

            def exponents(n):
                b = ALL[n]
                d, c = halves(diff[n % 2], b), halves(cs, b)
                r = c[:, :, 0, b - 1:b].to_broadcast([P, NH * T // (2 * b), b])
                link(V.tensor_tensor(d[:, :, 0, :], r, c[:, :, 0, :], ALU.subtract))
                say(V.tensor_tensor(d[:, :, 1, :], c[:, :, 1, :], r, ALU.subtract), "exponents")

            def gather(n):
                need("scores_summed", n + 1)
                if n == 0:
                    say(V.tensor_copy(flat(far), ps[:, 4, :]), "gathered")
                else:
                    src = ps[:, 4 + 2 * (n % 2):6 + 2 * (n % 2), :].rearrange("p a (b t) -> p (a b) t", t=P)
                    if n <= len(LEVELS):
                        lv = len(LEVELS) - n
                        m = mem.c("levels", len(LEVELS) * P)[:, lv * P:(lv + 1) * P]
                    else:
                        m = mem.c("ident")
                    say(V.copy_predicated(accs, m.unsqueeze(1).to_broadcast([P, 8, P]).bitcast(I32),
                                          src), "gathered")

            exponents(0)
            for n in range(len(ALL)):
                if n + 1 < len(ALL):
                    exponents(n + 1)
                need("decays", n + 1)
                d, o, b = halves(diff[n % 2], ALL[n]), halves(fac[n % 2], ALL[n]), ALL[n]
                if n >= 2:
                    need("scores_summed", n - 1)
                link(V.tensor_tensor(o[:, :, 0, :], halves(key, b)[:, :, 0, :], d[:, :, 0, :], ALU.mult))
                say(V.tensor_tensor(o[:, :, 1, :], halves(q, b)[:, :, 1, :], d[:, :, 1, :], ALU.mult),
                    "factors")
                if n:
                    gather(n - 1)
            gather(len(ALL) - 1)
            gather(len(ALL))
            need("out_summed", 1)
            link(V.tensor_copy(t1, two(0)))
            say(V.tensor_tensor(flat(t2), flat(t1), flat(t1), ALU.mult), "out_squares")
            need("out_square_sum", 1)
            say(V.tensor_scalar(t2, two(2), 1.0 / P, EPS, ALU.mult, ALU.add), "out_mean_square")
            need("out_root", 1)
            link(V.reciprocal(flat(t2), flat(t2)))
            link(V.tensor_tensor(flat(t1), flat(t1), flat(t2), ALU.mult))
            need("gate_sigmoid", 1)
            link(V.tensor_tensor(flat(g), flat(g), flat(key), ALU.mult))
            for h in range(NH):
                link(V.scalar_tensor_tensor(out=out[:, h, :], in0=t1[:, h, :],
                                            scalar=par[:, C1["b_gn_g"] + h:C1["b_gn_g"] + h + 1],
                                            in1=g[:, h, :], op0=ALU.mult, op1=ALU.mult))

        @block.scalar
        def _(act):
            link, say, need = linker(act, sig, "act_ops")
            A = nc.scalar.activation
            need("lb_logits", 1)
            say(A(lbt[:, 1:3, :], lbt[:, 1:3, :], ACT.Exp), "lb_exp")
            need("f_sizes", 1)
            link(A(flat(t1), flat(t1), ACT.Exp, scale=-1.0))
            link(A(flat(t2), flat(t2), ACT.Exp, scale=-1.0))
            say(A(flat(t1), flat(t1), ACT.Ln, bias=1.0), "log_terms")
            need("lower_bound", 1)
            for h in range(NH):
                say(A(t2[:, h, :], t2[:, h, :], ACT.Ln, bias=1.0, scale=lb[:, h:h + 1]), "log_terms")
            say(A(flat(key), flat(f), ACT.Sigmoid, scale=-1.0), "forget_inverse")
            for n in range(len(ALL)):
                need("exponents", n + 1)
                say(A(flat(diff[n % 2]), flat(diff[n % 2]), ACT.Exp), "decays")
            need("scores_summed", len(ALL) + 1)
            say(A(flat(key), flat(g), ACT.Sigmoid), "gate_sigmoid")
            need("out_mean_square", 1)
            say(A(flat(t2), flat(t2), ACT.Sqrt), "out_root")

        @block.tensor
        def _(pe):
            def need(name, n=1):
                pe.wait_ge(sig(name), n)

            for n in range(NBLK):
                for h in range(NH):
                    mm = pe.transpose(ps[:, n, h * P:(h + 1) * P], v[:, h, n * P:(n + 1) * P],
                                      mem.c("ident"))
            mm.then_inc(sig("values_turned"), 1)
            for n in range(len(ALL) + 1):
                if n < len(ALL):
                    need("factors", n + 1)
                    left = right = fac[n % 2]
                else:
                    left, right = key, q
                if n >= 2:
                    need("gathered", n - 1)
                for h in range(NH):
                    if n == 0:
                        mm = pe.matmul(ps[:, 4, h * P:(h + 1) * P], left[:, h, 0:P], right[:, h, P:T],
                                       start=True, stop=True)
                        continue
                    for blk in range(NBLK):
                        i = 2 * h + blk
                        mm = pe.matmul(ps[:, 4 + 2 * (n % 2) + i // 4, (i % 4) * P:(i % 4 + 1) * P],
                                       left[:, h, blk * P:(blk + 1) * P],
                                       right[:, h, blk * P:(blk + 1) * P], start=True, stop=True)
                mm.then_inc(sig("scores_summed"), 1)
            need("gathered", len(ALL) + 1)
            need("values_by_token", 1)
            for h in range(NH):
                o = two(0)[:, h, :]
                v0, v1 = (flat(vt)[:, n * MIX + h * P:n * MIX + (h + 1) * P] for n in range(2))
                pe.matmul(o[:, 0:P], v0, accs[:, 2 * h, :], start=True, stop=True)
                pe.matmul(o[:, P:T], v0, far[:, h, :], start=True, stop=False)
                mm = pe.matmul(o[:, P:T], v1, accs[:, 2 * h + 1, :], start=False, stop=True)
            mm.then_inc(sig("out_summed"), 1)
            need("out_squares", 1)
            for i in range(2):
                mm = pe.matmul(ps[:, 2 + i, :], mem.c("ones"), flat(t2[:, 2 * i:2 * i + 2, :]),
                               start=True, stop=True)
            mm.then_inc(sig("out_square_sum"), 1)
    sig.end()



class Attention:

    def __init__(self, mem, cut, q, k, v, scale, bias):
        self.mem, self.q, self.k, self.v, self.scale, self.bias = mem, q, k, v, scale, bias
        self.prob = [cut(T) for _ in range(3)]
        self.turned = [cut(T) for _ in range(3)]
        self.low, self.sums = cut(16), cut(16)
        self.units = [(h, n) for n in range(NBLK) for h in range(HEADS)]

    def vector(self, dve, nc, sig, link, say):
        V = nc.vector
        for i in range(len(self.units) + 1):
            if i < len(self.units):
                w = P * (self.units[i][1] + 1)
                dve.wait_ge(sig("scores"), i + 1)
                link(V.tensor_reduce(self.low[:, i:i + 1], self.mem.ps[:, i % 3, 0:w], AX_X, ALU.max))
                say(V.tensor_scalar(self.low[:, i:i + 1], self.low[:, i:i + 1], -self.scale, None,
                                    ALU.mult), "row_max")
            if i:
                j = i - 1
                w = P * (self.units[j][1] + 1)
                dve.wait_ge(sig("prob"), j + 1)
                link(V.reciprocal(self.sums[:, j:j + 1], self.sums[:, j:j + 1]))
                say(V.tensor_scalar(self.prob[j % 3][:, 0:w], self.prob[j % 3][:, 0:w],
                                    self.sums[:, j:j + 1], None, ALU.mult), "prob_scaled")

    def scalar(self, act, nc, sig, say):
        for i in range(len(self.units) + 2):
            if i < len(self.units):
                w = P * (self.units[i][1] + 1)
                act.wait_ge(sig("row_max"), i + 1)
                if i >= 3:
                    act.wait_ge(sig("prob_turned"), i - 2)
                say(nc.scalar.activation(self.prob[i % 3][:, 0:w], self.mem.ps[:, i % 3, 0:w], ACT.Exp,
                                         bias=self.low[:, i:i + 1], scale=self.scale,
                                         accum_out=self.sums[:, i:i + 1]), "prob")
            if i >= 2:
                j = i - 2
                w = P * (self.units[j][1] + 1)
                act.wait_ge(sig("prob_turned"), j + 1)
                if j >= 3:
                    act.wait_ge(sig("attended"), j - 2)
                say(nc.scalar.copy(self.turned[j % 3][:, 0:w], self.mem.ps[:, 3 + j % 2, 0:w]),
                    "turned_out")

    def tensor(self, pe, sig):
        mem, n_units = self.mem, len(self.units)
        for i in range(n_units + 4):
            if i < n_units:
                h, n = self.units[i]
                w = P * (n + 1)
                if i >= 3:
                    pe.wait_ge(sig("prob"), i - 2)
                o = mem.ps[:, i % 3, 0:w]
                pe.matmul(o, self.q(h)[:, n * P:(n + 1) * P], self.k(h)[:, 0:w], start=True, stop=False)
                self.bias(pe, mem.ps[:, i % 3, :], h, n).then_inc(sig("scores"), 1)
            if 2 <= i < n_units + 2:
                j = i - 2
                n = self.units[j][1]
                pe.wait_ge(sig("prob_scaled"), j + 1)
                if j >= 2:
                    pe.wait_ge(sig("turned_out"), j - 1)
                for b in range(n + 1):
                    mm = pe.transpose(mem.ps[:, 3 + j % 2, b * P:(b + 1) * P],
                                      self.prob[j % 3][:, b * P:(b + 1) * P], mem.c("ident"))
                mm.then_inc(sig("prob_turned"), 1)
            if i >= 4:
                j = i - 4
                h, n = self.units[j]
                pe.wait_ge(sig("turned_out"), j + 1)
                rows = slice(HD * (h % 2), HD * (h % 2) + HD)
                o = mem.ps[rows, 5 + n, (h // 2) * P:(h // 2 + 1) * P]
                for b in range(n + 1):
                    mm = pe.matmul(o, self.v(h, b), self.turned[j % 3][:, b * P:(b + 1) * P],
                                   start=(b == 0), stop=(b == n))
                mm.then_inc(sig("attended"), 1)

    def out_of_psum(self, dve, nc, sig, link, out):
        for n in range(NBLK):
            dve.wait_ge(sig("attended"), HEADS * (n + 1))
            link(nc.vector.tensor_copy(out[:, :, n * P:(n + 1) * P],
                                       self.mem.ps[:, 5 + n, :].rearrange("p (a t) -> p a t", a=MT_)))


def rope(dve_v, link, say, x, turned, cos, sin, name):
    n = x.shape[1]
    r = x.shape[0]
    link(dve_v.tensor_tensor(turned, turned, sin.unsqueeze(1).to_broadcast([r, n, T]), ALU.mult))
    link(dve_v.tensor_tensor(x, x, cos.unsqueeze(1).to_broadcast([r, n, T]), ALU.mult))
    say(dve_v.tensor_tensor(x, x, turned, ALU.add), name)



def dsa_stage(nc, mem, sig):
    cut = Cutter(mem.scratch)
    score = [cut(T) for _ in range(NBLK)]
    bias = [cut(T) for _ in range(NBLK)]
    part, wi, top, vt = cut(T), cut(NBLK, 4), cut(8), cut(NBLK, P)
    ps = mem.ps
    x = mem.proj[:, C_Q:C_KI + 1, :]
    qi, ki = mem.proj[:, C_QI:C_QI + 2, :], mem.proj[:, C_KI, :]
    NT = C_KI + 1 - C_Q

    def rows(h):
        return slice(HD * (h % 2), HD * (h % 2) + HD)

    def tiles(b, n):
        return ps[:, b:b + (n + 1) // 2, :].rearrange("p a (b t) -> p (a b) t", t=T)[:, 0:n, :]

    def add_bias(pe, o, h, n):
        w = P * (n + 1)
        return pe.matmul(o[:, 0:w], mem.c("ident"), bias[n][:, 0:w], start=False, stop=True)

    att = Attention(mem, cut,
                    q=lambda h: mem.proj[rows(h), C_Q + h // 2, :],
                    k=lambda h: mem.proj[rows(h), C_K + h // 4, :],
                    v=lambda h, b: vt[:, b, HD * (h // 4):HD * (h // 4) + HD],
                    scale=HD ** -0.5, bias=add_bias)

    with nc.Block() as block:
        @block.vector
        def _(dve):
            link, say, need = linker(dve, sig, "dve_ops")
            V = nc.vector
            need("halves_swapped", 1)
            rope(V, link, say, x, tiles(0, NT), mem.c("cos", T), mem.c("sin", T), "roped")
            need("by_token", 1)
            say(V.tensor_copy(vt, ps[:, 5, 0:T].rearrange("p (n d) -> p n d", n=NBLK)), "values")
            say(V.tensor_scalar(wi, ps[:, 5, T:T + 8].rearrange("p (n j) -> p n j", n=NBLK),
                                4 ** -0.5 * HD ** -0.5, None, ALU.mult), "values")
            for n in range(NBLK):
                w = P * (n + 1)
                need("dots", n + 1)
                for j in range(4):
                    src = ps[:, 2 * n + j % 2, (j // 2) * T:(j // 2) * T + w]
                    dst = score[n] if j == 0 else part
                    link(V.tensor_scalar(dst[:, 0:w], src, 0.0, wi[:, n, j:j + 1], ALU.max, ALU.mult))
                    if j:
                        link(V.tensor_tensor(score[n][:, 0:w], score[n][:, 0:w], part[:, 0:w], ALU.add))
                diag = slice(n * P, (n + 1) * P)
                link(V.tensor_tensor(score[n][:, diag], score[n][:, diag], mem.c("cbias"), ALU.add))
                for _ in range(TOPK // 8):
                    link(V.max(top, score[n][:, 0:w]))
                    link(V.match_replace(score[n][:, 0:w], top, score[n][:, 0:w], TAKEN))
                link(V.tensor_scalar(bias[n][:, 0:w], score[n][:, 0:w], TAKEN / 2, NEG,
                                     ALU.is_gt, ALU.mult))
                say(V.tensor_tensor(bias[n][:, diag], bias[n][:, diag], mem.c("cbias"), ALU.add),
                    "key_bias")
            att.vector(dve, nc, sig, link, say)
            att.out_of_psum(dve, nc, sig, link, mem.y[:, 8:12, :])

        @block.scalar
        def _(act):
            link, say, need = linker(act, sig, "act_ops")
            att.scalar(act, nc, sig, say)

        @block.tensor
        def _(pe):
            def need(name, n=1):
                pe.wait_ge(sig(name), n)

            for i in range(NT):
                mm = pe.matmul(tiles(0, NT)[:, i, :], mem.c("rot"), x[:, i, :], start=True, stop=True)
            mm.then_inc(sig("halves_swapped"), 1)
            need("roped", 1)
            for n in range(NBLK):
                pe.transpose(ps[:, 5, n * P:(n + 1) * P], mem.proj[:, C_V, n * P:(n + 1) * P],
                             mem.c("ident"))
                mm = pe.transpose(ps[:, 5, T + 4 * n:T + 4 * n + 4],
                                  mem.proj[0:4, C_WI, n * P:(n + 1) * P],
                                  mem.c("ident")[0:4, 0:4])
            mm.then_inc(sig("by_token"), 1)
            for n in range(NBLK):
                w = P * (n + 1)
                for j in range(4):
                    mm = pe.matmul(ps[:, 2 * n + j % 2, (j // 2) * T:(j // 2) * T + w],
                                   qi[rows(j), j // 2, n * P:(n + 1) * P], ki[rows(j), 0:w],
                                   start=True, stop=True)
                mm.then_inc(sig("dots"), 1)
            need("values", 2)
            need("key_bias", NBLK)
            att.tensor(pe, sig)
    sig.end()



def mla_angles_stage(nc, mem, sig, pos):
    cut = Cutter(mem.scratch)
    where, angle, turns = cut(T), cut(T), cut(T)
    whole = cut(T)
    PI2 = 2 * np.pi
    HI = float(np.float32(np.floor(PI2 * 512) / 512))
    MID = float(np.float32(np.floor((PI2 - HI) * 2 ** 21) / 2 ** 21))
    LOW = float(np.float32(PI2 - HI - MID))
    with nc.Block() as block:
        @block.sync
        def _(sp):
            sp.dma_start(where.bitcast(I32), pos.to_broadcast([P, T])).then_inc(sig("positions"), 16)

        @block.vector
        def _(dve):
            link, say, need = linker(dve, sig, "dve_ops")
            V = nc.vector
            need("positions", 16)
            link(V.tensor_copy(angle, where.bitcast(I32)))
            link(V.tensor_scalar(angle, angle, mem.const[:, CC["invf"]:CC["invf"] + 1], None, ALU.mult))
            for out, quarter in ((mem.mla_sin, 0.0), (mem.mla_cos, 0.25)):
                link(V.tensor_scalar(turns, angle, 1.0 / PI2, quarter, ALU.mult, ALU.add))
                link(V.tensor_copy(whole.bitcast(I32), turns))
                link(V.tensor_copy(turns, whole.bitcast(I32)))
                link(V.scalar_tensor_tensor(out=out[:], in0=turns, scalar=-HI, in1=angle,
                                            op0=ALU.mult, op1=ALU.add))
                link(V.scalar_tensor_tensor(out=out[:], in0=turns, scalar=-MID, in1=out[:],
                                            op0=ALU.mult, op1=ALU.add))
                link(V.scalar_tensor_tensor(out=out[:], in0=turns, scalar=-LOW, in1=out[:],
                                            op0=ALU.mult, op1=ALU.add))
                link(V.tensor_scalar(out[:], out[:], quarter * PI2, float(np.float32(3.1415925)),
                                     ALU.add, ALU.min))
                say(V.tensor_scalar(out[:], out[:], -float(np.float32(3.1415925)), None, ALU.max),
                    "reduced")

        @block.scalar
        def _(act):
            link, say, need = linker(act, sig, "act_ops")
            for n, out in enumerate((mem.mla_sin, mem.mla_cos)):
                need("reduced", n + 1)
                link(nc.scalar.activation(out[:], out[:], ACT.Sin))
    sig.end()


def in_groups_2():
    at = len(FFN_JOBS)
    groups = tile_groups([(at + i // 2, (i % 2) * P, P, 0, X_Q + i) for i in range(12)])
    groups += [[(at + 6, 0, P, 0, X_CQ), (at + 6, P, P, 0, X_CQ + 1)]]
    groups += [[(at + 7, 0, P, 0, X_CKV)], [(at + 7, P, 32, HD, X_KR)]]
    groups += [[(at + 8, 0, 8, 0, X_F), (at + 8, 8, 8, 0, X_B)], [(at + 8, 16, 8, 0, X_A)]]
    groups += tile_groups([(at + 9 + i // 2, (i % 2) * P, P, 0, X_DQ + i) for i in range(16)])
    return groups



def fox_stage(nc, mem, sig):
    cut = Cutter(mem.scratch)
    vt, logf, size, c8 = cut(NBLK, MIX), cut(T), cut(T), cut(T)
    ps, par = mem.ps, mem.par
    f = mem.proj[0:HEADS, X_F, :]
    logf, size, c8 = (b[0:HEADS, :] for b in (logf, size, c8))
    bias = par[0:HEADS, C2["fox_b"]:C2["fox_b"] + 1]

    def rows(h):
        return slice(HD * (h % 2), HD * (h % 2) + HD)

    def add_bias(pe, o, h, n):
        pe.matmul(o[:, 0:P * (n + 1)], mem.c("ident")[0:HEADS, h:h + 1].to_broadcast([HEADS, P]),
                  c8[:, 0:P * (n + 1)], start=False, stop=False)
        return pe.matmul(o[:, n * P:(n + 1) * P], mem.c("ident"), mem.c("cbias"),
                         start=False, stop=True)

    att = Attention(mem, cut,
                    q=lambda h: mem.proj[rows(h), X_Q + h // 2, :],
                    k=lambda h: mem.proj[rows(h), X_K + h // 2, :],
                    v=lambda h, b: vt[:, b, h * HD:(h + 1) * HD],
                    scale=HD ** -0.5, bias=add_bias)

    with nc.Block() as block:
        @block.vector
        def _(dve):
            link, say, need = linker(dve, sig, "dve_ops")
            V = nc.vector
            link(V.tensor_scalar(f, f, bias, None, ALU.add))
            say(V.scalar_tensor_tensor(out=size, in0=f, scalar=-1.0, in1=f, op0=ALU.mult, op1=ALU.max),
                "f_size")
            need("values_turned", 1)
            say(V.tensor_copy(vt, ps[:, 0:2, :]), "values")
            need("log_term", 1)
            link(V.scalar_tensor_tensor(out=logf, in0=f, scalar=0.0, in1=size, op0=ALU.min,
                                        op1=ALU.subtract))
            link(V.tensor_tensor_scan(c8, mem.c("ones", T)[0:HEADS, :], logf, 0.0, ALU.mult, ALU.add))
            say(V.tensor_scalar(c8, c8, -float(HD ** 0.5), None, ALU.mult), "forget_sums")
            att.vector(dve, nc, sig, link, say)
            att.out_of_psum(dve, nc, sig, link, mem.y[:, 0:4, :])

        @block.scalar
        def _(act):
            link, say, need = linker(act, sig, "act_ops")
            need("f_size", 1)
            link(nc.scalar.activation(size, size, ACT.Exp, scale=-1.0))
            say(nc.scalar.activation(size, size, ACT.Ln, bias=1.0), "log_term")
            att.scalar(act, nc, sig, say)

        @block.tensor
        def _(pe):
            for n in range(NBLK):
                for i in range(MT_):
                    mm = pe.transpose(ps[:, n, i * P:(i + 1) * P],
                                      mem.proj[:, X_V + i, n * P:(n + 1) * P], mem.c("ident"))
            mm.then_inc(sig("values_turned"), 1)
            pe.wait_ge(sig("values"), 1)
            pe.wait_ge(sig("forget_sums"), 1)
            att.tensor(pe, sig)
    sig.end()



def mla_stage(nc, mem, sig):
    W = HD + 32
    cut = Cutter(mem.scratch)
    qf, kf, vt = cut(HEADS, T), cut(HEADS, T), cut(NBLK, MIX)
    sq, rstd = cut(3, T), cut(2, T)
    ps, par = mem.ps, mem.par
    c_all = mem.proj[:, X_CQ:X_CKV + 1, :]
    kr = mem.proj[HD:W, X_KR:X_KR + 1, :]
    w_uq = mem.small_w[:, 0:1536].rearrange("p (k n) -> p k n", k=2)
    w_ukv = mem.small_w[:, 1536:2560]

    def tiles(b, n):
        return ps[:, b:b + (n + 1) // 2, :].rearrange("p a (b t) -> p (a b) t", t=T)[:, 0:n, :]

    def add_bias(pe, o, h, n):
        return pe.matmul(o[:, n * P:(n + 1) * P], mem.c("ident"), mem.c("cbias"),
                         start=False, stop=True)

    att = Attention(mem, cut, q=lambda h: qf[0:W, h, :], k=lambda h: kf[0:W, h, :],
                    v=lambda h, b: vt[:, b, h * HD:(h + 1) * HD], scale=W ** -0.5, bias=add_bias)

    with nc.Block() as block:
        @block.vector
        def _(dve):
            link, say, need = linker(dve, sig, "dve_ops")
            V = nc.vector
            say(V.tensor_tensor(sq, c_all, c_all, ALU.mult), "squares")
            need("square_sums", 1)
            link(V.tensor_scalar(rstd[:, 0, :], ps[:, 0, 0:T], 1.0 / 256, EPS, ALU.mult, ALU.add))
            say(V.tensor_scalar(rstd[:, 1, :], ps[:, 1, 0:T], 1.0 / 128, EPS, ALU.mult, ALU.add),
                "mean_squares")
            need("roots", 1)
            link(V.reciprocal(rstd, rstd))
            for i in range(3):
                g = C2["q_norm"] + i
                say(V.scalar_tensor_tensor(out=c_all[:, i, :], in0=c_all[:, i, :],
                                           scalar=par[:, g:g + 1], in1=rstd[:, i // 2, :],
                                           op0=ALU.mult, op1=ALU.mult), "latents")
            need("queries_out", 1)
            need("queries_swapped", 1)
            rope(V, link, say, qf[0:W], tiles(4, HEADS)[0:W], mem.mla_cos[0:W, :],
                 mem.mla_sin[0:W, :], "roped")
            need("key_swapped", 1)
            rope(V, link, say, kr, ps[HD:W, 0:1, 0:T], mem.mla_cos[HD:W, :], mem.mla_sin[HD:W, :],
                 "roped")
            say(V.tensor_copy(kf[HD:W], kr.to_broadcast([32, HEADS, T])), "keys")
            need("keys_summed", 1)
            say(V.tensor_copy(kf[0:HD], tiles(4, HEADS)[0:HD]), "keys")
            need("values_summed", 1)
            say(V.tensor_copy(vt, ps[:, 1:3, :]), "values")
            att.vector(dve, nc, sig, link, say)
            att.out_of_psum(dve, nc, sig, link, mem.y[:, 4:8, :])

        @block.scalar
        def _(act):
            link, say, need = linker(act, sig, "act_ops")
            need("mean_squares", 1)
            say(nc.scalar.activation(rstd, rstd, ACT.Sqrt), "roots")
            need("queries_summed", 1)
            say(nc.scalar.copy(qf[0:W], tiles(0, HEADS)[0:W]), "queries_out")
            att.scalar(act, nc, sig, say)

        @block.tensor
        def _(pe):
            def need(name, n=1):
                pe.wait_ge(sig(name), n)

            need("squares", 1)
            for i in range(3):
                mm = pe.matmul(ps[:, i // 2, 0:T], mem.c("ones"), sq[:, i, :],
                               start=(i != 1), stop=(i != 0))
            mm.then_inc(sig("square_sums"), 1)
            need("latents", 3)
            for h in range(HEADS):
                for k in range(2):
                    mm = pe.matmul(tiles(0, HEADS)[0:W, h, :], w_uq[:, k, h * W:(h + 1) * W],
                                   c_all[:, k, :], start=(k == 0), stop=(k == 1))
            mm.then_inc(sig("queries_summed"), 1)
            need("queries_out", 1)
            for h in range(HEADS):
                mm = pe.matmul(tiles(4, HEADS)[0:W, h, :], mem.c("rotm")[0:W, 0:W], qf[0:W, h, :],
                               start=True, stop=True)
            mm.then_inc(sig("queries_swapped"), 1)
            pe.matmul(ps[HD:W, 0, 0:T], mem.c("rotm")[HD:W, HD:W], kr[:, 0, :], start=True,
                      stop=True).then_inc(sig("key_swapped"), 1)
            for n in range(NBLK):
                mm = pe.matmul(ps[:, 1 + n, :], c_all[:, 2, n * P:(n + 1) * P],
                               w_ukv.rearrange("p (h a d) -> p h a d", h=HEADS, a=2)[:, :, 1, :],
                               start=True, stop=True)
            mm.then_inc(sig("values_summed"), 1)
            need("roped", 1)
            for h in range(HEADS):
                mm = pe.matmul(tiles(4, HEADS)[0:HD, h, :], w_ukv[:, h * P:h * P + HD],
                               c_all[:, 2, :], start=True, stop=True)
            mm.then_inc(sig("keys_summed"), 1)
            need("keys", 2)
            need("values", 1)
            att.tensor(pe, sig)
    sig.end()



def delta_stage(nc, mem, sig):
    cut = Cutter(mem.scratch)
    z = [cut(MT_, T) for _ in range(7)]
    kq = cut(MT_, NBLK, 2, P)
    vt, kt, qh, kh, vnew, rhs = cut(NBLK, MIX), cut(MIX), cut(MT_, P), cut(MT_, P), cut(MIX), cut(MIX)
    state, cols, rows = cut(MT_, HD), cut(2, NBLK, HEADS), cut(4, T)
    ps, par = mem.ps, mem.par
    b0, b1 = slice(0, P), slice(P, T)
    x = mem.proj[:, X_DQ:X_DZ, :]
    q, k, v, dz = (mem.proj[:, i:i + 4, :] for i in (X_DQ, X_DK, X_DV, X_DZ))
    conv = mem.scratch[:, 0:12 * T].rearrange("p (a t) -> p a t", a=12)
    out = mem.y[:, 8:12, :]
    mt, t_, tt, xx, c, qk, dec = (
        zi.rearrange("p a t -> p (a t)").rearrange("p (h t) -> p h t", h=HEADS) for zi in z)
    solver = Solver(mem, mt, t_, tt, xx, c)
    beta, decay = mem.proj[0:HEADS, X_B, :], mem.proj[0:HEADS, X_A, :]
    size, gsum, egsum = (rows[0:HEADS, i, :] for i in range(3))
    ea = rows[0:HEADS, 3, 0:1]

    def flat(ap):
        return ap.rearrange("p a t -> p (a t)")

    def two(b):
        return ps[:, b:b + 2, :].rearrange("p a (b t) -> p (a b) t", t=T)

    def hp(s):
        return slice(HD * (s // 4), HD * (s // 4) + HD)

    def head(s):
        return 2 * (s % 4) + s // 4

    def par8(name):
        return par[0:HEADS, C2[name]:C2[name] + 1]

    with nc.Block() as block:
        @block.vector
        def _(dve):
            link, say, need = linker(dve, sig, "dve_ops")
            V = nc.vector
            link(V.tensor_scalar(decay, decay, par8("dt_bias"), None, ALU.add))
            say(V.scalar_tensor_tensor(out=size, in0=decay, scalar=-1.0, in1=decay,
                                       op0=ALU.mult, op1=ALU.max), "a_size")
            for i in range(12):
                tap = C2["dn_conv"] + i
                link(V.tensor_scalar(conv[:, i, :], x[:, i, :], par[:, tap + 36:tap + 37], None, ALU.mult))
                for lag in (1, 2, 3):
                    w = tap + 12 * (3 - lag)
                    ins = V.scalar_tensor_tensor(out=conv[:, i, lag:T], in0=x[:, i, 0:T - lag],
                                                 scalar=par[:, w:w + 1], in1=conv[:, i, lag:T],
                                                 op0=ALU.mult, op1=ALU.add)
                    if lag == 3:
                        say(ins, "convolved")
                    else:
                        link(ins)
            need("log_term", 1)
            link(V.scalar_tensor_tensor(out=size, in0=decay, scalar=0.0, in1=size, op0=ALU.max,
                                        op1=ALU.add))
            link(V.tensor_scalar(size, size, ea, -1.0, ALU.mult, ALU.mult))
            for n in range(NBLK):
                at = slice(n * P, (n + 1) * P)
                ins = V.tensor_tensor_scan(gsum[:, at], mem.c("ones", T)[0:HEADS, at], size[:, at], 0.0,
                                           ALU.mult, ALU.add)
                say(ins, "gate_sums")
            need("silu_gate", 1)
            link(V.tensor_tensor(x, x, conv, ALU.mult))
            for i in range(2):
                s = mem.scratch[:, i * 4 * T:(i + 1) * 4 * T]
                say(V.tensor_tensor(s, flat(x[:, 4 * i:4 * i + 4, :]), flat(x[:, 4 * i:4 * i + 4, :]),
                                    ALU.mult), "squares")
            for i in range(2):
                need("square_sums", i + 1)
                say(V.tensor_scalar(z[i], two(2 * i), EPS, None, ALU.add), "sums_out")
            for i in range(2):
                need("roots", i + 1)
                link(V.reciprocal(flat(z[i]), flat(z[i])))
                say(V.scalar_tensor_tensor(out=flat(x[:, 4 * i:4 * i + 4, :]),
                                           in0=flat(x[:, 4 * i:4 * i + 4, :]),
                                           scalar=HD ** -0.5 if i == 0 else 1.0,
                                           in1=flat(z[i]), op0=ALU.mult, op1=ALU.mult), "unit")
            need("columns_turned", 1)
            src = ps[:, 0, 0:4 * HEADS].rearrange("p (a n h) -> p a n h", a=2, n=NBLK)
            link(V.tensor_scalar(cols[:, 0, :, :], src[:, 0, :, :], -1.0, None, ALU.mult))
            say(V.tensor_copy(cols[:, 1, :, :], src[:, 1, :, :]), "columns")
            need("beta_spread", 1)
            kq5 = kq.rearrange("p a n w t -> p (a n) w t")
            k3 = flat(k).rearrange("p (a t) -> p a t", t=P)
            link(V.scalar_tensor_tensor(out=kq5[:, :, 0, :], in0=k3, scalar=-1.0,
                                        in1=ps[:, 4:6, :].rearrange("p a (b t) -> p (a b) t", t=P),
                                        op0=ALU.mult, op1=ALU.mult))
            link(V.tensor_copy(kq5[:, :, 1, :], flat(q).rearrange("p (a t) -> p a t", t=P)))
            spread = ps[:, 6, :].rearrange("p (a t) -> p a t", a=MT_)
            link(V.tensor_tensor(kh, kq[:, :, 1, 0, :], spread, ALU.mult))
            say(V.tensor_tensor(qh, q[:, :, b1], spread, ALU.mult), "operands")
            need("turned", 1)
            beta_t = cols[:, 1, :, :].rearrange("p n h -> p (n h)").unsqueeze(2)
            link(V.tensor_tensor(flat(vt).rearrange("p (h d) -> p h d", d=HD),
                                 ps[:, 1:3, :].rearrange("p a (h d) -> p (a h) d", d=HD),
                                 beta_t.to_broadcast([P, 16, HD]), ALU.mult))
            say(V.tensor_copy(kt, ps[:, 3, :]), "by_token")
            for n in range(NBLK):
                need("decay", 8 * (n + 1))
                for j in range(4):
                    need("pairs_summed", 4 * n + j + 1)
                    hs = slice(2 * j, 2 * j + 2)
                    src = ps[:, 4 + j, :].rearrange("p (h w t) -> p h w t", h=2, w=2)
                    link(V.tensor_tensor(mt[:, hs, :], src[:, :, 0, :], dec[:, hs, :], ALU.mult))
                    ins = V.tensor_tensor(qk[:, hs, :], src[:, :, 1, :], dec[:, hs, :], ALU.mult)
                    if j == 3:
                        say(ins, "masked")
                    else:
                        link(ins)
                if n == 0:
                    kt4 = kt.rearrange("p (a b d) -> p b a d", a=4, b=2)
                    for b in range(2):
                        ins = V.tensor_tensor(kt4[:, b, :, :], kt4[:, b, :, :],
                                              dec[:, 4 * b:4 * b + 4, P - 1:P].to_broadcast([P, 4, HD]),
                                              ALU.mult)
                        say(ins, "keys_to_end")
                solver.vector(dve, nc, sig, n, link, say)
                vb = vt[:, n, :].rearrange("p (a b d) -> p b a d", a=4, b=2)
                r4 = rhs.rearrange("p (b a d) -> p b a d", b=2, a=4)
                for b in range(2):
                    if n == 0:
                        say(V.tensor_copy(r4[:, b, :, :], vb[:, b, :, :]), "rhs")
                    else:
                        need("seen_summed", 1)
                        src = ps[:, 6 + b, 0:T].rearrange("p (a d) -> p a d", a=4)
                        say(V.tensor_tensor(r4[:, b, :, :], vb[:, b, :, :], src, ALU.add), "rhs")
                need("new_summed", n + 1)
                say(V.tensor_copy(vnew, ps[:, 4, :]), "new")
                need("out_summed", n + 1)
                say(V.tensor_copy(out[:, :, n * P:n * P + P],
                                  ps[:, 0, :].rearrange("p (a t) -> p a t", a=MT_)), "out")
                if n == 0:
                    need("state_summed", 1)
                    say(V.tensor_copy(flat(state), ps[:, 1, 0:MT_ * HD]), "state")
            say(V.tensor_tensor(z[0], out, out, ALU.mult), "out_squares")
            need("out_square_sums", 1)
            say(V.tensor_scalar(z[0], two(2), 1.0 / HD, EPS, ALU.mult, ALU.add), "out_mean")
            need("out_root", 1)
            link(V.reciprocal(flat(z[0]), flat(z[0])))
            link(V.tensor_tensor(out, out, z[0], ALU.mult))
            link(V.tensor_tensor(flat(z[1]), flat(z[1]), flat(dz), ALU.mult))
            link(V.scalar_tensor_tensor(out=out.rearrange("p a t -> p (a t)"),
                                        in0=out.rearrange("p a t -> p (a t)"),
                                        scalar=par[:, C2["o_norm"]:C2["o_norm"] + 1],
                                        in1=flat(z[1]), op0=ALU.mult, op1=ALU.mult))

        @block.scalar
        def _(act):
            link, say, need = linker(act, sig, "act_ops")
            A = nc.scalar.activation
            link(A(ea, par8("a_log"), ACT.Exp))
            need("a_size", 1)
            link(A(size, size, ACT.Exp, scale=-1.0))
            say(A(size, size, ACT.Ln, bias=1.0), "log_term")
            say(A(beta, beta, ACT.Sigmoid), "beta")
            need("convolved", 12)
            link(nc.scalar.copy(x, conv))
            say(A(conv, conv, ACT.Sigmoid), "silu_gate")
            for i in range(2):
                need("sums_out", i + 1)
                say(A(flat(z[i]), flat(z[i]), ACT.Sqrt), "roots")
            need("gate_sums", NBLK)
            say(A(egsum, gsum, ACT.Exp), "gate_exp")
            for n in range(NBLK):
                if n:
                    need("masked", n)
                    need("keys_to_end", 2)
                for s in range(HEADS):
                    need("rows_spread", n * 2 + s // 4 + 1)
                    say(A(dec[:, s, :], ps[:, 2 + s // 4, (s % 4) * P:(s % 4 + 1) * P], ACT.Exp,
                          bias=cols[:, 0, n, head(s):head(s) + 1]), "decay")
                solver.scalar(act, nc, sig, n)
            need("out_summed", 2)
            link(A(flat(z[1]), flat(dz), ACT.Sigmoid))
            need("out_mean", 1)
            say(A(flat(z[0]), flat(z[0]), ACT.Sqrt), "out_root")

        @block.gpsimd
        def _(pool):
            for n in range(NBLK):
                solver.pool(pool, nc, sig, n)

        @block.tensor
        def _(pe):
            def need(name, n=1):
                pe.wait_ge(sig(name), n)

            def head_sums(b, src, name):
                for i in range(2):
                    mm = pe.matmul(ps[:, b + i, :], mem.c("bones"), src[:, 2 * i * T:2 * (i + 1) * T],
                                   start=True, stop=True)
                mm.then_inc(sig(name), 1)

            for i in range(2):
                need("squares", i + 1)
                head_sums(2 * i, mem.scratch[:, i * 4 * T:(i + 1) * 4 * T], "square_sums")
            hsel = mem.c("hsel", MT_ * P)
            need("beta", 1)
            for i in range(MT_):
                mm = pe.matmul(two(4)[:, i, :], hsel[0:HEADS, i * P:(i + 1) * P], beta,
                               start=True, stop=True)
            mm.then_inc(sig("beta_spread"), 1)
            need("gate_exp", 1)
            for i in range(MT_):
                pe.matmul(ps[:, 6, i * P:(i + 1) * P], hsel[0:HEADS, i * P:(i + 1) * P], egsum[:, b1],
                          start=True, stop=True)
            need("unit", 2)
            eye8 = mem.c("ident")[0:HEADS, 0:HEADS]
            for w, src in enumerate((gsum, beta)):
                for n in range(NBLK):
                    at = (w * NBLK + n) * HEADS
                    mm = pe.transpose(ps[:, 0, at:at + HEADS], src[:, n * P:(n + 1) * P], eye8)
            mm.then_inc(sig("columns_turned"), 1)
            for i in range(MT_):
                for n in range(NBLK):
                    pe.transpose(ps[:, 1 + n, i * P:(i + 1) * P], v[:, i, n * P:(n + 1) * P],
                                 mem.c("ident"))
                mm = pe.transpose(ps[:, 3, i * P:(i + 1) * P], k[:, i, b0], mem.c("ident"))
            mm.then_inc(sig("turned"), 1)
            need("operands", 1)
            need("by_token", 1)
            need("columns", 1)
            for n in range(NBLK):
                if n:
                    need("state", 1)
                for s in range(HEADS):
                    o = ps[:, 2 + s // 4, (s % 4) * P:(s % 4 + 1) * P]
                    h = head(s)
                    pe.matmul(o, mem.c("ident")[0:HEADS, h:h + 1].to_broadcast([HEADS, P]),
                              gsum[:, n * P:(n + 1) * P], start=True, stop=False)
                    mm = pe.matmul(o, mem.c("ident"), mem.c("cbiasT"), start=False, stop=True)
                    if s % 4 == 3:
                        mm.then_inc(sig("rows_spread"), 1)
                for s in range(HEADS):
                    mm = pe.matmul(ps[:, 4 + s // 2, (s % 2) * T:(s % 2 + 1) * T],
                                   k[hp(s), s % 4, n * P:(n + 1) * P],
                                   kq[hp(s), s % 4, n, :, :].rearrange("p w t -> p (w t)"),
                                   start=True, stop=True)
                    if s % 2:
                        mm.then_inc(sig("pairs_summed"), 1)
                need("masked", n + 1)
                solver.tensor(pe, sig, n)
                if n:
                    for s in range(HEADS):
                        mm = pe.matmul(ps[:, 6 + s // 4, (s % 4) * HD:(s % 4 + 1) * HD],
                                       kh[hp(s), s % 4, :], state[hp(s), s % 4, :],
                                       start=True, stop=True)
                    mm.then_inc(sig("seen_summed"), 1)
                need("rhs", 2 * (n + 1))
                need("t_ready", 2 * len(LEVELS) * (n + 1))
                for s in range(HEADS):
                    mm = pe.matmul(ps[:, 4, s * HD:(s + 1) * HD], tt[:, s, :],
                                   rhs[:, s * HD:(s + 1) * HD], start=True, stop=True)
                mm.then_inc(sig("new_summed"), 1)
                need("new", n + 1)
                for s in range(HEADS):
                    o = ps[hp(s), 0, (s % 4) * P:(s % 4 + 1) * P]
                    mm = pe.matmul(o, vnew[:, s * HD:(s + 1) * HD], qk[:, s, :], start=True,
                                   stop=(n == 0))
                    if n:
                        mm = pe.matmul(o, state[hp(s), s % 4, :], qh[hp(s), s % 4, :],
                                       start=False, stop=True)
                mm.then_inc(sig("out_summed"), 1)
                if n == 0:
                    need("keys_to_end", 2)
                    for s in range(HEADS):
                        h = head(s)
                        mm = pe.matmul(ps[hp(s), 1, (s % 4) * HD:(s % 4 + 1) * HD],
                                       kt[:, h * HD:(h + 1) * HD], vnew[:, s * HD:(s + 1) * HD],
                                       start=True, stop=True)
                    mm.then_inc(sig("state_summed"), 1)
            need("out_squares", 1)
            head_sums(2, flat(z[0]), "out_square_sums")
    sig.end()


def in_groups():
    groups = tile_groups([(i // 2, (i % 2) * P, P, 0, i) for i in range(C_WI)])
    return groups + [[(C_WI // 2, 0, 4, 0, C_WI)]]


def hybrid_blocks(nc, w1, w2, par1, par2, small1, small2, xt, const, pos, out):
    with ExitStack() as ctx:
        mem = Memory(nc, ctx)
        full = [ctx.enter_context(nc.semaphore("slot_full_%d" % i)) for i in range(RING)]
        sig = Signals(nc)

        def clear_ring():
            nc.all_engine_barrier(sems_to_clear=range(full[0].num, full[-1].num + 1))

        def row(ap, layer):
            return ap[bass.ds(layer, 1)].rearrange("a p n -> (a p) n")

        with nc.Block() as block:
            @block.sync
            def _(sp):
                sp.dma_start(mem.h[:], xt).then_inc(sig("loaded"), 16)
                sp.dma_start(mem.const[:], const).then_inc(sig("loaded"), 16)
                sp.wait_ge(sig("loaded"), 32)
        sig.end()

        with nc.Fori(0, DEPTH) as layer:
            stream = Stream(mem, w1, JOBS1, full)
            loads = [lambda sp: sp.dma_start(mem.par[:, 0:N_PAR1], row(par1, layer)),
                     lambda sp: sp.dma_start(mem.small_w[:, 0:2 * MIX], row(small1, layer))]
            project_stage(nc, mem, sig, stream, layer, in_groups(), 0, C1["mix_g"], loads)
            rwkv_stage(nc, mem, sig)
            hgrn_stage(nc, mem, sig)
            dsa_stage(nc, mem, sig)
            gates_stage(nc, mem, sig, stream, layer, GATES_AT1, None)
            merge_stage(nc, mem, sig, stream, layer, GATES_AT1 + GATE_JOBS)
            ffn_stage(nc, mem, sig, stream, layer, FFN_AT1, C1["ffn_g"],
                      (C1["conv_w"], C1["conv_b"]), 1.0)
            clear_ring()
        final_norm_stage(nc, mem, sig, C1["fin_g"])
        mla_angles_stage(nc, mem, sig, pos)
        with nc.Fori(0, DEPTH) as layer:
            stream = Stream(mem, w2, JOBS2, full)
            loads = [lambda sp: sp.dma_start(mem.par[:, 0:N_PAR2], row(par2, layer)),
                     lambda sp: sp.dma_start(mem.small_w[:], row(small2, layer))]
            ffn_stage(nc, mem, sig, stream, layer, 0, C2["ffn1_g"], None, 0.5, loads)
            project_stage(nc, mem, sig, stream, layer, in_groups_2(), len(FFN_JOBS), C2["mix_g"], [])
            fox_stage(nc, mem, sig)
            mla_stage(nc, mem, sig)
            delta_stage(nc, mem, sig)
            gates_stage(nc, mem, sig, stream, layer, GATES_AT2, C2["b_gate"])
            merge_stage(nc, mem, sig, stream, layer, GATES_AT2 + GATE_JOBS)
            ffn_stage(nc, mem, sig, stream, layer, FFN_AT2, C2["ffn2_g"], None, 0.5)
            clear_ring()
        final_norm_stage(nc, mem, sig, C2["fin_g"], store=out)
    return mem



def cols_of(v):
    v = np.asarray(v)
    return v.reshape(-1, P).T


def job_block(w, cols=None):
    w = w if cols is None else np.concatenate([w[:, a:b] for a, b in cols], axis=1)
    k, n = w.shape
    return w.reshape(k // P, P, n).transpose(1, 0, 2).reshape(P, -1)


def fill(dst, src):
    dst[:, :src.shape[1]] = src


def column_jobs(w, a, b):
    return [job_block(w, [(x, x + 2 * P)]) for x in range(a, b, 2 * P)]


def merge_jobs(branches, w_out):
    halves = [job_block(w, [(a, a + 512)]) for w in branches for a in (0, 512)]
    return halves + column_jobs(w_out, 0, D)


def ffn_jobs(up, down):
    pairs = [job_block(up, [(j, j + P), (D_FF + j, D_FF + j + P)]) for j in range(0, D_FF, P)]
    return pairs + [job_block(down[a:a + 2 * P]) for a in range(0, D_FF, 2 * P)]


def pack_block1(i):
    w1 = np.zeros((DEPTH, len(JOBS1), P, SLOT), np.float32)
    par = np.zeros((DEPTH, P, N_PAR1), np.float32)
    small = np.zeros((DEPTH, P, 2 * MIX), np.float32)
    c0, gate0 = 1792 + 2048, 1792 + 2048 + 1092
    for l in range(DEPTH):
        w = i["w_in"][l]
        jobs = column_jobs(w, 0, c0 + 512)
        k, v, qi, ki, wi = c0 + 512, c0 + 640, c0 + 768, c0 + 1024, c0 + 1088
        jobs += [job_block(w, [(k, k + 64)] * 2 + [(k + 64, k + 128)] * 2)]
        jobs += [job_block(w, [(qi, qi + 256)])]
        jobs += [job_block(w, [(ki, ki + 64)] * 2 + [(v, v + 128)])]
        jobs += [job_block(w, [(wi, wi + 4)])]
        jobs += column_jobs(w, gate0, gate0 + 3072)
        jobs += merge_jobs([i["w_branch"][l, n] for n in range(3)], i["w_o"][l])
        jobs += ffn_jobs(i["w_up"][l], i["w_down"][l])
        assert len(jobs) == len(JOBS1)
        for g, job in enumerate(jobs):
            fill(w1[l, g], job)
        table = {"mix_g": i["norm_mix_g"][l], "mu": i["a_mu"][l], "w0": i["a_w0"][l],
                 "a0": i["a_a0"][l], "k_k": i["a_k_k"][l], "k_a": i["a_k_a"][l],
                 "r_k": i["a_r_k"][l].reshape(-1), "gn_g": i["a_gn_g"][l], "gn_b": i["a_gn_b"][l],
                 "lb0": i["b_lb_logits"][0], "lb1": i["b_lb_logits"][1], "b_gn_g": i["b_gn_g"][l],
                 "ffn_g": i["norm_ffn_g"][l], "conv_w": i["conv_w"][l].reshape(-1),
                 "conv_b": i["conv_b"][l], "fin_g": i["norm_final_g"]}
        for name, v in table.items():
            fill(par[l, :, C1[name]:], cols_of(v))
        par[l, :, C1["layer"]] = float(l)
        small[l, 0:HD, 0:MIX] = i["a_w_up"][l]
        small[l, HD:P, 0:MIX] = i["a_a_up"][l]
        small[l, :, MIX:] = i["a_g_up"][l]
    return w1, par, small


def pack_block2(i):
    w2 = np.zeros((DEPTH, len(JOBS2), P, SLOT), np.float32)
    par = np.zeros((DEPTH, P, N_PAR2), np.float32)
    small = np.zeros((DEPTH, P, 2560), np.float32)
    for l in range(DEPTH):
        w = i["w_in_2"][l]
        jobs = ffn_jobs(i["ffn1_w_gu_2"][l], i["ffn1_w_down_2"][l])
        jobs += column_jobs(w, 0, 1536)
        jobs += [job_block(w, [(1544, 1800)]), job_block(w, [(1800, 1960)])]
        jobs += [job_block(w, [(1536, 1544), (4008, 4024)])]
        jobs += column_jobs(w, 1960, 4008)
        jobs += column_jobs(w, 4024, 7096)
        jobs += merge_jobs([i[n][l] for n in ("w_br_fox_2", "w_br_mla_2", "w_br_dn_2")],
                           i["w_out_2"][l])
        jobs += ffn_jobs(i["ffn2_w_gu_2"][l], i["ffn2_w_down_2"][l])
        assert len(jobs) == len(JOBS2)
        for g, job in enumerate(jobs):
            fill(w2[l, g], job)
        table = {"ffn1_g": i["ffn1_norm_2"][l], "mix_g": i["mix_norm_2"][l],
                 "ffn2_g": i["ffn2_norm_2"][l], "fin_g": i["final_norm_2"],
                 "b_gate": i["b_gate_2"][l], "q_norm": i["mla_q_norm_2"][l],
                 "kv_norm": i["mla_kv_norm_2"][l], "dn_conv": i["dn_conv_w_2"][l].reshape(-1)}
        for name, v in table.items():
            fill(par[l, :, C2[name]:], cols_of(v))
        par[l, 0:HD, C2["o_norm"]] = i["dn_o_norm_2"][l]
        par[l, HD:P, C2["o_norm"]] = i["dn_o_norm_2"][l]
        par[l, 0:HEADS, C2["fox_b"]] = i["fox_b_f_2"][l]
        par[l, 0:HEADS, C2["a_log"]] = i["dn_a_log_2"][l]
        par[l, 0:HEADS, C2["dt_bias"]] = i["dn_dt_bias_2"][l]
        fill(small[l], job_block(i["mla_w_uq_2"][l]))
        small[l, :, 1536:] = i["mla_w_ukv_2"][l]
    return w2, par, small


def kernel(**inputs):
    import concourse.bacc as bacc
    from concourse.bass_utils import run_bass_kernel_spmd as run

    i = {k: np.asarray(v) for k, v in inputs.items()}
    w1, par1, small1 = pack_block1(i)
    w2, par2, small2 = pack_block2(i)
    xt = np.ascontiguousarray(i["x"][0].T.reshape(KT, P, T).transpose(1, 0, 2))
    pos = np.ascontiguousarray(i["positions_2"].astype(np.int32))
    arrays = {"w1": w1, "w2": w2, "par1": par1, "par2": par2, "small1": small1, "small2": small2,
              "xt": xt, "const": const_array(), "pos": pos}
    nc = bacc.Bacc("TRN2", target_bir_lowering=False, num_devices=1)
    aps = [nc.dram_tensor(n, a.shape, mybir.dt.from_np(a.dtype), kind="ExternalInput").ap()
           for n, a in arrays.items()]
    out = nc.dram_tensor("out", (P, KT, T), F32, kind="ExternalOutput").ap()
    hybrid_blocks(nc, *aps, out)
    got = run(nc, [arrays], core_ids=[0]).results[0]["out"]
    return np.ascontiguousarray(got.transpose(1, 0, 2).reshape(D, T).T)[None]
```

```python
from contextlib import ExitStack

import numpy as np
import concourse.bass as bass
from concourse import mybir

F32 = mybir.dt.float32
I32 = mybir.dt.int32
ALU = mybir.AluOpType
ACT = mybir.ActivationFunctionType
AX_X = mybir.AxisListType.X

P = 128
T = 256
NBLK = T // P
D = 1024
KT = D // P
DEPTH = 2
D_FF = 2816
MIX = 512
MT_ = MIX // P
HEADS = 8
HD = 64
RING = 3
SLOT = 2048
HEAD_ORDER = (0, 4, 1, 5, 2, 6, 3, 7)
BANK_ORDER = (0, 2, 1, 3)
LEVELS = (1, 2, 4, 8, 16, 32, 64)
NEG = -1e30
TAKEN = -3e38
TOPK = min(256, T // 4)
EPS = 1e-6
GN_EPS = 64e-5
KAPPA = float(np.exp(-0.5))

W_SCALE = 256.0
X_SCALE = 8.0
H_SCALE = 4.0
F16 = mybir.dt.float16
PART_X = 1.0 / (W_SCALE * X_SCALE)
PART_H = 1.0 / (W_SCALE * H_SCALE)

A_R, A_K, A_V, A_WA, A_G = 0, 4, 8, 12, 13
B_Q, B_F, B_I, B_G = 14, 18, 22, 26
C_Q, C_K, C_QI, C_KI, C_V, C_WI = 30, 34, 36, 38, 39, 40
X_Q, X_K, X_V, X_F, X_CQ, X_CKV, X_KR, X_B, X_A, X_DQ, X_DK, X_DV, X_DZ = (
    0, 4, 8, 12, 13, 15, 16, 17, 18, 19, 23, 27, 31)
P_TILES = 41

PAR1 = [("mix_g", 8), ("mu", 14), ("w0", 4), ("a0", 4), ("k_k", 4), ("k_a", 4), ("r_k", 4),
        ("gn_g", 4), ("gn_b", 4), ("lb0", 4), ("lb1", 4), ("b_gn_g", 4), ("ffn_g", 8),
        ("conv_w", 132), ("conv_b", 44), ("layer", 1), ("fin_g", 8)]
PAR2 = [("ffn1_g", 8), ("mix_g", 8), ("ffn2_g", 8), ("fin_g", 8), ("b_gate", 24), ("q_norm", 2),
        ("kv_norm", 1), ("dn_conv", 48), ("o_norm", 1), ("fox_b", 1), ("a_log", 1), ("dt_bias", 1)]


def columns(table):
    at, out = 0, {}
    for name, n in table:
        out[name] = at
        at += n
    return out, at


C1, N_PAR1 = columns(PAR1)
C2, N_PAR2 = columns(PAR2)
N_PAR = max(N_PAR1, N_PAR2)

CONSTS = [("ident", P), ("ones", T), ("bones", P), ("rot", P), ("rotm", P), ("cbias", P),
          ("cbiasT", P), ("strict", P), ("incl", P), ("levels", len(LEVELS) * P),
          ("cos", T), ("sin", T), ("hsel", MT_ * P), ("invf", 1)]
CC, N_CONST = columns(CONSTS)

PAIR, BRANCH, ROWS = (8, 256), (4, 512), (2, 1024)
FFN_JOBS = [PAIR] * 22 + [ROWS] * 11
MERGE_JOBS = [BRANCH] * 6 + [PAIR] * 4
JOBS1 = [PAIR] * 20 + [(8, 4)] + [PAIR] * 12 + MERGE_JOBS + FFN_JOBS
JOBS2 = (FFN_JOBS + [(8, 24)] + [PAIR] * 13 + [(8, 160)] + [PAIR] * 2 + [PAIR] * 12
         + MERGE_JOBS + FFN_JOBS)
GATE_JOBS = 12
GATES_AT1 = 21
FFN_AT1 = len(JOBS1) - len(FFN_JOBS)
GATES_AT2 = len(FFN_JOBS) + 17
FFN_AT2 = len(JOBS2) - len(FFN_JOBS)


def const_array():
    c = np.zeros((P, N_CONST), np.float32)
    i = np.arange(P)
    c[:, CC["ident"]:][:, :P] = np.eye(P)
    c[:, CC["ones"]:][:, :T] = 1.0
    c[:, CC["bones"]:][:, :P] = (i[:, None] // HD == i[None, :] // HD)
    rot = np.zeros((P, P))
    rotm = np.zeros((P, P))
    for m in range(P):
        if m % HD < HD // 2:
            rot[m + HD // 2, m] = -1.0
        else:
            rot[m - HD // 2, m] = 1.0
    for m in range(16):
        rotm[HD + 16 + m, HD + m] = -1.0
        rotm[HD + m, HD + 16 + m] = 1.0
    c[:, CC["rot"]:][:, :P] = rot
    c[:, CC["rotm"]:][:, :P] = rotm
    c[:, CC["cbias"]:][:, :P] = np.where(i[None, :] > i[:, None], NEG, 0.0)
    c[:, CC["cbiasT"]:][:, :P] = np.where(i[:, None] > i[None, :], NEG, 0.0)
    c[:, CC["strict"]:][:, :P] = i[:, None] < i[None, :]
    c[:, CC["incl"]:][:, :P] = i[:, None] <= i[None, :]
    for n, b in enumerate(LEVELS):
        s, t = i[:, None], i[None, :]
        m = (s // (2 * b) == t // (2 * b)) & (s % (2 * b) < b) & (t % (2 * b) >= b)
        c[:, CC["levels"] + n * P:][:, :P] = m
    freq = np.float32(10000.0) ** (-np.arange(HD // 2, dtype=np.float32) * np.float32(2.0 / HD))
    ang = np.arange(T, dtype=np.float32)[None, :] * freq[i % (HD // 2)][:, None]
    c[:, CC["cos"]:][:, :T] = np.cos(ang)
    c[:, CC["sin"]:][:, :T] = np.sin(ang)
    for n in range(MT_):
        for h in range(HEADS):
            c[h, CC["hsel"] + n * P:][:P] = (i // HD + 2 * n == h)
    invf = np.float32(10000.0) ** (-np.arange(16, dtype=np.float32) / np.float32(16))
    c[HD:HD + 32, CC["invf"]] = np.concatenate([invf, invf])
    return c


class Signals:

    def __init__(self, nc):
        self.nc, self.by_name, self.stack = nc, {}, ExitStack()

    def __call__(self, name):
        if name not in self.by_name:
            self.by_name[name] = self.stack.enter_context(self.nc.semaphore(name))
        return self.by_name[name]

    def end(self):
        nums = sorted(s.num for s in self.by_name.values())
        assert nums == list(range(nums[0], nums[-1] + 1)), nums
        self.nc.all_engine_barrier(sems_to_clear=range(nums[0], nums[-1] + 1))
        self.stack.close()


def linker(eng, sig, own):
    count = {}

    def say(ins, name):
        count[name] = count.get(name, 0) + 1
        ins.then_inc(sig(name), 1)
        eng.wait_ge(sig(name), count[name])

    def link(ins):
        say(ins, own)

    def need(name, n=1):
        eng.wait_ge(sig(name), n)

    return link, say, need


class Memory:

    def __init__(self, nc, ctx):
        def sb(name, shape, dt=F32):
            return ctx.enter_context(nc.sbuf_tensor(name, shape, dt))

        self.ring = sb("weight_ring", [P, RING, SLOT])
        self.w_high = sb("weights_high", [P, RING, SLOT], F16)
        self.w_low = sb("weights_low", [P, RING, SLOT], F16)
        self.proj = sb("projected", [P, P_TILES, T])
        self.scratch = sb("scratch", [P, 64 * 256])
        self.h = sb("residual", [P, KT, T])
        self.u_high = sb("normed_high", [P, KT, T], F16)
        self.u_low = sb("normed_low", [P, KT, T], F16)
        self.y = sb("branch_out", [P, 3 * MT_, T])
        self.par = sb("parameters", [P, N_PAR])
        self.small_w = sb("small_weights", [P, 2560])
        self.const = sb("constants", [P, N_CONST])
        self.mla_cos = sb("mla_cos", [P, T])
        self.mla_sin = sb("mla_sin", [P, T])
        self.ps = ctx.enter_context(nc.psum_tensor("banks", [P, 8, 512], F32))
        self.gates = self.scratch[:, 40 * 256:64 * 256].rearrange("p (a t) -> p a t", t=T)
        self.beside_gates = self.scratch[:, 0:40 * 256]

    def c(self, name, width=P):
        return self.const[:, CC[name]:CC[name] + width]


class Cutter:

    def __init__(self, buffer):
        self.buffer, self.at = buffer, 0

    def __call__(self, *shape):
        n = int(np.prod(shape))
        part = self.buffer[:, self.at:self.at + n]
        self.at += n
        assert self.at <= self.buffer.shape[1]
        if len(shape) == 1:
            return part
        names = "abcd"[:len(shape)]
        return part.rearrange("p (%s) -> p %s" % (" ".join(names), " ".join(names)),
                              **dict(zip(names, shape)))


class Stream:

    def __init__(self, mem, dram, jobs, full):
        self.mem, self.dram, self.jobs, self.full = mem, dram, jobs, full

    def load(self, sp, layer, g):
        nk, n = self.jobs[g]
        sp.dma_start(self.mem.ring[:, g % RING, 0:nk * n],
                     self.dram[bass.ds(layer, 1), g, :, 0:nk * n].rearrange("a p n -> (a p) n")
                     ).then_inc(self.full[g % RING], 16)

    def load_behind(self, sp, sig, layer, first, count):
        for n in range(count):
            if first + n + RING < len(self.jobs):
                sp.wait_ge(sig("lows"), n + 1)
                self.load(sp, layer, first + n + RING)

    def part(self, buffer, g):
        nk, n = self.jobs[g]
        return buffer[:, g % RING, 0:nk * n]

    def arrived(self, eng, g):
        eng.wait_ge(self.full[g % RING], 16 * (g // RING + 1))

    def high(self, act, nc, sig, g, used):
        self.arrived(act, g)
        if used:
            act.wait_ge(sig(used[0]), used[1])
        nc.scalar.activation(self.part(self.mem.w_high, g), self.part(self.mem.ring, g), ACT.Copy,
                             scale=W_SCALE).then_inc(sig("highs"), 1)

    def low(self, dve, nc, sig, g, n):
        dve.wait_ge(sig("highs"), n + 1)
        nc.vector.scalar_tensor_tensor(out=self.part(self.mem.w_low, g),
                                       in0=self.part(self.mem.ring, g), scalar=W_SCALE,
                                       in1=self.part(self.mem.w_high, g), op0=ALU.mult,
                                       op1=ALU.subtract).then_inc(sig("lows"), 1)

    def weight(self, g, k, c0, m):
        n = self.jobs[g][1]
        at = slice(k * n + c0, k * n + c0 + m)
        return self.mem.w_high[:, g % RING, at], self.mem.w_low[:, g % RING, at]


def product(pe, out, weight, high, low, start, stop, skip=False):
    w_high, w_low = weight
    pe.matmul(out, w_high, high, start=start, stop=False, skip_group_check=skip)
    pe.matmul(out, w_high, low, start=False, stop=False, skip_group_check=skip)
    return pe.matmul(out, w_low, high, start=False, stop=stop, skip_group_check=skip)


def split(nc, act, dve, sig, x, high, low, scale, name, n):
    if act is not None:
        nc.scalar.activation(high, x, ACT.Copy, scale=scale).then_inc(sig(name + "_high"), 1)
    else:
        dve.wait_ge(sig(name + "_high"), n)
        nc.vector.scalar_tensor_tensor(out=low, in0=x, scalar=scale, in1=high, op0=ALU.mult,
                                       op1=ALU.subtract).then_inc(sig(name + "_low"), 1)


def flat(ap):
    return ap.rearrange("p a t -> p (a t)")



class Norm:

    def __init__(self, mem, cut, gain):
        self.mem, self.gain = mem, gain
        self.sq, self.rstd, self.u = cut(KT, T), cut(T), cut(KT, T)

    def squares(self, nc, link, say, need):
        V, h, sq = nc.vector, self.mem.h, self.sq
        link(V.tensor_tensor(sq[:, 0:4, :], h[:, 0:4, :], h[:, 0:4, :], ALU.mult))
        need("upper_squares", 1)
        link(V.tensor_tensor(sq[:, 0:4, :], sq[:, 0:4, :], sq[:, 4:8, :], ALU.add))
        link(V.tensor_tensor(sq[:, 0:2, :], sq[:, 0:2, :], sq[:, 2:4, :], ALU.add))
        say(V.tensor_tensor(sq[:, 0, :], sq[:, 0, :], sq[:, 1, :], ALU.add), "squares")

    def upper_squares(self, nc, say):
        say(nc.scalar.activation(self.sq[:, 4:8, :], self.mem.h[:, 4:8, :], ACT.Square),
            "upper_squares")

    def sum(self, pe, sig):
        pe.wait_ge(sig("squares"), 1)
        pe.matmul(self.mem.ps[:, 7, 0:T], self.mem.c("ones"), self.sq[:, 0, :],
                  start=True, stop=True).then_inc(sig("square_sum"), 1)

    def mean(self, dve, nc, sig, say):
        dve.wait_ge(sig("square_sum"), 1)
        say(nc.vector.tensor_scalar(self.rstd, self.mem.ps[:, 7, 0:T], 1.0 / D, EPS,
                                    ALU.mult, ALU.add), "mean_square")

    def root(self, act, nc, sig, say):
        act.wait_ge(sig("mean_square"), 1)
        say(nc.scalar.activation(self.rstd, self.rstd, ACT.Sqrt), "root")

    def scale(self, dve, nc, sig, link, say, out=None):
        dve.wait_ge(sig("root"), 1)
        link(nc.vector.reciprocal(self.rstd, self.rstd))
        dst = self.u if out is None else out
        for k in range(KT):
            gain = self.mem.par[:, self.gain + k:self.gain + k + 1]
            say(nc.vector.scalar_tensor_tensor(out=dst[:, k, :], in0=self.mem.h[:, k, :],
                                               scalar=gain, in1=self.rstd, op0=ALU.mult,
                                               op1=ALU.mult), "normed")
            if out is None and k:
                self.pair(nc, sig, k - 1, dve=dve)
        if out is None:
            self.pair(nc, sig, KT - 1, dve=dve)

    def pair(self, nc, sig, k, act=None, dve=None):
        mem = self.mem
        split(nc, act, dve, sig, self.u[:, k, :], mem.u_high[:, k, :], mem.u_low[:, k, :],
              X_SCALE, "u", k + 1)

    def highs(self, act, nc, sig):
        for k in range(KT):
            act.wait_ge(sig("normed"), k + 1)
            self.pair(nc, sig, k, act=act)



def project_stage(nc, mem, sig, stream, layer, groups, first, gain, loads, beside):
    norm = Norm(mem, Cutter(mem.scratch), gain)
    BANKS = 2
    jobs = sorted({t[0] for grp in groups for t in grp})
    used = {g: 1 + max(i for i, grp in enumerate(groups) if any(t[0] == g for t in grp))
            for g in jobs}

    def after(g):
        return ("tiles_done", used[g - RING]) if g - RING >= first else None

    with nc.Block() as block:
        @block.sync
        def _(sp):
            if first == 0:
                for g in range(RING):
                    stream.load(sp, layer, g)
            for load in loads:
                load(sp).then_inc(sig("params"), 16)
            stream.load_behind(sp, sig, layer, first, len(jobs))

        @block.vector
        def _(dve):
            link, say, need = linker(dve, sig, "dve_ops")
            norm.squares(nc, link, say, need)
            norm.mean(dve, nc, sig, say)
            stream.low(dve, nc, sig, first, 0)
            if loads:
                need("params", 16 * len(loads))
            norm.scale(dve, nc, sig, link, say)
            stream.low(dve, nc, sig, first + 1, 1)
            need("u_low", KT)
            for n, g in enumerate(jobs[2:]):
                stream.low(dve, nc, sig, g, n + 2)
                for step in beside.vector.get(n + 2, ()):
                    step(link, say, need)
            for step in beside.vector["end"]:
                step(link, say, need)

        @block.scalar
        def _(act):
            link, say, need = linker(act, sig, "act_ops")
            split_jobs = iter(jobs)
            norm.upper_squares(nc, say)
            stream.high(act, nc, sig, next(split_jobs), None)
            norm.root(act, nc, sig, say)
            stream.high(act, nc, sig, next(split_jobs), None)
            norm.highs(act, nc, sig)
            stream.high(act, nc, sig, next(split_jobs), None)
            split_up_to = first + 2
            for i, grp in enumerate(groups):
                act.wait_ge(sig("tiles_done"), i + 1)
                for n, (g, c0, m, part, tile) in enumerate(grp):
                    ins = nc.scalar.activation(mem.proj[part:part + m, tile, :],
                                               mem.ps[part:part + m, i % BANKS, n * T:(n + 1) * T],
                                               ACT.Copy, scale=PART_X)
                ins.then_inc(sig("bank_free"), 1)
                while split_up_to < jobs[-1] and used[split_up_to + 1 - RING] <= i + 1:
                    split_up_to += 1
                    stream.high(act, nc, sig, split_up_to, after(split_up_to))
                for step in beside.scalar.get(i, ()):
                    step(link, say, need)
            for step in beside.scalar["end"]:
                step(link, say, need)

        @block.tensor
        def _(pe):
            def need(name, n=1):
                pe.wait_ge(sig(name), n)

            norm.sum(pe, sig)
            seen = 0
            for i, grp in enumerate(groups):
                if i >= BANKS:
                    pe.wait_ge(sig("bank_free"), i - BANKS + 1)
                for n, (g, c0, m, part, tile) in enumerate(grp):
                    if g - first + 1 > seen:
                        seen = g - first + 1
                        pe.wait_ge(sig("lows"), seen)
                    for k in range(KT):
                        if i == 0 and n == 0:
                            pe.wait_ge(sig("u_low"), k + 1)
                        mm = product(pe, mem.ps[part:part + m, i % BANKS, n * T:(n + 1) * T],
                                     stream.weight(g, k, c0, m), mem.u_high[:, k, :],
                                     mem.u_low[:, k, :], k == 0, k == KT - 1)
                mm.then_inc(sig("tiles_done"), 1)
                for step in beside.tensor.get(i, ()):
                    step(pe, need)
            for step in beside.tensor["end"]:
                step(pe, need)
    sig.end()


def tile_groups(spec):
    return [spec[i:i + 2] for i in range(0, len(spec), 2)]



class Gates:

    def __init__(self, mem, stream, layer, first, a, b, banks, plan, first_banks=()):
        self.mem, self.stream, self.layer = mem, stream, layer
        self.jobs = list(range(a, b))
        tiles, self.first = 2 * len(self.jobs), first
        self.banks = (first_banks + banks * tiles)[:tiles]
        assert sum(plan) == 2 * len(self.jobs)
        self.slots = [range(sum(plan[:k]), sum(plan[:k + 1])) for k in range(len(plan))]

    def bank(self, i):
        return self.mem.ps[:, self.banks[i], 0:T]

    def sync(self, sp, sig):
        self.stream.load_behind(sp, sig, self.layer, self.first + self.jobs[0], len(self.jobs))

    def high(self, act, nc, sig, n):
        st, g = self.stream, self.first + self.jobs[n]
        st.arrived(act, g)
        raw = st.part(self.mem.ring, g)
        nc.scalar.activation(raw, raw, ACT.Copy, scale=W_SCALE).then_inc(sig("scaled"), 1)
        act.wait_ge(sig("scaled"), n + 1)
        if n >= RING:
            act.wait_ge(sig("gate_done"), 2 * (n - RING + 1))
        nc.scalar.copy(st.part(self.mem.w_high, g), raw).then_inc(sig("highs"), 1)

    def lows(self, pool, nc, sig):
        for n, j in enumerate(self.jobs):
            st, g = self.stream, self.first + j
            pool.wait_ge(sig("highs"), n + 1)
            nc.gpsimd.tensor_tensor(st.part(self.mem.w_low, g), st.part(self.mem.ring, g),
                                    st.part(self.mem.w_high, g), ALU.subtract
                                    ).then_inc(sig("lows"), 1)

    def tensor(self, pe, sig, slot):
        mem = self.mem
        for i in self.slots[slot] if slot < len(self.slots) else ():
            n = i // 2
            if i % 2 == 0:
                pe.wait_ge(sig("lows"), n + 1)
            before = [t for t in range(i) if self.banks[t] == self.banks[i]]
            if before:
                pe.wait_ge(sig("gates_out"), before[-1] + 1)
            for k in range(KT):
                mm = product(pe, self.bank(i),
                             self.stream.weight(self.first + self.jobs[n], k, i % 2 * P, P),
                             mem.u_high[:, k, :], mem.u_low[:, k, :], k == 0, k == KT - 1)
            mm.then_inc(sig("gate_done"), 1)

    def out(self, act, nc, sig, i):
        act.wait_ge(sig("gate_done"), i + 1)
        nc.scalar.activation(self.mem.gates[:, 2 * self.jobs[0] + i, :], self.bank(i), ACT.Copy,
                             scale=PART_X).then_inc(sig("gates_out"), 1)

    def begin(self, act, nc, sig):
        for n in range(min(2, len(self.jobs))):
            self.high(act, nc, sig, n)

    def scalar(self, act, nc, sig, slot):
        for i in self.slots[slot] if slot < len(self.slots) else ():
            if i:
                self.out(act, nc, sig, i - 1)
            if i % 2 == 0 and i // 2 + 2 < len(self.jobs):
                self.high(act, nc, sig, i // 2 + 2)

    def end(self, act, nc, sig):
        self.out(act, nc, sig, 2 * len(self.jobs) - 1)



def merge_stage(nc, mem, sig, stream, layer, first, bias):
    y_pair = mem.proj[:, 0:3 * MT_, :].bitcast(F16)
    m_pair = mem.proj[:, 3 * MT_:3 * MT_ + KT, :].bitcast(F16)
    cut = Cutter(mem.beside_gates)
    merged, part = cut(KT, T), cut(2 * T)
    BR, WO = 12, 4
    jobs = list(range(first, first + 10))
    done = [2 * (n + 1) if n < 6 else BR + n - 5 for n in range(10)]

    def high(act, n):
        stream.high(act, nc, sig, jobs[n], ("tiles_done", done[n - RING]) if n >= RING else None)

    def open_gates(act, br):
        gates = mem.gates[:, KT * br:KT * (br + 1), :]
        if bias is None:
            ins = nc.scalar.activation(flat(gates), flat(gates), ACT.Sigmoid)
        else:
            for k in range(KT):
                at = bias + KT * br + k
                ins = nc.scalar.activation(gates[:, k, :], gates[:, k, :], ACT.Sigmoid,
                                           bias=mem.par[:, at:at + 1])
        ins.then_inc(sig("gates_open"), 1)

    def pair(buffer, k):
        return buffer[:, k, 0:T], buffer[:, k, T:2 * T]

    with nc.Block() as block:
        @block.sync
        def _(sp):
            stream.load_behind(sp, sig, layer, first, len(jobs))

        @block.scalar
        def _(act):
            high(act, 0)
            for br in range(3):
                split(nc, act, None, sig, mem.y[:, MT_ * br:MT_ * (br + 1), :],
                      y_pair[:, MT_ * br:MT_ * (br + 1), 0:T], None, X_SCALE, "y", br + 1)
            high(act, 1)
            open_gates(act, 0)
            high(act, 2)
            for n in range(3, 9):
                high(act, n)
                if n in (3, 5):
                    open_gates(act, n // 2)
            for j in range(4):
                act.wait_ge(sig("merged"), 9 + j)
                split(nc, act, None, sig, merged[:, 2 * j:2 * j + 2, :],
                      m_pair[:, 2 * j:2 * j + 2, 0:T], None, X_SCALE, "m", j + 1)
            high(act, 9)

        @block.vector
        def _(dve):
            link, say, need = linker(dve, sig, "dve_ops")

            def low(n):
                stream.low(dve, nc, sig, jobs[n], n)

            low(0)
            for br in range(3):
                split(nc, None, dve, sig, mem.y[:, MT_ * br:MT_ * (br + 1), :],
                      y_pair[:, MT_ * br:MT_ * (br + 1), 0:T],
                      y_pair[:, MT_ * br:MT_ * (br + 1), T:2 * T], X_SCALE, "y", br + 1)
            low(1)
            low(2)
            for i in range(BR):
                br, j = divmod(i, 4)
                need("tiles_done", i + 1)
                need("gates_open", br + 1)
                g = flat(mem.gates[:, KT * br + 2 * j:KT * br + 2 * j + 2, :])
                m = flat(merged[:, 2 * j:2 * j + 2, :])
                dst = m if br == 0 else part
                ins = nc.vector.scalar_tensor_tensor(out=dst, in0=mem.ps[:, i % 4, :], scalar=PART_X,
                                                     in1=g, op0=ALU.mult, op1=ALU.mult)
                if br == 0:
                    say(ins, "merged")
                else:
                    link(ins)
                    say(nc.vector.tensor_tensor(m, m, part, ALU.add), "merged")
                if i % 2 and i // 2 + 3 < 9:
                    low(i // 2 + 3)
                if br == 2:
                    split(nc, None, dve, sig, merged[:, 2 * j:2 * j + 2, :],
                          m_pair[:, 2 * j:2 * j + 2, 0:T], m_pair[:, 2 * j:2 * j + 2, T:2 * T],
                          X_SCALE, "m", j + 1)
            low(9)
            for j in range(WO):
                need("tiles_done", BR + j + 1)
                h = flat(mem.h[:, 2 * j:2 * j + 2, :])
                say(nc.vector.scalar_tensor_tensor(out=h, in0=mem.ps[:, j, :], scalar=PART_X,
                                                   in1=h, op0=ALU.mult, op1=ALU.add), "residual")

        @block.tensor
        def _(pe):
            for i in range(BR):
                br, j = divmod(i, 4)
                if i >= 4:
                    pe.wait_ge(sig("merged"), i - 3)
                if i % 2 == 0:
                    pe.wait_ge(sig("lows"), i // 2 + 1)
                if j == 0:
                    pe.wait_ge(sig("y_low"), br + 1)
                for n in range(2):
                    for k in range(MT_):
                        mm = product(pe, mem.ps[:, i % 4, n * T:(n + 1) * T],
                                     stream.weight(jobs[i // 2], k, (2 * (j % 2) + n) * P, P),
                                     *pair(y_pair, MT_ * br + k), k == 0, k == MT_ - 1)
                mm.then_inc(sig("tiles_done"), 1)
            for j in range(WO):
                pe.wait_ge(sig("merged"), 9 + j)
                pe.wait_ge(sig("lows"), 6 + j + 1)
                for n in range(2):
                    for k in range(KT):
                        if j == 0 and n == 0 and k % 2 == 0:
                            pe.wait_ge(sig("m_low"), k // 2 + 1)
                        mm = product(pe, mem.ps[:, j, n * T:(n + 1) * T],
                                     stream.weight(jobs[6 + j], k, n * P, P), *pair(m_pair, k),
                                     k == 0, k == KT - 1)
                mm.then_inc(sig("tiles_done"), 1)
    sig.end()



def ffn_stage(nc, mem, sig, stream, layer, first, gain, conv, factor, loads=()):
    cut = Cutter(mem.scratch)
    norm = Norm(mem, cut, gain)
    RB = 3
    c, sg, hid, taps = cut(RB, 2, T), cut(RB, T), cut(RB, T), cut(132)
    PAIRS = D_FF // P
    hidden = mem.proj[:, 0:PAIRS, :].bitcast(F16)
    DOWN = PAIRS // 2
    jobs = list(range(first, first + PAIRS + DOWN))

    def high(act, n):
        stream.high(act, nc, sig, jobs[n], ("tiles_done", n - RING + 1) if n >= RING else None)

    def low(dve, n):
        stream.low(dve, nc, sig, jobs[n], n)

    def half(j, n, a=0, b=T):
        return mem.ps[:, j % 4, n * T + a:n * T + b]

    with nc.Block() as block:
        @block.sync
        def _(sp):
            if first == 0:
                for g in range(RING):
                    stream.load(sp, layer, g)
            for load in loads:
                load(sp).then_inc(sig("params"), 16)
            stream.load_behind(sp, sig, layer, first, len(jobs))

        @block.scalar
        def _(act):
            link, say, need = linker(act, sig, "act_ops")
            norm.upper_squares(nc, say)
            high(act, 0)
            norm.root(act, nc, sig, say)
            high(act, 1)
            norm.highs(act, nc, sig)
            high(act, 2)
            for j in range(PAIRS):
                need("tiles_done", j + 1)
                if j >= RB:
                    need("hidden_low", j - RB + 1)
                if conv:
                    for n in range(2):
                        col = 2 * 44 + j + 22 * n
                        b = conv[1] + j + 22 * n
                        ins = nc.scalar.activation(c[:, j % RB, n, :], half(j, n), ACT.Identity,
                                                   bias=mem.par[:, b:b + 1],
                                                   scale=taps[:, col:col + 1])
                    ins.then_inc(sig("tap_now"), 1)
                    high(act, j + 3)
                    need("convolved", j + 1)
                    say(nc.scalar.activation(sg[:, j % RB, :], c[:, j % RB, 0, :], ACT.Sigmoid),
                        "gate_sigmoid")
                else:
                    say(nc.scalar.activation(sg[:, j % RB, :], half(j, 0), ACT.Sigmoid,
                                             scale=PART_X), "gate_sigmoid")
                    high(act, j + 3)
                need("hidden", j + 1)
                split(nc, act, None, sig, hid[:, j % RB, :], hidden[:, j, 0:T], None, H_SCALE,
                      "hidden", j + 1)
            for n in range(PAIRS + 3, len(jobs)):
                high(act, n)

        @block.vector
        def _(dve):
            link, say, need = linker(dve, sig, "dve_ops")
            norm.squares(nc, link, say, need)
            norm.mean(dve, nc, sig, say)
            low(dve, 0)
            if loads:
                need("params", 16 * len(loads))
            if conv:
                link(nc.vector.tensor_scalar(taps, mem.par[:, conv[0]:conv[0] + 132], PART_X, None,
                                             ALU.mult))
            norm.scale(dve, nc, sig, link, say)
            low(dve, 1)
            low(dve, 2)
            for j in range(PAIRS):
                if conv:
                    need("tap_now", j + 1)
                    for lag in (1, 2):
                        for n in range(2):
                            col = (2 - lag) * 44 + j + 22 * n
                            ins = nc.vector.scalar_tensor_tensor(
                                out=c[:, j % RB, n, lag:T], in0=half(j, n, 0, T - lag),
                                scalar=taps[:, col:col + 1], in1=c[:, j % RB, n, lag:T],
                                op0=ALU.mult, op1=ALU.add)
                            if (lag, n) == (2, 1):
                                say(ins, "convolved")
                            else:
                                link(ins)
                    low(dve, j + 3)
                    need("gate_sigmoid", j + 1)
                    s, gate, val = sg[:, j % RB, :], c[:, j % RB, 0, :], c[:, j % RB, 1, :]
                    link(nc.vector.tensor_tensor(s, gate, s, ALU.mult))
                    say(nc.vector.tensor_tensor(hid[:, j % RB, :], s, val, ALU.mult), "hidden")
                else:
                    need("gate_sigmoid", j + 1)
                    s = sg[:, j % RB, :]
                    link(nc.vector.scalar_tensor_tensor(out=s, in0=half(j, 0), scalar=PART_X, in1=s,
                                                        op0=ALU.mult, op1=ALU.mult))
                    say(nc.vector.scalar_tensor_tensor(out=hid[:, j % RB, :], in0=half(j, 1),
                                                       scalar=PART_X, in1=s, op0=ALU.mult,
                                                       op1=ALU.mult), "hidden")
                    low(dve, j + 3)
                split(nc, None, dve, sig, hid[:, j % RB, :], hidden[:, j, 0:T],
                      hidden[:, j, T:2 * T], H_SCALE, "hidden", j + 1)
            for n in range(PAIRS + 3, len(jobs)):
                low(dve, n)
            need("tiles_done", len(jobs))
            for b in range(4):
                h = flat(mem.h[:, 2 * b:2 * b + 2, :])
                say(nc.vector.scalar_tensor_tensor(out=h, in0=mem.ps[:, 4 + b, :],
                                                   scalar=factor * PART_H, in1=h, op0=ALU.mult,
                                                   op1=ALU.add), "residual")

        @block.tensor
        def _(pe):
            norm.sum(pe, sig)
            for j in range(PAIRS):
                if j >= 4:
                    pe.wait_ge(sig("convolved" if conv else "hidden"), j - 3)
                pe.wait_ge(sig("lows"), j + 1)
                for n in range(2):
                    for k in range(KT):
                        if j == 0 and n == 0:
                            pe.wait_ge(sig("u_low"), k + 1)
                        mm = product(pe, half(j, n), stream.weight(jobs[j], k, n * P, P),
                                     mem.u_high[:, k, :], mem.u_low[:, k, :], k == 0, k == KT - 1)
                mm.then_inc(sig("tiles_done"), 1)
            for i in range(DOWN):
                n = PAIRS + i
                pe.wait_ge(sig("lows"), n + 1)
                pe.wait_ge(sig("hidden_low"), 2 * (i + 1))
                for o in range(KT):
                    for k in range(2):
                        x = hidden[:, 2 * i + k, :]
                        mm = product(pe, mem.ps[:, 4 + o // 2, (o % 2) * T:(o % 2 + 1) * T],
                                     stream.weight(jobs[n], k, o * P, P), x[:, 0:T], x[:, T:2 * T],
                                     i == 0 and k == 0 and o % 2 == 0,
                                     i == DOWN - 1 and k == 1, skip=True)
                mm.then_inc(sig("tiles_done"), 1)
    sig.end()



def final_norm_stage(nc, mem, sig, gain, store=None):
    norm = Norm(mem, Cutter(mem.scratch), gain)
    with nc.Block() as block:
        @block.vector
        def _(dve):
            link, say, need = linker(dve, sig, "dve_ops")
            norm.squares(nc, link, say, need)
            norm.mean(dve, nc, sig, say)
            norm.scale(dve, nc, sig, link, say, out=mem.h)

        @block.scalar
        def _(act):
            link, say, need = linker(act, sig, "act_ops")
            norm.upper_squares(nc, say)
            norm.root(act, nc, sig, say)

        @block.tensor
        def _(pe):
            norm.sum(pe, sig)

        if store is not None:
            @block.sync
            def _(sp):
                sp.wait_ge(sig("normed"), KT)
                sp.dma_start(store, mem.h[:]).then_inc(sig("stored"), 16)
                sp.wait_ge(sig("stored"), 16)
    sig.end()



class Solver:
    def __init__(self, mem, mt, t, tt, x, c):
        self.mem, self.mt, self.t, self.tt, self.x, self.c = mem, mt, t, tt, x, c

    def pool(self, pool, nc, sig, n):
        mem, LV = self.mem, len(LEVELS)
        pool.wait_ge(sig("mt_ready"), n + 1)
        for lv in range(LV):
            c = self.x if lv == 0 else self.c
            if lv > 1:
                pool.wait_ge(sig("c_used"), n * LV + lv)
            mask = mem.c("levels", LV * P)[:, lv * P:(lv + 1) * P]
            for g in range(2):
                hs = slice(4 * g, 4 * g + 4)
                ins = nc.gpsimd.tensor_tensor(c[:, hs, :], self.mt[:, hs, :],
                                              mask.unsqueeze(1).to_broadcast([P, 4, P]), ALU.mult)
                ins.then_inc(sig("c_ready"), 1)

    def tensor(self, pe, sig, n):
        mem, LV = self.mem, len(LEVELS)
        pe.wait_ge(sig("c_ready"), 2 * (n * LV + 1))
        for h in range(HEADS):
            mm = pe.transpose(mem.ps[:, h // 4, (h % 4) * P:(h % 4 + 1) * P], self.x[:, h, :],
                              mem.c("ident"))
        mm.then_inc(sig("c_used"), 1)
        pe.wait_ge(sig("masked"), n + 1)
        for lv in range(1, LV):
            pe.wait_ge(sig("c_ready"), 2 * (n * LV + lv + 1))
            for g in range(2):
                pe.wait_ge(sig("t_ready"), 2 * (n * (LV) + lv - 1) + g + 1)
                for h in range(4 * g, 4 * g + 4):
                    mm = pe.matmul(mem.ps[:, g, (h % 4) * P:(h % 4 + 1) * P], self.c[:, h, :],
                                   self.t[:, h, :], start=True, stop=True)
                mm.then_inc(sig("x_summed" if g == 0 else "c_used"), 1)
            for g in range(2):
                pe.wait_ge(sig("x_ready"), 2 * (n * (LV - 1) + lv - 1) + g + 1)
                for h in range(4 * g, 4 * g + 4):
                    at = slice((h % 4) * P, (h % 4 + 1) * P)
                    mm = pe.matmul(mem.ps[:, 2 + g, at], self.x[:, h, :], self.tt[:, h, :],
                                   start=True, stop=True)
                    if lv < LV - 1:
                        mm = pe.matmul(mem.ps[:, 4 + g, at], self.tt[:, h, :], self.x[:, h, :],
                                       start=True, stop=True)
                mm.then_inc(sig("growth_summed"), 1)

    def scalar(self, act, nc, sig, n):
        mem, LV = self.mem, len(LEVELS)
        for lv in range(1, LV):
            for g in range(2):
                if g == 0:
                    act.wait_ge(sig("x_summed"), n * (LV - 1) + lv)
                else:
                    act.wait_ge(sig("c_used"), n * LV + lv + 1)
                nc.scalar.copy(self.x[:, 4 * g:4 * g + 4, :].rearrange("p h t -> p (h t)"),
                               mem.ps[:, g, :]).then_inc(sig("x_ready"), 1)

    def vector(self, dve, nc, sig, n, link, say):
        mem, LV = self.mem, len(LEVELS)
        eye = mem.c("ident").unsqueeze(1).to_broadcast([P, 4, P])

        def four(buffer, g):
            return buffer[:, 4 * g:4 * g + 4, :]

        def bank(b):
            return mem.ps[:, b, :].rearrange("p (h t) -> p h t", h=4)

        dve.wait_ge(sig("c_used"), n * LV + 1)
        for g in range(2):
            link(nc.vector.tensor_tensor(four(self.t, g), bank(g), eye, ALU.add))
            say(nc.vector.tensor_tensor(four(self.tt, g), four(self.x, g), eye, ALU.add), "t_ready")
        for lv in range(1, LV):
            for g in range(2):
                dve.wait_ge(sig("growth_summed"), 2 * (n * (LV - 1) + lv - 1) + g + 1)
                if lv < LV - 1:
                    link(nc.vector.tensor_tensor(four(self.t, g), four(self.t, g), bank(4 + g),
                                                 ALU.add))
                say(nc.vector.tensor_tensor(four(self.tt, g), four(self.tt, g), bank(2 + g),
                                            ALU.add), "t_ready")



class Rwkv:

    def __init__(self, nc, mem, sig):
        self.nc, self.mem, self.sig = nc, mem, sig
        cut = Cutter(mem.scratch)
        self.z = z = [cut(MT_, T) for _ in range(8)]
        self.ar = cut(MT_, 4, 2, HD)
        self.bt, self.kt, self.btp, self.ktp = (cut(MT_, T) for _ in range(4))
        self.rhs, self.sa, self.state, self.kh_t = cut(MIX), cut(MIX), cut(MT_, HD), cut(MIX)
        self.jump, self.one_ka, self.mids = cut(MT_, 2), cut(MT_), cut(MT_, 4)
        self.p_r, self.p_k, self.p_v = (mem.proj[:, i:i + 4, :] for i in (A_R, A_K, A_V))
        self.wa, self.gd = mem.proj[:, A_WA, :], mem.proj[:, A_G, :]
        self.bonus, self.gate, self.out = mem.y[:, 4:8, :], mem.y[:, 8:12, :], mem.y[:, 0:4, :]
        self.mixed = cut.buffer[:, 0:14 * T].rearrange("p (a t) -> p a t", a=14)
        self.vector = {9: [self.shift_low_rank], 10: [self.shift], 11: [self.keys_squared],
                       13: [self.decays_summed], 14: [self.decays_centred],
                       15: [self.keys_guarded, self.keys_mixed], 16: [self.bonus_products],
                       17: [self.keys_unit], 18: [self.bonus_values, self.operands_near],
                       19: [self.operands_far], 20: [self.operands_state], "end": []}
        self.scalar = {8: [self.low_rank_in], 10: [self.gates_of_a], 13: [self.exps],
                       14: [self.keys_root], "end": []}
        self.tensor = {9: [self.low_rank_up], 11: [self.keys_sum], 15: [self.bonus_sum], "end": []}

    def two(self, b):
        return self.mem.ps[:, b:b + 2, :].rearrange("p a (b t) -> p (a b) t", t=T)

    def col(self, name, i):
        return self.mem.par[:, C1[name] + i:C1[name] + i + 1]

    @staticmethod
    def q64(ap):
        return flat(ap).rearrange("p (q t) -> p q t", t=HD)


    def shift_low_rank(self, link, say, need):
        V, mixed, a_all = self.nc.vector, self.mixed, self.mem.proj[:, 0:14, :]
        need("bank_free", 7)
        link(V.tensor_tensor(mixed[:, :, 1:T], a_all[:, :, 0:T - 1], a_all[:, :, 1:T], ALU.subtract))
        link(V.tensor_scalar(mixed[:, :, 0:1], a_all[:, :, 0:1], -1.0, None, ALU.mult))
        self.shift(link, say, need, (12, 13))

    def shift(self, link, say, need, tiles=tuple(range(12))):
        for i in tiles:
            p = self.mem.proj[:, i, :]
            say(self.nc.vector.scalar_tensor_tensor(out=p, in0=self.mixed[:, i, :],
                                                    scalar=self.col("mu", i), in1=p,
                                                    op0=ALU.mult, op1=ALU.add), "shifted")

    def keys_squared(self, link, say, need):
        V, z = self.nc.vector, self.z
        for i in range(MT_):
            link(V.tensor_scalar(z[2][:, i, :], self.p_k[:, i, :], self.col("k_k", i), None, ALU.mult))
        say(V.tensor_tensor(flat(self.bt), flat(z[2]), flat(z[2]), ALU.mult), "kk_squares")

    def keys_guarded(self, link, say, need):
        need("kk_sum", 1)
        say(self.nc.vector.tensor_scalar(self.bt, self.two(2), 1e-24, None, ALU.max), "kk_guarded")

    def keys_unit(self, link, say, need):
        V, z = self.nc.vector, self.z
        need("kk_root", 1)
        link(V.reciprocal(flat(self.bt), flat(self.bt)))
        link(V.tensor_tensor(flat(z[2]), flat(z[2]), flat(self.bt), ALU.mult))
        link(V.tensor_tensor(flat(z[1]), flat(z[1]), flat(z[2]), ALU.mult))

    def decays_summed(self, link, say, need):
        V, z = self.nc.vector, self.z
        need("decay_sigmoid", 4)
        for i in range(MT_):
            link(V.tensor_tensor_scan(z[4][:, i, :], self.mem.c("ones", T), z[0][:, i, :], 0.0,
                                      ALU.mult, ALU.add))

    def decays_centred(self, link, say, need):
        V, z, mids, b1 = self.nc.vector, self.z, self.mids, slice(P, T)
        link(V.tensor_copy(mids[:], self.q64(z[4]).rearrange("p (a q) t -> p a q t", q=4)[:, :, :, 31]))
        mid = flat(mids).unsqueeze(2).to_broadcast([P, 16, HD])
        link(V.tensor_tensor(self.q64(z[5]), self.q64(z[4]), mid, ALU.subtract))
        say(V.tensor_tensor(flat(z[6]), flat(z[5]), flat(z[0]), ALU.subtract), "sums_centred")
        m2 = mids.rearrange("p a (b q) -> p a b q", q=2)
        say(V.tensor_tensor(self.jump[:], m2[:, :, :, 1], m2[:, :, :, 0], ALU.subtract), "jump_sums")
        link(V.tensor_tensor(z[3], z[4], z[4][:, :, P - 1:P].to_broadcast([P, MT_, T]), ALU.subtract))
        say(V.tensor_tensor(z[4][:, :, b1], z[3][:, :, b1], z[0][:, :, b1], ALU.subtract),
            "sums_from_half")

    def keys_mixed(self, link, say, need):
        V, z, one_ka = self.nc.vector, self.z, self.one_ka
        need("a_sigmoid", 4)
        k_a = self.mem.par[:, C1["k_a"]:C1["k_a"] + 4]
        link(V.tensor_scalar(one_ka, k_a, -1.0, 1.0, ALU.mult, ALU.add))
        for i in range(MT_):
            link(V.tensor_scalar(self.kt[:, i, :], z[1][:, i, :], k_a[:, i:i + 1], one_ka[:, i:i + 1],
                                 ALU.mult, ALU.add))
        link(V.tensor_tensor(flat(self.p_k), flat(self.p_k), flat(self.kt), ALU.mult))

    def bonus_products(self, link, say, need):
        V = self.nc.vector
        for i in range(MT_):
            say(V.scalar_tensor_tensor(out=self.kt[:, i, :], in0=self.p_r[:, i, :],
                                       scalar=self.col("r_k", i), in1=self.p_k[:, i, :],
                                       op0=ALU.mult, op1=ALU.mult), "rk")

    def bonus_values(self, link, say, need):
        need("bonus_sum", 1)
        say(self.nc.vector.tensor_tensor(self.bonus, self.two(4), self.p_v, ALU.mult), "bonus")

    def operands_near(self, link, say, need):
        V, z, ar, q64 = self.nc.vector, self.z, self.ar, self.q64
        need("exps", 7)
        link(V.scalar_tensor_tensor(out=ar.rearrange("p a q r t -> p (a q) r t")[:, :, 0, :],
                                    in0=q64(z[2]), scalar=-1.0, in1=q64(z[6]),
                                    op0=ALU.mult, op1=ALU.mult))
        link(V.tensor_tensor(ar.rearrange("p a q r t -> p (a q) r t")[:, :, 1, :],
                             q64(self.p_r), q64(z[7]), ALU.mult))
        link(V.tensor_tensor(flat(self.bt), flat(z[1]), flat(z[5]), ALU.mult))
        link(V.tensor_tensor(flat(self.kt), flat(self.p_k), flat(z[5]), ALU.mult))

    def operands_far(self, link, say, need):
        V = self.nc.vector
        for near, far in ((self.bt, self.btp), (self.kt, self.ktp)):
            n4, f4 = (v.rearrange("p a (b q t) -> p (a b) q t", b=2, q=2) for v in (near, far))
            link(V.tensor_copy(f4[:, :, 1, :], n4[:, :, 1, :]))
            link(V.tensor_tensor(f4[:, :, 0, :], n4[:, :, 0, :],
                                 flat(self.jump).unsqueeze(2).to_broadcast([P, 8, HD]), ALU.mult))

    def operands_state(self, link, say, need):
        V, z, p_r, p_k = self.nc.vector, self.z, self.p_r, self.p_k
        b0, b1 = slice(0, P), slice(P, T)
        link(V.tensor_tensor(p_r[:, :, b0], z[1][:, :, b0], z[3][:, :, b0], ALU.mult))
        link(V.tensor_tensor(p_r[:, :, b1], p_r[:, :, b1], z[3][:, :, b1], ALU.mult))
        link(V.tensor_tensor(p_k[:, :, b0], p_k[:, :, b0], z[3][:, :, b0], ALU.mult))
        link(V.scalar_tensor_tensor(out=p_k[:, :, b1], in0=z[2][:, :, b1], scalar=-1.0,
                                    in1=z[4][:, :, b1], op0=ALU.mult, op1=ALU.mult))


    def low_rank_in(self, link, say, need):
        need("shifted", 2)
        A, wa, gd = self.nc.scalar.activation, self.wa, self.gd
        link(A(wa[0:HD, :], wa[0:HD, :], ACT.Tanh))
        say(A(gd, gd, ACT.Sigmoid), "low_rank_ready")

    def gates_of_a(self, link, say, need):
        need("shifted", 14)
        need("up_summed", 3)
        A = self.nc.scalar.activation
        for i in range(MT_):
            say(A(self.z[0][:, i, :], self.two(2)[:, i, :], ACT.Sigmoid, bias=self.col("w0", i)),
                "decay_sigmoid")
        for i in range(MT_):
            say(A(self.z[1][:, i, :], self.two(4)[:, i, :], ACT.Sigmoid, bias=self.col("a0", i)),
                "a_sigmoid")
        link(self.nc.scalar.copy(self.gate, self.two(6)))

    def keys_root(self, link, say, need):
        need("kk_guarded", 1)
        say(self.nc.scalar.activation(flat(self.bt), flat(self.bt), ACT.Sqrt), "kk_root")

    def exps(self, link, say, need):
        A, z, b0, b1 = self.nc.scalar.activation, self.z, slice(0, P), slice(P, T)
        need("sums_centred", 1)
        say(A(flat(z[6]), flat(z[6]), ACT.Exp, scale=-KAPPA), "exps")
        say(A(flat(z[7]), flat(z[5]), ACT.Exp, scale=-KAPPA), "exps")
        say(A(flat(z[5]), flat(z[5]), ACT.Exp, scale=KAPPA), "exps")
        need("jump_sums", 1)
        say(A(self.jump[:], self.jump[:], ACT.Exp, scale=-KAPPA), "exps")
        need("sums_from_half", 1)
        say(A(z[4][:, :, b1], z[4][:, :, b1], ACT.Exp, scale=-KAPPA), "exps")
        say(A(z[3][:, :, b1], z[3][:, :, b1], ACT.Exp, scale=-KAPPA), "exps")
        say(A(z[3][:, :, b0], z[3][:, :, b0], ACT.Exp, scale=KAPPA), "exps")


    def low_rank_up(self, pe, need):
        w_up_a_up = self.mem.small_w[:, 0:MIX]
        g_up = self.mem.small_w[:, MIX:2 * MIX]
        need("low_rank_ready", 1)
        for rows, weight, src, b in ((slice(0, HD), w_up_a_up, self.wa, 2),
                                     (slice(HD, P), w_up_a_up, self.wa, 4),
                                     (slice(0, P), g_up, self.gd, 6)):
            for i in range(MT_):
                mm = pe.matmul(self.two(b)[:, i, :], weight[rows, i * P:(i + 1) * P], src[rows, :],
                               start=True, stop=True)
            mm.then_inc(self.sig("up_summed"), 1)

    def head_sums(self, pe, b, src, name):
        for i in range(2):
            mm = pe.matmul(self.mem.ps[:, b + i, :], self.mem.c("bones"),
                           flat(src[:, 2 * i:2 * i + 2, :]), start=True, stop=True)
        mm.then_inc(self.sig(name), 1)

    def keys_sum(self, pe, need):
        need("decay_sigmoid", 4)
        need("kk_squares", 1)
        self.head_sums(pe, 2, self.bt, "kk_sum")

    def bonus_sum(self, pe, need):
        need("a_sigmoid", 4)
        need("rk", 4)
        self.head_sums(pe, 4, self.kt, "bonus_sum")


def rwkv_stage(nc, mem, sig, rwkv, gates):
    z, ar, bt, kt, btp, ktp = rwkv.z, rwkv.ar, rwkv.bt, rwkv.kt, rwkv.btp, rwkv.ktp
    rhs, sa, state, kh_t = rwkv.rhs, rwkv.sa, rwkv.state, rwkv.kh_t
    p_r, p_k, p_v = rwkv.p_r, rwkv.p_k, rwkv.p_v
    bonus, gate, out = rwkv.bonus, rwkv.gate, rwkv.out
    ps, two, col, head_sums = mem.ps, rwkv.two, rwkv.col, rwkv.head_sums
    b0, b1 = slice(0, P), slice(P, T)
    bh_t = mem.proj[:, A_WA:A_WA + 2, :].rearrange("p a t -> p (a t)")
    mt, t_, tt, x, c, qb, ak, qk = (
        zi.rearrange("p a t -> p (a t)").rearrange("p (h t) -> p h t", h=HEADS) for zi in z)
    solver = Solver(mem, mt, t_, tt, x, c)

    def hp(s):
        return slice(HD * (s // 4), HD * (s // 4) + HD)

    with nc.Block() as block:
        @block.sync
        def _(sp):
            gates.sync(sp, sig)

        @block.vector
        def _(dve):
            link, say, need = linker(dve, sig, "dve_ops")
            V = nc.vector
            need("turned", 1)
            say(V.tensor_copy(p_v, two(4)), "by_token")
            say(V.tensor_copy(bh_t, ps[:, 6, :]), "by_token")
            say(V.tensor_copy(kh_t, ps[:, 7, :]), "by_token")
            for n in range(NBLK):
                for kind, (seen_a, seen_r) in enumerate(((mt, qb), (ak, qk))):
                    for i, j in enumerate(BANK_ORDER):
                        need("pairs_summed", n * 8 + kind * 4 + i + 1)
                        src = ps[:, 4 * kind + j, :].rearrange("p (h q r t) -> p h q r t", h=2, q=2, r=2)
                        for r, (dst, mask) in enumerate(((seen_a, "strict"), (seen_r, "incl"))):
                            m = mem.c(mask).rearrange("p (q t) -> p q t", q=2).unsqueeze(1)
                            ins = V.tensor_tensor(
                                dst[:, 2 * j:2 * j + 2, :].rearrange("p h (q t) -> p h q t", q=2),
                                src[:, :, :, r, :], m.to_broadcast([P, 2, 2, HD]), ALU.mult)
                            if (kind, j, r) == (1, 3, 1):
                                say(ins, "masked")
                            elif (kind, j, r) == (0, 3, 0):
                                say(ins, "mt_ready")
                            else:
                                link(ins)
                solver.vector(dve, nc, sig, n, link, say)
                need("rhs_summed", n + 1)
                say(V.tensor_copy(rhs.rearrange("p (b a) -> p b a", b=2), ps[:, 6:8, 0:T]), "rhs")
                need("sa_summed", n + 1)
                say(V.tensor_copy(sa, ps[:, 4, :]), "sa")
                need("y_summed", n + 1)
                say(V.tensor_copy(out[:, :, n * P:n * P + P],
                                  ps[:, 0, :].rearrange("p (a t) -> p a t", a=MT_)), "y_out")
                if n == 0:
                    need("state_summed", 1)
                    say(V.tensor_copy(flat(state), ps[:, 1, 0:MT_ * HD]), "state")
            need("mean_sum", 1)
            link(V.scalar_tensor_tensor(out=z[0], in0=two(2), scalar=-1.0 / HD, in1=out,
                                        op0=ALU.mult, op1=ALU.add))
            say(V.tensor_tensor(flat(z[1]), flat(z[0]), flat(z[0]), ALU.mult), "deviations")
            need("var_sum", 1)
            say(V.tensor_scalar(z[1], two(4), 1.0 / HD, GN_EPS, ALU.mult, ALU.add), "variance")
            need("std", 1)
            link(V.reciprocal(flat(z[1]), flat(z[1])))
            link(V.tensor_tensor(flat(z[0]), flat(z[0]), flat(z[1]), ALU.mult))
            for i in range(MT_):
                link(V.tensor_scalar(z[0][:, i, :], z[0][:, i, :], col("gn_g", i), col("gn_b", i),
                                     ALU.mult, ALU.add))
            link(V.tensor_tensor(z[0], z[0], bonus, ALU.add))
            link(V.tensor_tensor(out, z[0], gate, ALU.mult))

        @block.scalar
        def _(act):
            link, say, need = linker(act, sig, "act_ops")
            A = nc.scalar.activation
            gates.begin(act, nc, sig)
            for n in range(NBLK):
                solver.scalar(act, nc, sig, n)
            gates.scalar(act, nc, sig, 0)
            gates.scalar(act, nc, sig, 1)
            need("variance", 1)
            say(A(flat(z[1]), flat(z[1]), ACT.Sqrt), "std")
            gates.scalar(act, nc, sig, 2)
            gates.end(act, nc, sig)

        @block.gpsimd
        def _(pool):
            for n in range(NBLK):
                solver.pool(pool, nc, sig, n)
            gates.lows(pool, nc, sig)

        @block.tensor
        def _(pe):
            def need(name, n=1):
                pe.wait_ge(sig(name), n)

            for i in range(MT_):
                for n in range(NBLK):
                    pe.transpose(ps[:, 4 + n, i * P:(i + 1) * P], p_v[:, i, n * P:(n + 1) * P],
                                 mem.c("ident"))
                pe.transpose(ps[:, 6, i * P:(i + 1) * P], p_r[:, i, b0], mem.c("ident"))
                mm = pe.transpose(ps[:, 7, i * P:(i + 1) * P], p_k[:, i, b0], mem.c("ident"))
            mm.then_inc(sig("turned"), 1)
            need("by_token", 3)

            def of_head(by_token, s, n=0):
                at = n * MIX + (2 * (s % 4) + s // 4) * HD
                return by_token[:, at:at + HD]

            def v_t(n, s):
                return of_head(flat(p_v), s, n)

            for n in range(NBLK):
                if n:
                    need("state", 1)
                for kind, (near, far) in enumerate(((bt, btp), (kt, ktp))):
                    for h in HEAD_ORDER:
                        o = ps[:, 4 * kind + h // 2, (h % 2) * T:(h % 2 + 1) * T]
                        for q, left in enumerate((near, far)):
                            mm = pe.matmul(o[:, q * P:(q + 1) * P],
                                           left[hp(h), h % 4, n * P:(n + 1) * P],
                                           ar[hp(h), h % 4, 2 * n + q, :, :].rearrange("p r t -> p (r t)"),
                                           start=True, stop=True)
                        if h % 2:
                            mm.then_inc(sig("pairs_summed"), 1)
                solver.tensor(pe, sig, n)
                for h in range(HEADS):
                    o = ps[:, 6 + h // 4, (h % 4) * HD:(h % 4 + 1) * HD]
                    mm = pe.matmul(o, ak[:, h, :], v_t(n, h), start=True, stop=(n == 0))
                    if n:
                        mm = pe.matmul(o, p_k[hp(h), h % 4, b1], state[hp(h), h % 4, :],
                                       start=False, stop=True)
                mm.then_inc(sig("rhs_summed"), 1)
                need("rhs", n + 1)
                need("t_ready", 2 * len(LEVELS) * (n + 1))
                for h in range(HEADS):
                    mm = pe.matmul(ps[:, 4, h * HD:(h + 1) * HD], tt[:, h, :],
                                   rhs[:, h * HD:(h + 1) * HD], start=True, stop=True)
                mm.then_inc(sig("sa_summed"), 1)
                need("sa", n + 1)
                for h in range(HEADS):
                    o = ps[hp(h), 0, (h % 4) * P:(h % 4 + 1) * P]
                    pe.matmul(o, sa[:, h * HD:(h + 1) * HD], qb[:, h, :], start=True, stop=False)
                    mm = pe.matmul(o, v_t(n, h), qk[:, h, :], start=False, stop=(n == 0))
                    if n:
                        mm = pe.matmul(o, state[hp(h), h % 4, :], p_r[hp(h), h % 4, b1],
                                       start=False, stop=True)
                mm.then_inc(sig("y_summed"), 1)
                if n == 0:
                    for h in range(HEADS):
                        o = ps[hp(h), 1, (h % 4) * HD:(h % 4 + 1) * HD]
                        pe.matmul(o, of_head(bh_t, h), sa[:, h * HD:(h + 1) * HD],
                                  start=True, stop=False)
                        mm = pe.matmul(o, of_head(kh_t, h), v_t(n, h),
                                       start=False, stop=True)
                    mm.then_inc(sig("state_summed"), 1)
            gates.tensor(pe, sig, 0)
            need("y_out", 2)
            head_sums(pe, 2, out, "mean_sum")
            gates.tensor(pe, sig, 1)
            need("deviations", 1)
            head_sums(pe, 4, z[1], "var_sum")
            gates.tensor(pe, sig, 2)
    sig.end()



def hgrn_stage(nc, mem, sig, gates):
    NH = MIX // P
    cut = Cutter(mem.beside_gates)
    key, cs, acc, vt = (cut(NH, T) for _ in range(4))
    diff = [cut(NH, T) for _ in range(2)]
    fac = [cut(NH, T) for _ in range(2)]
    far = cut(NH, P)
    t1, t2 = mem.proj[:, 0:NH, :], mem.proj[:, NH:2 * NH, :]
    lb, lb_inv, lbt = cut(NH), cut(NH), cut(3, NH)
    ps, par = mem.ps, mem.par
    q, f, v, g = (mem.proj[:, i:i + 4, :] for i in (B_Q, B_F, B_I, B_G))
    out = mem.y[:, 4:8, :]
    ALL = (P,) + tuple(reversed(LEVELS))
    accs = acc.rearrange("p h t -> p (h t)").rearrange("p (g t) -> p g t", t=P)

    def flat(ap):
        return ap.rearrange("p a t -> p (a t)")

    def halves(ap, b):
        return flat(ap).rearrange("p (m h b) -> p m h b", h=2, b=b)

    def cols(name):
        return par[:, C1[name]:C1[name] + NH]

    def two(b):
        return ps[:, b:b + 2, :].rearrange("p a (b t) -> p (a b) t", t=T)

    with nc.Block() as block:
        @block.vector
        def _(dve):
            link, say, need = linker(dve, sig, "dve_ops")
            V = nc.vector
            link(V.tensor_tensor(lbt[:, 0, :], cols("lb0"), cols("lb1"), ALU.max))
            link(V.tensor_tensor(lbt[:, 1, :], cols("lb0"), lbt[:, 0, :], ALU.subtract))
            say(V.tensor_tensor(lbt[:, 2, :], cols("lb1"), lbt[:, 0, :], ALU.subtract), "lb_logits")
            link(V.scalar_tensor_tensor(out=flat(t1), in0=flat(f), scalar=-1.0, in1=flat(f),
                                        op0=ALU.mult, op1=ALU.max))
            say(V.tensor_scalar(flat(t2), flat(f), -40.0, None, ALU.max), "f_sizes")
            need("lb_exp", 1)
            link(V.tensor_tensor(lbt[:, 0, :], lbt[:, 1, :], lbt[:, 2, :], ALU.add))
            link(V.reciprocal(lbt[:, 0, :], lbt[:, 0, :]))
            link(V.scalar_tensor_tensor(out=lb, in0=lbt[:, 2, :],
                                        scalar=par[:, C1["layer"]:C1["layer"] + 1],
                                        in1=lbt[:, 0, :], op0=ALU.mult, op1=ALU.mult))
            say(V.tensor_scalar(lb_inv, lb, -1.0, 1.0, ALU.mult, ALU.add), "lower_bound")
            need("log_terms", 1 + NH)
            link(V.scalar_tensor_tensor(out=flat(t1), in0=flat(f), scalar=0.0, in1=flat(t1),
                                        op0=ALU.min, op1=ALU.subtract))
            link(V.tensor_tensor(flat(t1), flat(t1), flat(t2), ALU.add))
            for h in range(NH):
                link(V.tensor_tensor_scan(cs[:, h, :], mem.c("ones", T), t1[:, h, :], 0.0,
                                          ALU.mult, ALU.add))
            need("forget_inverse", 1)
            for h in range(NH):
                ins = V.tensor_scalar(key[:, h, :], key[:, h, :], lb_inv[:, h:h + 1], None, ALU.mult)
                say(ins, "keys")
            say(V.memset(flat(acc), 0.0), "cleared")
            need("values_turned", 1)
            say(V.tensor_copy(vt, two(0)), "values_by_token")

            def exponents(n):
                b = ALL[n]
                d, c = halves(diff[n % 2], b), halves(cs, b)
                r = c[:, :, 0, b - 1:b].to_broadcast([P, NH * T // (2 * b), b])
                link(V.tensor_tensor(d[:, :, 0, :], r, c[:, :, 0, :], ALU.subtract))
                say(V.tensor_tensor(d[:, :, 1, :], c[:, :, 1, :], r, ALU.subtract), "exponents")

            def gather(n):
                need("scores_summed", n + 1)
                if n == 0:
                    say(V.tensor_copy(flat(far), ps[:, 4, :]), "gathered")
                else:
                    src = ps[:, 4 + 2 * (n % 2):6 + 2 * (n % 2), :].rearrange("p a (b t) -> p (a b) t", t=P)
                    if n <= len(LEVELS):
                        lv = len(LEVELS) - n
                        m = mem.c("levels", len(LEVELS) * P)[:, lv * P:(lv + 1) * P]
                    else:
                        m = mem.c("ident")
                    say(V.copy_predicated(accs, m.unsqueeze(1).to_broadcast([P, 8, P]).bitcast(I32),
                                          src), "gathered")

            exponents(0)
            for n in range(len(ALL)):
                if n + 1 < len(ALL):
                    exponents(n + 1)
                need("decays", n + 1)
                d, o, b = halves(diff[n % 2], ALL[n]), halves(fac[n % 2], ALL[n]), ALL[n]
                if n >= 2:
                    need("scores_summed", n - 1)
                link(V.tensor_tensor(o[:, :, 0, :], halves(key, b)[:, :, 0, :], d[:, :, 0, :], ALU.mult))
                say(V.tensor_tensor(o[:, :, 1, :], halves(q, b)[:, :, 1, :], d[:, :, 1, :], ALU.mult),
                    "factors")
                if n:
                    gather(n - 1)
            gather(len(ALL) - 1)
            gather(len(ALL))
            need("out_summed", 1)
            link(V.tensor_copy(t1, two(0)))
            say(V.tensor_tensor(flat(t2), flat(t1), flat(t1), ALU.mult), "out_squares")
            need("out_square_sum", 1)
            say(V.tensor_scalar(t2, two(4), 1.0 / P, EPS, ALU.mult, ALU.add), "out_mean_square")
            need("out_root", 1)
            link(V.reciprocal(flat(t2), flat(t2)))
            link(V.tensor_tensor(flat(t1), flat(t1), flat(t2), ALU.mult))
            need("gate_sigmoid", 1)
            link(V.tensor_tensor(flat(g), flat(g), flat(key), ALU.mult))
            for h in range(NH):
                link(V.scalar_tensor_tensor(out=out[:, h, :], in0=t1[:, h, :],
                                            scalar=par[:, C1["b_gn_g"] + h:C1["b_gn_g"] + h + 1],
                                            in1=g[:, h, :], op0=ALU.mult, op1=ALU.mult))

        @block.sync
        def _(sp):
            gates.sync(sp, sig)

        @block.gpsimd
        def _(pool):
            gates.lows(pool, nc, sig)

        @block.scalar
        def _(act):
            link, say, need = linker(act, sig, "act_ops")
            A = nc.scalar.activation
            gates.high(act, nc, sig, 0)
            need("lb_logits", 1)
            say(A(lbt[:, 1:3, :], lbt[:, 1:3, :], ACT.Exp), "lb_exp")
            need("f_sizes", 1)
            link(A(flat(t1), flat(t1), ACT.Exp, scale=-1.0))
            link(A(flat(t2), flat(t2), ACT.Exp, scale=-1.0))
            say(A(flat(t1), flat(t1), ACT.Ln, bias=1.0), "log_terms")
            need("lower_bound", 1)
            for h in range(NH):
                say(A(t2[:, h, :], t2[:, h, :], ACT.Ln, bias=1.0, scale=lb[:, h:h + 1]), "log_terms")
            say(A(flat(key), flat(f), ACT.Sigmoid, scale=-1.0), "forget_inverse")
            gates.high(act, nc, sig, 1)
            gates.scalar(act, nc, sig, 0)
            for n in range(len(ALL)):
                need("exponents", n + 1)
                say(A(flat(diff[n % 2]), flat(diff[n % 2]), ACT.Exp), "decays")
                gates.scalar(act, nc, sig, n + 1)
            gates.scalar(act, nc, sig, len(ALL) + 1)
            need("scores_summed", len(ALL) + 1)
            say(A(flat(key), flat(g), ACT.Sigmoid), "gate_sigmoid")
            gates.scalar(act, nc, sig, len(ALL) + 2)
            need("out_mean_square", 1)
            say(A(flat(t2), flat(t2), ACT.Sqrt), "out_root")
            gates.scalar(act, nc, sig, len(ALL) + 3)
            gates.end(act, nc, sig)

        @block.tensor
        def _(pe):
            def need(name, n=1):
                pe.wait_ge(sig(name), n)

            for n in range(NBLK):
                for h in range(NH):
                    mm = pe.transpose(ps[:, n, h * P:(h + 1) * P], v[:, h, n * P:(n + 1) * P],
                                      mem.c("ident"))
            mm.then_inc(sig("values_turned"), 1)
            gates.tensor(pe, sig, 0)
            for n in range(len(ALL) + 1):
                if n < len(ALL):
                    need("factors", n + 1)
                    left = right = fac[n % 2]
                else:
                    left, right = key, q
                if n >= 2:
                    need("gathered", n - 1)
                for h in range(NH):
                    if n == 0:
                        mm = pe.matmul(ps[:, 4, h * P:(h + 1) * P], left[:, h, 0:P], right[:, h, P:T],
                                       start=True, stop=True)
                        continue
                    for blk in range(NBLK):
                        i = 2 * h + blk
                        mm = pe.matmul(ps[:, 4 + 2 * (n % 2) + i // 4, (i % 4) * P:(i % 4 + 1) * P],
                                       left[:, h, blk * P:(blk + 1) * P],
                                       right[:, h, blk * P:(blk + 1) * P], start=True, stop=True)
                mm.then_inc(sig("scores_summed"), 1)
                gates.tensor(pe, sig, n + 1)
            need("gathered", len(ALL) + 1)
            need("values_by_token", 1)
            for h in range(NH):
                o = two(0)[:, h, :]
                v0, v1 = (flat(vt)[:, n * MIX + h * P:n * MIX + (h + 1) * P] for n in range(2))
                pe.matmul(o[:, 0:P], v0, accs[:, 2 * h, :], start=True, stop=True)
                pe.matmul(o[:, P:T], v0, far[:, h, :], start=True, stop=False)
                mm = pe.matmul(o[:, P:T], v1, accs[:, 2 * h + 1, :], start=False, stop=True)
            mm.then_inc(sig("out_summed"), 1)
            gates.tensor(pe, sig, len(ALL) + 2)
            need("out_squares", 1)
            for i in range(2):
                mm = pe.matmul(ps[:, 4 + i, :], mem.c("ones"), flat(t2[:, 2 * i:2 * i + 2, :]),
                               start=True, stop=True)
            mm.then_inc(sig("out_square_sum"), 1)
            gates.tensor(pe, sig, len(ALL) + 3)
    sig.end()



class Attention:

    def __init__(self, mem, cut, q, k, v, scale, bias, gates, first_slot=0):
        self.gates, self.first_slot = gates, first_slot
        self.mem, self.q, self.k, self.v, self.scale, self.bias = mem, q, k, v, scale, bias
        self.prob = [cut(T) for _ in range(3)]
        self.turned = [cut(T) for _ in range(3)]
        self.low, self.sums = cut(16), cut(16)
        self.units = [(h, n) for n in range(NBLK) for h in range(HEADS)]

    def vector(self, dve, nc, sig, link, say):
        V = nc.vector
        for i in range(len(self.units) + 1):
            if i < len(self.units):
                w = P * (self.units[i][1] + 1)
                dve.wait_ge(sig("scores"), i + 1)
                link(V.tensor_reduce(self.low[:, i:i + 1], self.mem.ps[:, i % 2, 0:w], AX_X, ALU.max))
                say(V.tensor_scalar(self.low[:, i:i + 1], self.low[:, i:i + 1], -self.scale, None,
                                    ALU.mult), "row_max")
            if i:
                j = i - 1
                w = P * (self.units[j][1] + 1)
                dve.wait_ge(sig("prob"), j + 1)
                link(V.reciprocal(self.sums[:, j:j + 1], self.sums[:, j:j + 1]))
                say(V.tensor_scalar(self.prob[j % 3][:, 0:w], self.prob[j % 3][:, 0:w],
                                    self.sums[:, j:j + 1], None, ALU.mult), "prob_scaled")

    def scalar(self, act, nc, sig, say):
        for i in range(len(self.units) + 2):
            if i < len(self.units):
                w = P * (self.units[i][1] + 1)
                act.wait_ge(sig("row_max"), i + 1)
                if i >= 3:
                    act.wait_ge(sig("prob_turned"), i - 2)
                say(nc.scalar.activation(self.prob[i % 3][:, 0:w], self.mem.ps[:, i % 2, 0:w], ACT.Exp,
                                         bias=self.low[:, i:i + 1], scale=self.scale,
                                         accum_out=self.sums[:, i:i + 1]), "prob")
            if i >= 2:
                j = i - 2
                w = P * (self.units[j][1] + 1)
                act.wait_ge(sig("prob_turned"), j + 1)
                if j >= 3:
                    act.wait_ge(sig("attended"), j - 2)
                say(nc.scalar.copy(self.turned[j % 3][:, 0:w], self.mem.ps[:, 3 + j % 2, 0:w]),
                    "turned_out")
            self.gates.scalar(act, nc, sig, self.first_slot + i)
        self.gates.end(act, nc, sig)

    def tensor(self, pe, sig):
        mem, n_units = self.mem, len(self.units)
        for i in range(n_units + 4):
            if i < n_units:
                h, n = self.units[i]
                w = P * (n + 1)
                if i >= 2:
                    pe.wait_ge(sig("prob"), i - 1)
                o = mem.ps[:, i % 2, 0:w]
                pe.matmul(o, self.q(h)[:, n * P:(n + 1) * P], self.k(h)[:, 0:w], start=True, stop=False)
                self.bias(pe, mem.ps[:, i % 2, :], h, n).then_inc(sig("scores"), 1)
            if 2 <= i < n_units + 2:
                j = i - 2
                n = self.units[j][1]
                pe.wait_ge(sig("prob_scaled"), j + 1)
                if j >= 2:
                    pe.wait_ge(sig("turned_out"), j - 1)
                elif j == 0 and self.first_slot > 1:
                    pe.wait_ge(sig("gates_out"), 2)
                for b in range(n + 1):
                    mm = pe.transpose(mem.ps[:, 3 + j % 2, b * P:(b + 1) * P],
                                      self.prob[j % 3][:, b * P:(b + 1) * P], mem.c("ident"))
                mm.then_inc(sig("prob_turned"), 1)
            if i >= 4:
                j = i - 4
                h, n = self.units[j]
                pe.wait_ge(sig("turned_out"), j + 1)
                rows = slice(HD * (h % 2), HD * (h % 2) + HD)
                o = mem.ps[rows, 5 + n, (h // 2) * P:(h // 2 + 1) * P]
                for b in range(n + 1):
                    mm = pe.matmul(o, self.v(h, b), self.turned[j % 3][:, b * P:(b + 1) * P],
                                   start=(b == 0), stop=(b == n))
                mm.then_inc(sig("attended"), 1)
            if i < n_units + 2:
                self.gates.tensor(pe, sig, self.first_slot + i)

    def out_of_psum(self, dve, nc, sig, link, out):
        for n in range(NBLK):
            dve.wait_ge(sig("attended"), HEADS * (n + 1))
            link(nc.vector.tensor_copy(out[:, :, n * P:(n + 1) * P],
                                       self.mem.ps[:, 5 + n, :].rearrange("p (a t) -> p a t", a=MT_)))


def rope(dve_v, link, say, x, turned, cos, sin, name):
    n = x.shape[1]
    r = x.shape[0]
    link(dve_v.tensor_tensor(turned, turned, sin.unsqueeze(1).to_broadcast([r, n, T]), ALU.mult))
    link(dve_v.tensor_tensor(x, x, cos.unsqueeze(1).to_broadcast([r, n, T]), ALU.mult))
    say(dve_v.tensor_tensor(x, x, turned, ALU.add), name)



def dsa_stage(nc, mem, sig, gates):
    cut = Cutter(mem.beside_gates)
    score = [cut(T) for _ in range(NBLK)]
    bias = [cut(T) for _ in range(NBLK)]
    part, wi, top, vt = cut(T), cut(NBLK, 4), cut(8), cut(NBLK, P)
    ps = mem.ps
    x = mem.proj[:, C_Q:C_KI + 1, :]
    qi, ki = mem.proj[:, C_QI:C_QI + 2, :], mem.proj[:, C_KI, :]
    NT = C_KI + 1 - C_Q

    def rows(h):
        return slice(HD * (h % 2), HD * (h % 2) + HD)

    def tiles(b, n):
        return ps[:, b:b + (n + 1) // 2, :].rearrange("p a (b t) -> p (a b) t", t=T)[:, 0:n, :]

    def add_bias(pe, o, h, n):
        w = P * (n + 1)
        return pe.matmul(o[:, 0:w], mem.c("ident"), bias[n][:, 0:w], start=False, stop=True)

    att = Attention(mem, cut,
                    q=lambda h: mem.proj[rows(h), C_Q + h // 2, :],
                    k=lambda h: mem.proj[rows(h), C_K + h // 4, :],
                    v=lambda h, b: vt[:, b, HD * (h // 4):HD * (h // 4) + HD],
                    scale=HD ** -0.5, bias=add_bias, gates=gates, first_slot=1)

    with nc.Block() as block:
        @block.vector
        def _(dve):
            link, say, need = linker(dve, sig, "dve_ops")
            V = nc.vector
            need("halves_swapped", 1)
            rope(V, link, say, x, tiles(0, NT), mem.c("cos", T), mem.c("sin", T), "roped")
            need("by_token", 1)
            say(V.tensor_copy(vt, ps[:, 5, 0:T].rearrange("p (n d) -> p n d", n=NBLK)), "values")
            say(V.tensor_scalar(wi, ps[:, 5, T:T + 8].rearrange("p (n j) -> p n j", n=NBLK),
                                4 ** -0.5 * HD ** -0.5, None, ALU.mult), "values")
            for n in range(NBLK):
                w = P * (n + 1)
                need("dots", n + 1)
                for j in range(4):
                    src = ps[:, 3 * n + j % 2, (j // 2) * T:(j // 2) * T + w]
                    dst = score[n] if j == 0 else part
                    link(V.tensor_scalar(dst[:, 0:w], src, 0.0, wi[:, n, j:j + 1], ALU.max, ALU.mult))
                    if j:
                        link(V.tensor_tensor(score[n][:, 0:w], score[n][:, 0:w], part[:, 0:w], ALU.add))
                diag = slice(n * P, (n + 1) * P)
                link(V.tensor_tensor(score[n][:, diag], score[n][:, diag], mem.c("cbias"), ALU.add))
                for _ in range(TOPK // 8):
                    link(V.max(top, score[n][:, 0:w]))
                    link(V.match_replace(score[n][:, 0:w], top, score[n][:, 0:w], TAKEN))
                link(V.tensor_scalar(bias[n][:, 0:w], score[n][:, 0:w], TAKEN / 2, NEG,
                                     ALU.is_gt, ALU.mult))
                say(V.tensor_tensor(bias[n][:, diag], bias[n][:, diag], mem.c("cbias"), ALU.add),
                    "key_bias")
            att.vector(dve, nc, sig, link, say)
            att.out_of_psum(dve, nc, sig, link, mem.y[:, 8:12, :])

        @block.scalar
        def _(act):
            link, say, need = linker(act, sig, "act_ops")
            gates.begin(act, nc, sig)
            gates.scalar(act, nc, sig, 0)
            att.scalar(act, nc, sig, say)

        @block.sync
        def _(sp):
            gates.sync(sp, sig)

        @block.gpsimd
        def _(pool):
            gates.lows(pool, nc, sig)

        @block.tensor
        def _(pe):
            def need(name, n=1):
                pe.wait_ge(sig(name), n)

            for i in range(NT):
                mm = pe.matmul(tiles(0, NT)[:, i, :], mem.c("rot"), x[:, i, :], start=True, stop=True)
            mm.then_inc(sig("halves_swapped"), 1)
            need("roped", 1)
            for n in range(NBLK):
                pe.transpose(ps[:, 5, n * P:(n + 1) * P], mem.proj[:, C_V, n * P:(n + 1) * P],
                             mem.c("ident"))
                mm = pe.transpose(ps[:, 5, T + 4 * n:T + 4 * n + 4],
                                  mem.proj[0:4, C_WI, n * P:(n + 1) * P],
                                  mem.c("ident")[0:4, 0:4])
            mm.then_inc(sig("by_token"), 1)
            for n in range(NBLK):
                w = P * (n + 1)
                for j in range(4):
                    mm = pe.matmul(ps[:, 3 * n + j % 2, (j // 2) * T:(j // 2) * T + w],
                                   qi[rows(j), j // 2, n * P:(n + 1) * P], ki[rows(j), 0:w],
                                   start=True, stop=True)
                mm.then_inc(sig("dots"), 1)
            gates.tensor(pe, sig, 0)
            need("values", 2)
            need("key_bias", NBLK)
            att.tensor(pe, sig)
    sig.end()



def mla_angles_stage(nc, mem, sig, pos):
    cut = Cutter(mem.scratch)
    where, angle, turns = cut(T), cut(T), cut(T)
    whole = cut(T)
    PI2 = 2 * np.pi
    HI = float(np.float32(np.floor(PI2 * 512) / 512))
    MID = float(np.float32(np.floor((PI2 - HI) * 2 ** 21) / 2 ** 21))
    LOW = float(np.float32(PI2 - HI - MID))
    with nc.Block() as block:
        @block.sync
        def _(sp):
            sp.dma_start(where.bitcast(I32), pos.to_broadcast([P, T])).then_inc(sig("positions"), 16)

        @block.vector
        def _(dve):
            link, say, need = linker(dve, sig, "dve_ops")
            V = nc.vector
            need("positions", 16)
            link(V.tensor_copy(angle, where.bitcast(I32)))
            link(V.tensor_scalar(angle, angle, mem.const[:, CC["invf"]:CC["invf"] + 1], None, ALU.mult))
            for out, quarter in ((mem.mla_sin, 0.0), (mem.mla_cos, 0.25)):
                link(V.tensor_scalar(turns, angle, 1.0 / PI2, quarter, ALU.mult, ALU.add))
                link(V.tensor_copy(whole.bitcast(I32), turns))
                link(V.tensor_copy(turns, whole.bitcast(I32)))
                link(V.scalar_tensor_tensor(out=out[:], in0=turns, scalar=-HI, in1=angle,
                                            op0=ALU.mult, op1=ALU.add))
                link(V.scalar_tensor_tensor(out=out[:], in0=turns, scalar=-MID, in1=out[:],
                                            op0=ALU.mult, op1=ALU.add))
                link(V.scalar_tensor_tensor(out=out[:], in0=turns, scalar=-LOW, in1=out[:],
                                            op0=ALU.mult, op1=ALU.add))
                link(V.tensor_scalar(out[:], out[:], quarter * PI2, float(np.float32(3.1415925)),
                                     ALU.add, ALU.min))
                say(V.tensor_scalar(out[:], out[:], -float(np.float32(3.1415925)), None, ALU.max),
                    "reduced")

        @block.scalar
        def _(act):
            link, say, need = linker(act, sig, "act_ops")
            for n, out in enumerate((mem.mla_sin, mem.mla_cos)):
                need("reduced", n + 1)
                link(nc.scalar.activation(out[:], out[:], ACT.Sin))
    sig.end()


def in_groups_2():
    at = len(FFN_JOBS)
    groups = [[(at, 0, 8, 0, X_F), (at, 8, 8, 0, X_B)], [(at, 16, 8, 0, X_A)]]
    groups += tile_groups([(at + 1 + i // 2, (i % 2) * P, P, 0, X_DQ + i) for i in range(12)])
    groups += tile_groups([(at + 7 + i // 2, (i % 2) * P, P, 0, X_Q + i) for i in range(12)])
    groups += [[(at + 13, 0, P, 0, X_CQ), (at + 13, P, P, 0, X_CQ + 1)]]
    groups += [[(at + 14, 0, P, 0, X_CKV)], [(at + 14, P, 32, HD, X_KR)]]
    groups += tile_groups([(at + 15 + i // 2, (i % 2) * P, P, 0, X_DZ + i) for i in range(4)])
    return groups



def fox_stage(nc, mem, sig, gates):
    cut = Cutter(mem.beside_gates)
    vt, logf, size, c8 = cut(NBLK, MIX), cut(T), cut(T), cut(T)
    ps, par = mem.ps, mem.par
    f = mem.proj[0:HEADS, X_F, :]
    logf, size, c8 = (b[0:HEADS, :] for b in (logf, size, c8))
    bias = par[0:HEADS, C2["fox_b"]:C2["fox_b"] + 1]

    def rows(h):
        return slice(HD * (h % 2), HD * (h % 2) + HD)

    def add_bias(pe, o, h, n):
        pe.matmul(o[:, 0:P * (n + 1)], mem.c("ident")[0:HEADS, h:h + 1].to_broadcast([HEADS, P]),
                  c8[:, 0:P * (n + 1)], start=False, stop=False)
        return pe.matmul(o[:, n * P:(n + 1) * P], mem.c("ident"), mem.c("cbias"),
                         start=False, stop=True)

    att = Attention(mem, cut,
                    q=lambda h: mem.proj[rows(h), X_Q + h // 2, :],
                    k=lambda h: mem.proj[rows(h), X_K + h // 2, :],
                    v=lambda h, b: vt[:, b, h * HD:(h + 1) * HD],
                    scale=HD ** -0.5, bias=add_bias, gates=gates)

    with nc.Block() as block:
        @block.vector
        def _(dve):
            link, say, need = linker(dve, sig, "dve_ops")
            V = nc.vector
            link(V.tensor_scalar(f, f, bias, None, ALU.add))
            say(V.scalar_tensor_tensor(out=size, in0=f, scalar=-1.0, in1=f, op0=ALU.mult, op1=ALU.max),
                "f_size")
            need("values_turned", 1)
            say(V.tensor_copy(vt, ps[:, 0:2, :]), "values")
            need("log_term", 1)
            link(V.scalar_tensor_tensor(out=logf, in0=f, scalar=0.0, in1=size, op0=ALU.min,
                                        op1=ALU.subtract))
            link(V.tensor_tensor_scan(c8, mem.c("ones", T)[0:HEADS, :], logf, 0.0, ALU.mult, ALU.add))
            say(V.tensor_scalar(c8, c8, -float(HD ** 0.5), None, ALU.mult), "forget_sums")
            att.vector(dve, nc, sig, link, say)
            att.out_of_psum(dve, nc, sig, link, mem.y[:, 0:4, :])

        @block.scalar
        def _(act):
            link, say, need = linker(act, sig, "act_ops")
            need("f_size", 1)
            link(nc.scalar.activation(size, size, ACT.Exp, scale=-1.0))
            say(nc.scalar.activation(size, size, ACT.Ln, bias=1.0), "log_term")
            gates.high(act, nc, sig, 0)
            gates.high(act, nc, sig, 1)
            att.scalar(act, nc, sig, say)

        @block.sync
        def _(sp):
            gates.sync(sp, sig)

        @block.gpsimd
        def _(pool):
            gates.lows(pool, nc, sig)

        @block.tensor
        def _(pe):
            for n in range(NBLK):
                for i in range(MT_):
                    mm = pe.transpose(ps[:, n, i * P:(i + 1) * P],
                                      mem.proj[:, X_V + i, n * P:(n + 1) * P], mem.c("ident"))
            mm.then_inc(sig("values_turned"), 1)
            pe.wait_ge(sig("values"), 1)
            pe.wait_ge(sig("forget_sums"), 1)
            att.tensor(pe, sig)
    sig.end()



def mla_stage(nc, mem, sig, gates):
    W = HD + 32
    cut = Cutter(mem.beside_gates)
    qf, kf, vt = cut(HEADS, T), cut(HEADS, T), cut(NBLK, MIX)
    sq, rstd = cut(3, T), cut(2, T)
    ps, par = mem.ps, mem.par
    c_all = mem.proj[:, X_CQ:X_CKV + 1, :]
    kr = mem.proj[HD:W, X_KR:X_KR + 1, :]
    w_uq = mem.small_w[:, 0:1536].rearrange("p (k n) -> p k n", k=2)
    w_ukv = mem.small_w[:, 1536:2560]

    def tiles(b, n):
        return ps[:, b:b + (n + 1) // 2, :].rearrange("p a (b t) -> p (a b) t", t=T)[:, 0:n, :]

    def add_bias(pe, o, h, n):
        return pe.matmul(o[:, n * P:(n + 1) * P], mem.c("ident"), mem.c("cbias"),
                         start=False, stop=True)

    att = Attention(mem, cut, q=lambda h: qf[0:W, h, :], k=lambda h: kf[0:W, h, :],
                    v=lambda h, b: vt[:, b, h * HD:(h + 1) * HD], scale=W ** -0.5, bias=add_bias,
                    gates=gates, first_slot=2)

    with nc.Block() as block:
        @block.vector
        def _(dve):
            link, say, need = linker(dve, sig, "dve_ops")
            V = nc.vector
            say(V.tensor_tensor(sq, c_all, c_all, ALU.mult), "squares")
            need("square_sums", 1)
            link(V.tensor_scalar(rstd[:, 0, :], ps[:, 0, 0:T], 1.0 / 256, EPS, ALU.mult, ALU.add))
            say(V.tensor_scalar(rstd[:, 1, :], ps[:, 1, 0:T], 1.0 / 128, EPS, ALU.mult, ALU.add),
                "mean_squares")
            need("roots", 1)
            link(V.reciprocal(rstd, rstd))
            for i in range(3):
                g = C2["q_norm"] + i
                say(V.scalar_tensor_tensor(out=c_all[:, i, :], in0=c_all[:, i, :],
                                           scalar=par[:, g:g + 1], in1=rstd[:, i // 2, :],
                                           op0=ALU.mult, op1=ALU.mult), "latents")
            need("queries_out", 1)
            need("queries_swapped", 1)
            rope(V, link, say, qf[0:W], tiles(4, HEADS)[0:W], mem.mla_cos[0:W, :],
                 mem.mla_sin[0:W, :], "roped")
            need("key_swapped", 1)
            rope(V, link, say, kr, ps[HD:W, 0:1, 0:T], mem.mla_cos[HD:W, :], mem.mla_sin[HD:W, :],
                 "roped")
            say(V.tensor_copy(kf[HD:W], kr.to_broadcast([32, HEADS, T])), "keys")
            need("keys_summed", 1)
            say(V.tensor_copy(kf[0:HD], tiles(4, HEADS)[0:HD]), "keys")
            need("values_summed", 1)
            say(V.tensor_copy(vt, ps[:, 1:3, :]), "values")
            att.vector(dve, nc, sig, link, say)
            att.out_of_psum(dve, nc, sig, link, mem.y[:, 4:8, :])

        @block.scalar
        def _(act):
            link, say, need = linker(act, sig, "act_ops")
            need("mean_squares", 1)
            say(nc.scalar.activation(rstd, rstd, ACT.Sqrt), "roots")
            gates.high(act, nc, sig, 0)
            need("queries_summed", 1)
            say(nc.scalar.copy(qf[0:W], tiles(0, HEADS)[0:W]), "queries_out")
            gates.high(act, nc, sig, 1)
            gates.scalar(act, nc, sig, 0)
            gates.scalar(act, nc, sig, 1)
            att.scalar(act, nc, sig, say)

        @block.sync
        def _(sp):
            gates.sync(sp, sig)

        @block.gpsimd
        def _(pool):
            gates.lows(pool, nc, sig)

        @block.tensor
        def _(pe):
            def need(name, n=1):
                pe.wait_ge(sig(name), n)

            need("squares", 1)
            for i in range(3):
                mm = pe.matmul(ps[:, i // 2, 0:T], mem.c("ones"), sq[:, i, :],
                               start=(i != 1), stop=(i != 0))
            mm.then_inc(sig("square_sums"), 1)
            need("latents", 3)
            for h in range(HEADS):
                for k in range(2):
                    mm = pe.matmul(tiles(0, HEADS)[0:W, h, :], w_uq[:, k, h * W:(h + 1) * W],
                                   c_all[:, k, :], start=(k == 0), stop=(k == 1))
            mm.then_inc(sig("queries_summed"), 1)
            need("queries_out", 1)
            for h in range(HEADS):
                mm = pe.matmul(tiles(4, HEADS)[0:W, h, :], mem.c("rotm")[0:W, 0:W], qf[0:W, h, :],
                               start=True, stop=True)
            mm.then_inc(sig("queries_swapped"), 1)
            pe.matmul(ps[HD:W, 0, 0:T], mem.c("rotm")[HD:W, HD:W], kr[:, 0, :], start=True,
                      stop=True).then_inc(sig("key_swapped"), 1)
            for n in range(NBLK):
                mm = pe.matmul(ps[:, 1 + n, :], c_all[:, 2, n * P:(n + 1) * P],
                               w_ukv.rearrange("p (h a d) -> p h a d", h=HEADS, a=2)[:, :, 1, :],
                               start=True, stop=True)
            mm.then_inc(sig("values_summed"), 1)
            gates.tensor(pe, sig, 0)
            need("roped", 1)
            for h in range(HEADS):
                mm = pe.matmul(tiles(4, HEADS)[0:HD, h, :], w_ukv[:, h * P:h * P + HD],
                               c_all[:, 2, :], start=True, stop=True)
            mm.then_inc(sig("keys_summed"), 1)
            gates.tensor(pe, sig, 1)
            need("keys", 2)
            need("values", 1)
            att.tensor(pe, sig)
    sig.end()



class Delta:

    def __init__(self, nc, mem, sig):
        self.nc, self.mem, self.sig = nc, mem, sig
        cut = Cutter(mem.scratch)
        self.z = [cut(MT_, T) for _ in range(7)]
        self.kq = cut(MT_, NBLK, 2, P)
        self.vt, self.kt, self.qh, self.kh = cut(NBLK, MIX), cut(MIX), cut(MT_, P), cut(MT_, P)
        self.vnew, self.rhs, self.state = cut(MIX), cut(MIX), cut(MT_, HD)
        self.cols, self.rows = cut(2, NBLK, HEADS), cut(4, T)
        self.x = mem.proj[:, X_DQ:X_DZ, :]
        self.q, self.k, self.v, self.dz = (mem.proj[:, i:i + 4, :] for i in (X_DQ, X_DK, X_DV, X_DZ))
        self.conv = mem.scratch[:, 0:12 * T].rearrange("p (a t) -> p a t", a=12)
        self.squares = self.z[3:5]
        self.beta, self.decay = mem.proj[0:HEADS, X_B, :], mem.proj[0:HEADS, X_A, :]
        self.size, self.gsum, self.egsum = (self.rows[0:HEADS, i, :] for i in range(3))
        self.ea = self.rows[0:HEADS, 3, 0:1]
        self.vector = {4: [self.gate_sizes], 7: [self.gate_sums], 14: [self.unit_q, self.sum_k],
                       16: [self.unit_k, self.columns], "end": [self.operands, self.by_token]}
        self.scalar = {3: [self.gate_logs], 8: [self.gate_exp], 11: [], 13: [self.root_k],
                       "end": []}
        self.tensor = {5: [self.beta_spread], 9: [self.square_sum_q], 11: [self.square_sum_k],
                       12: [self.gate_spread], 15: [self.turn_v], "end": [self.turn_k]}
        for p in range(6):
            self.vector.setdefault(5 + p, []).append(self.of_pair(self.convolve, p))
            self.vector.setdefault(8 + p, []).append(self.of_pair(self.silu, p))
            self.scalar.setdefault(6 + p, []).append(self.of_pair(self.silu_gate, p))
        self.vector[9].append(self.square_q)
        self.vector[11].append(self.square_k)
        self.vector[12].append(self.sum_q)
        self.scalar[11].append(self.root_q)

    @staticmethod
    def of_pair(step, p):
        return lambda link, say, need: step(p, link, say, need)

    def two(self, b):
        return self.mem.ps[:, b:b + 2, :].rearrange("p a (b t) -> p (a b) t", t=T)

    def par8(self, name):
        return self.mem.par[0:HEADS, C2[name]:C2[name] + 1]


    def gate_sizes(self, link, say, need):
        V, decay = self.nc.vector, self.decay
        need("bank_free", 2)
        link(V.tensor_scalar(decay, decay, self.par8("dt_bias"), None, ALU.add))
        say(V.scalar_tensor_tensor(out=self.size, in0=decay, scalar=-1.0, in1=decay,
                                   op0=ALU.mult, op1=ALU.max), "a_size")

    def gate_sums(self, link, say, need):
        V, size = self.nc.vector, self.size
        need("log_term", 1)
        link(V.scalar_tensor_tensor(out=size, in0=self.decay, scalar=0.0, in1=size, op0=ALU.max,
                                    op1=ALU.add))
        link(V.tensor_scalar(size, size, self.ea, -1.0, ALU.mult, ALU.mult))
        for n in range(NBLK):
            at = slice(n * P, (n + 1) * P)
            say(V.tensor_tensor_scan(self.gsum[:, at], self.mem.c("ones", T)[0:HEADS, at],
                                     size[:, at], 0.0, ALU.mult, ALU.add), "gate_sums")

    def convolve(self, p, link, say, need):
        V, x, conv, par = self.nc.vector, self.x, self.conv, self.mem.par
        need("bank_free", 2 + p + 1)
        for i in (2 * p, 2 * p + 1):
            tap = C2["dn_conv"] + i
            link(V.tensor_scalar(conv[:, i, :], x[:, i, :], par[:, tap + 36:tap + 37], None, ALU.mult))
            for lag in (1, 2, 3):
                w = tap + 12 * (3 - lag)
                ins = V.scalar_tensor_tensor(out=conv[:, i, lag:T], in0=x[:, i, 0:T - lag],
                                             scalar=par[:, w:w + 1], in1=conv[:, i, lag:T],
                                             op0=ALU.mult, op1=ALU.add)
                if lag == 3:
                    say(ins, "convolved")
                else:
                    link(ins)

    def silu(self, p, link, say, need):
        need("silu_gate", p + 1)
        x, conv = (flat(t[:, 2 * p:2 * p + 2, :]) for t in (self.x, self.conv))
        say(self.nc.vector.tensor_tensor(x, x, conv, ALU.mult), "activated")

    def square_q(self, link, say, need):
        say(self.nc.vector.tensor_tensor(flat(self.squares[0]), flat(self.q), flat(self.q), ALU.mult),
            "q_squares")

    def square_k(self, link, say, need):
        say(self.nc.vector.tensor_tensor(flat(self.squares[1]), flat(self.k), flat(self.k), ALU.mult),
            "k_squares")

    def sum_q(self, link, say, need):
        need("q_square_sums", 1)
        say(self.nc.vector.tensor_scalar(self.squares[0], self.two(2), EPS, None, ALU.add), "q_sums")

    def sum_k(self, link, say, need):
        need("k_square_sums", 1)
        say(self.nc.vector.tensor_scalar(self.squares[1], self.two(4), EPS, None, ALU.add), "k_sums")

    def unit_q(self, link, say, need):
        need("q_root", 1)
        self.unit(self.q, self.squares[0], HD ** -0.5, link, say)

    def unit_k(self, link, say, need):
        need("k_root", 1)
        self.unit(self.k, self.squares[1], 1.0, link, say)

    def unit(self, x, root, factor, link, say):
        V = self.nc.vector
        link(V.reciprocal(flat(root), flat(root)))
        say(V.scalar_tensor_tensor(out=flat(x), in0=flat(x), scalar=factor, in1=flat(root),
                                   op0=ALU.mult, op1=ALU.mult), "unit")

    def columns(self, link, say, need):
        V, cols = self.nc.vector, self.cols
        need("columns_turned", 1)
        src = self.mem.ps[:, 3, 0:4 * HEADS].rearrange("p (a n h) -> p a n h", a=2, n=NBLK)
        link(V.tensor_scalar(cols[:, 0, :, :], src[:, 0, :, :], -1.0, None, ALU.mult))
        link(V.tensor_copy(cols[:, 1, :, :], src[:, 1, :, :]))

    def operands(self, link, say, need):
        V, kq, b1 = self.nc.vector, self.kq, slice(P, T)
        need("beta_spread", 1)
        kq5 = kq.rearrange("p a n w t -> p (a n) w t")
        say(V.scalar_tensor_tensor(out=kq5[:, :, 0, :],
                                   in0=flat(self.k).rearrange("p (a t) -> p a t", t=P), scalar=-1.0,
                                   in1=self.mem.ps[:, 6:8, :].rearrange("p a (b t) -> p (a b) t", t=P),
                                   op0=ALU.mult, op1=ALU.mult), "beta_keys")
        link(V.tensor_copy(kq5[:, :, 1, :], flat(self.q).rearrange("p (a t) -> p a t", t=P)))
        spread = self.mem.ps[:, 2, :].rearrange("p (a t) -> p a t", a=MT_)
        link(V.tensor_tensor(self.kh, kq[:, :, 1, 0, :], spread, ALU.mult))
        link(V.tensor_tensor(self.qh, self.q[:, :, b1], spread, ALU.mult))

    def by_token(self, link, say, need):
        V = self.nc.vector
        need("v_turned", 1)
        beta_t = self.cols[:, 1, :, :].rearrange("p n h -> p (n h)").unsqueeze(2)
        link(V.tensor_tensor(flat(self.vt).rearrange("p (h d) -> p h d", d=HD),
                             self.mem.ps[:, 4:6, :].rearrange("p a (h d) -> p (a h) d", d=HD),
                             beta_t.to_broadcast([P, 16, HD]), ALU.mult))
        need("k_turned", 1)
        link(V.tensor_copy(self.kt, self.mem.ps[:, 6, :]))


    def gate_logs(self, link, say, need):
        A, size = self.nc.scalar.activation, self.size
        need("a_size", 1)
        link(A(self.ea, self.par8("a_log"), ACT.Exp))
        link(A(size, size, ACT.Exp, scale=-1.0))
        say(A(size, size, ACT.Ln, bias=1.0), "log_term")
        say(A(self.beta, self.beta, ACT.Sigmoid), "beta")

    def gate_exp(self, link, say, need):
        need("gate_sums", NBLK)
        say(self.nc.scalar.activation(self.egsum, self.gsum, ACT.Exp), "gate_exp")

    def silu_gate(self, p, link, say, need):
        need("convolved", 2 * (p + 1))
        x, conv = (flat(t[:, 2 * p:2 * p + 2, :]) for t in (self.x, self.conv))
        say(self.nc.scalar.activation(x, conv, ACT.Sigmoid), "silu_gate")

    def root_q(self, link, say, need):
        need("q_sums", 1)
        x = flat(self.squares[0])
        say(self.nc.scalar.activation(x, x, ACT.Sqrt), "q_root")

    def root_k(self, link, say, need):
        need("k_sums", 1)
        x = flat(self.squares[1])
        say(self.nc.scalar.activation(x, x, ACT.Sqrt), "k_root")


    def head_sums(self, pe, b, src, name):
        for i in range(2):
            mm = pe.matmul(self.mem.ps[:, b + i, :], self.mem.c("bones"),
                           flat(src[:, 2 * i:2 * i + 2, :]), start=True, stop=True)
        mm.then_inc(self.sig(name), 1)

    def square_sum_q(self, pe, need):
        need("q_squares", 1)
        self.head_sums(pe, 2, self.squares[0], "q_square_sums")

    def square_sum_k(self, pe, need):
        need("k_squares", 1)
        self.head_sums(pe, 4, self.squares[1], "k_square_sums")

    def beta_spread(self, pe, need):
        need("beta", 1)
        for i in range(MT_):
            mm = pe.matmul(self.two(6)[:, i, :],
                           self.mem.c("hsel", MT_ * P)[0:HEADS, i * P:(i + 1) * P], self.beta,
                           start=True, stop=True)
        mm.then_inc(self.sig("beta_spread"), 1)

    def gate_spread(self, pe, need):
        ps, mem = self.mem.ps, self.mem
        need("gate_exp", 1)
        need("q_sums", 1)
        for i in range(MT_):
            pe.matmul(ps[:, 2, i * P:(i + 1) * P],
                      mem.c("hsel", MT_ * P)[0:HEADS, i * P:(i + 1) * P], self.egsum[:, P:T],
                      start=True, stop=True)
        for w, src in enumerate((self.gsum, self.beta)):
            for n in range(NBLK):
                at = (w * NBLK + n) * HEADS
                mm = pe.transpose(ps[:, 3, at:at + HEADS], src[:, n * P:(n + 1) * P],
                                  mem.c("ident")[0:HEADS, 0:HEADS])
        mm.then_inc(self.sig("columns_turned"), 1)

    def turn_v(self, pe, need):
        need("k_sums", 1)
        need("activated", 6)
        for i in range(MT_):
            for n in range(NBLK):
                mm = pe.transpose(self.mem.ps[:, 4 + n, i * P:(i + 1) * P],
                                  self.v[:, i, n * P:(n + 1) * P], self.mem.c("ident"))
        mm.then_inc(self.sig("v_turned"), 1)

    def turn_k(self, pe, need):
        need("unit", 2)
        need("beta_keys", 1)
        for i in range(MT_):
            mm = pe.transpose(self.mem.ps[:, 6, i * P:(i + 1) * P], self.k[:, i, 0:P],
                              self.mem.c("ident"))
        mm.then_inc(self.sig("k_turned"), 1)


def delta_stage(nc, mem, sig, delta, gates):
    z, kq, vt, kt, qh, kh = delta.z, delta.kq, delta.vt, delta.kt, delta.qh, delta.kh
    vnew, rhs, state, cols, gsum = delta.vnew, delta.rhs, delta.state, delta.cols, delta.gsum
    k, dz, two, ps, par = delta.k, delta.dz, delta.two, mem.ps, mem.par
    out = mem.y[:, 8:12, :]
    mt, t_, tt, xx, c, qk, dec = (
        zi.rearrange("p a t -> p (a t)").rearrange("p (h t) -> p h t", h=HEADS) for zi in z)
    solver = Solver(mem, mt, t_, tt, xx, c)

    def hp(s):
        return slice(HD * (s // 4), HD * (s // 4) + HD)

    def head(s):
        return 2 * (s % 4) + s // 4

    with nc.Block() as block:
        @block.sync
        def _(sp):
            gates.sync(sp, sig)

        @block.vector
        def _(dve):
            link, say, need = linker(dve, sig, "dve_ops")
            V = nc.vector
            for n in range(NBLK):
                need("decay", 8 * (n + 1))
                for w, dst in enumerate((mt, qk)):
                    for i, j in enumerate(BANK_ORDER):
                        need("pairs_summed", 4 * n + i + 1)
                        hs = slice(2 * j, 2 * j + 2)
                        src = ps[:, 4 + j, :].rearrange("p (h w t) -> p h w t", h=2, w=2)
                        ins = V.tensor_tensor(dst[:, hs, :], src[:, :, w, :], dec[:, hs, :], ALU.mult)
                        if j == 3:
                            say(ins, ("mt_ready", "masked")[w])
                        else:
                            link(ins)
                if n == 0:
                    kt4 = kt.rearrange("p (a b d) -> p b a d", a=4, b=2)
                    for b in range(2):
                        ins = V.tensor_tensor(kt4[:, b, :, :], kt4[:, b, :, :],
                                              dec[:, 4 * b:4 * b + 4, P - 1:P].to_broadcast([P, 4, HD]),
                                              ALU.mult)
                        say(ins, "keys_to_end")
                solver.vector(dve, nc, sig, n, link, say)
                vb = vt[:, n, :].rearrange("p (a b d) -> p b a d", a=4, b=2)
                r4 = rhs.rearrange("p (b a d) -> p b a d", b=2, a=4)
                for b in range(2):
                    if n == 0:
                        say(V.tensor_copy(r4[:, b, :, :], vb[:, b, :, :]), "rhs")
                    else:
                        need("seen_summed", 1)
                        src = ps[:, 6 + b, 0:T].rearrange("p (a d) -> p a d", a=4)
                        say(V.tensor_tensor(r4[:, b, :, :], vb[:, b, :, :], src, ALU.add), "rhs")
                need("new_summed", n + 1)
                say(V.tensor_copy(vnew, ps[:, 4, :]), "new")
                need("out_summed", n + 1)
                say(V.tensor_copy(out[:, :, n * P:n * P + P],
                                  ps[:, 0, :].rearrange("p (a t) -> p a t", a=MT_)), "out")
                if n == 0:
                    need("state_summed", 1)
                    say(V.tensor_copy(flat(state), ps[:, 1, 0:MT_ * HD]), "state")
            say(V.tensor_tensor(z[0], out, out, ALU.mult), "out_squares")
            need("out_square_sums", 1)
            say(V.tensor_scalar(z[0], two(2), 1.0 / HD, EPS, ALU.mult, ALU.add), "out_mean")
            need("out_root", 1)
            link(V.reciprocal(flat(z[0]), flat(z[0])))
            link(V.tensor_tensor(out, out, z[0], ALU.mult))
            link(V.tensor_tensor(flat(z[1]), flat(z[1]), flat(dz), ALU.mult))
            link(V.scalar_tensor_tensor(out=out.rearrange("p a t -> p (a t)"),
                                        in0=out.rearrange("p a t -> p (a t)"),
                                        scalar=par[:, C2["o_norm"]:C2["o_norm"] + 1],
                                        in1=flat(z[1]), op0=ALU.mult, op1=ALU.mult))

        @block.scalar
        def _(act):
            link, say, need = linker(act, sig, "act_ops")
            A = nc.scalar.activation
            for n in range(NBLK):
                if n:
                    need("masked", n)
                    need("keys_to_end", 2)
                for s in range(HEADS):
                    need("rows_spread", n * 2 + s // 4 + 1)
                    say(A(dec[:, s, :], ps[:, 2 + s // 4, (s % 4) * P:(s % 4 + 1) * P], ACT.Exp,
                          bias=cols[:, 0, n, head(s):head(s) + 1]), "decay")
                gates.high(act, nc, sig, n)
                solver.scalar(act, nc, sig, n)
            need("out_summed", 2)
            say(A(flat(z[1]), flat(dz), ACT.Sigmoid), "z_sigmoid")
            gates.scalar(act, nc, sig, 0)
            need("out_mean", 1)
            say(A(flat(z[0]), flat(z[0]), ACT.Sqrt), "out_root")
            gates.scalar(act, nc, sig, 1)
            gates.end(act, nc, sig)

        @block.gpsimd
        def _(pool):
            for n in range(NBLK):
                solver.pool(pool, nc, sig, n)
            gates.lows(pool, nc, sig)

        @block.tensor
        def _(pe):
            def need(name, n=1):
                pe.wait_ge(sig(name), n)

            for n in range(NBLK):
                if n:
                    need("state", 1)
                for s in range(HEADS):
                    o = ps[:, 2 + s // 4, (s % 4) * P:(s % 4 + 1) * P]
                    h = head(s)
                    pe.matmul(o, mem.c("ident")[0:HEADS, h:h + 1].to_broadcast([HEADS, P]),
                              gsum[:, n * P:(n + 1) * P], start=True, stop=False)
                    mm = pe.matmul(o, mem.c("ident"), mem.c("cbiasT"), start=False, stop=True)
                    if s % 4 == 3:
                        mm.then_inc(sig("rows_spread"), 1)
                for s in HEAD_ORDER:
                    mm = pe.matmul(ps[:, 4 + s // 2, (s % 2) * T:(s % 2 + 1) * T],
                                   k[hp(s), s % 4, n * P:(n + 1) * P],
                                   kq[hp(s), s % 4, n, :, :].rearrange("p w t -> p (w t)"),
                                   start=True, stop=True)
                    if s % 2:
                        mm.then_inc(sig("pairs_summed"), 1)
                solver.tensor(pe, sig, n)
                if n:
                    for s in range(HEADS):
                        mm = pe.matmul(ps[:, 6 + s // 4, (s % 4) * HD:(s % 4 + 1) * HD],
                                       kh[hp(s), s % 4, :], state[hp(s), s % 4, :],
                                       start=True, stop=True)
                    mm.then_inc(sig("seen_summed"), 1)
                need("rhs", 2 * (n + 1))
                need("t_ready", 2 * len(LEVELS) * (n + 1))
                for s in range(HEADS):
                    mm = pe.matmul(ps[:, 4, s * HD:(s + 1) * HD], tt[:, s, :],
                                   rhs[:, s * HD:(s + 1) * HD], start=True, stop=True)
                mm.then_inc(sig("new_summed"), 1)
                need("new", n + 1)
                for s in range(HEADS):
                    o = ps[hp(s), 0, (s % 4) * P:(s % 4 + 1) * P]
                    mm = pe.matmul(o, vnew[:, s * HD:(s + 1) * HD], qk[:, s, :], start=True,
                                   stop=(n == 0))
                    if n:
                        mm = pe.matmul(o, state[hp(s), s % 4, :], qh[hp(s), s % 4, :],
                                       start=False, stop=True)
                mm.then_inc(sig("out_summed"), 1)
                if n == 0:
                    need("keys_to_end", 2)
                    for s in range(HEADS):
                        h = head(s)
                        mm = pe.matmul(ps[hp(s), 1, (s % 4) * HD:(s % 4 + 1) * HD],
                                       kt[:, h * HD:(h + 1) * HD], vnew[:, s * HD:(s + 1) * HD],
                                       start=True, stop=True)
                    mm.then_inc(sig("state_summed"), 1)
            gates.tensor(pe, sig, 0)
            need("out_squares", 1)
            delta.head_sums(pe, 2, z[0], "out_square_sums")
            gates.tensor(pe, sig, 1)
    sig.end()


def in_groups():
    groups = tile_groups([(i // 2, (i % 2) * P, P, 0, i) for i in range(C_WI)])
    return groups + [[(C_WI // 2, 0, 4, 0, C_WI)]]


RWKV_SLOTS = (1, 1, 4)
HGRN_SLOTS = (2,) + (1, 1, 0) * 2 + (1, 0, 0, 2, 1)
DSA_SLOTS = (4,) + (1, 0, 0) * 4
DELTA_SLOTS = (1, 5)
FOX_SLOTS = (1, 1, 0) * 4
MLA_SLOTS = (1, 1) + (1, 0) * 8


def hybrid_blocks(nc, w1, w2, par1, par2, small1, small2, xt, const, pos, out):
    with ExitStack() as ctx:
        mem = Memory(nc, ctx)
        full = [ctx.enter_context(nc.semaphore("slot_full_%d" % i)) for i in range(RING)]
        sig = Signals(nc)

        def clear_ring():
            nc.all_engine_barrier(sems_to_clear=range(full[0].num, full[-1].num + 1))

        def row(ap, layer):
            return ap[bass.ds(layer, 1)].rearrange("a p n -> (a p) n")

        with nc.Block() as block:
            @block.sync
            def _(sp):
                sp.dma_start(mem.h[:], xt).then_inc(sig("loaded"), 16)
                sp.dma_start(mem.const[:], const).then_inc(sig("loaded"), 16)
                sp.wait_ge(sig("loaded"), 32)
        sig.end()

        with nc.Fori(0, DEPTH) as layer:
            stream = Stream(mem, w1, JOBS1, full)
            loads = [lambda sp: sp.dma_start(mem.par[:, 0:N_PAR1], row(par1, layer)),
                     lambda sp: sp.dma_start(mem.small_w[:, 0:2 * MIX], row(small1, layer))]
            rwkv = Rwkv(nc, mem, sig)
            project_stage(nc, mem, sig, stream, layer, in_groups(), 0, C1["mix_g"], loads,
                          rwkv)
            rwkv_stage(nc, mem, sig, rwkv,
                       Gates(mem, stream, layer, GATES_AT1, 0, 3, (1, 6, 7), RWKV_SLOTS))
            hgrn_stage(nc, mem, sig,
                       Gates(mem, stream, layer, GATES_AT1, 3, 8, (2, 3), HGRN_SLOTS))
            dsa_stage(nc, mem, sig,
                      Gates(mem, stream, layer, GATES_AT1, 8, GATE_JOBS, (2, 7), DSA_SLOTS))
            merge_stage(nc, mem, sig, stream, layer, GATES_AT1 + GATE_JOBS, None)
            ffn_stage(nc, mem, sig, stream, layer, FFN_AT1, C1["ffn_g"],
                      (C1["conv_w"], C1["conv_b"]), 1.0)
            clear_ring()
        final_norm_stage(nc, mem, sig, C1["fin_g"])
        mla_angles_stage(nc, mem, sig, pos)
        with nc.Fori(0, DEPTH) as layer:
            stream = Stream(mem, w2, JOBS2, full)
            loads = [lambda sp: sp.dma_start(mem.par[:, 0:N_PAR2], row(par2, layer)),
                     lambda sp: sp.dma_start(mem.small_w[:], row(small2, layer))]
            ffn_stage(nc, mem, sig, stream, layer, 0, C2["ffn1_g"], None, 0.5, loads)
            delta = Delta(nc, mem, sig)
            project_stage(nc, mem, sig, stream, layer, in_groups_2(), len(FFN_JOBS), C2["mix_g"],
                          [], delta)
            delta_stage(nc, mem, sig, delta,
                        Gates(mem, stream, layer, GATES_AT2, 0, 3, (1, 6, 7), DELTA_SLOTS))
            fox_stage(nc, mem, sig, Gates(mem, stream, layer, GATES_AT2, 3, 7, (2, 7), FOX_SLOTS))
            mla_stage(nc, mem, sig,
                      Gates(mem, stream, layer, GATES_AT2, 7, GATE_JOBS, (2, 7), MLA_SLOTS, (3, 3)))
            merge_stage(nc, mem, sig, stream, layer, GATES_AT2 + GATE_JOBS, C2["b_gate"])
            ffn_stage(nc, mem, sig, stream, layer, FFN_AT2, C2["ffn2_g"], None, 0.5)
            clear_ring()
        final_norm_stage(nc, mem, sig, C2["fin_g"], store=out)
    return mem



def cols_of(v):
    v = np.asarray(v)
    return v.reshape(-1, P).T


def job_block(w, cols=None):
    w = w if cols is None else np.concatenate([w[:, a:b] for a, b in cols], axis=1)
    k, n = w.shape
    return w.reshape(k // P, P, n).transpose(1, 0, 2).reshape(P, -1)


def fill(dst, src):
    dst[:, :src.shape[1]] = src


def column_jobs(w, a, b):
    return [job_block(w, [(x, x + 2 * P)]) for x in range(a, b, 2 * P)]


def merge_jobs(branches, w_out):
    halves = [job_block(w, [(a, a + 512)]) for w in branches for a in (0, 512)]
    return halves + column_jobs(w_out, 0, D)


def ffn_jobs(up, down):
    pairs = [job_block(up, [(j, j + P), (D_FF + j, D_FF + j + P)]) for j in range(0, D_FF, P)]
    return pairs + [job_block(down[a:a + 2 * P]) for a in range(0, D_FF, 2 * P)]


def pack_block1(i):
    w1 = np.zeros((DEPTH, len(JOBS1), P, SLOT), np.float32)
    par = np.zeros((DEPTH, P, N_PAR1), np.float32)
    small = np.zeros((DEPTH, P, 2 * MIX), np.float32)
    c0, gate0 = 1792 + 2048, 1792 + 2048 + 1092
    for l in range(DEPTH):
        w = i["w_in"][l]
        jobs = column_jobs(w, 0, c0 + 512)
        k, v, qi, ki, wi = c0 + 512, c0 + 640, c0 + 768, c0 + 1024, c0 + 1088
        jobs += [job_block(w, [(k, k + 64)] * 2 + [(k + 64, k + 128)] * 2)]
        jobs += [job_block(w, [(qi, qi + 256)])]
        jobs += [job_block(w, [(ki, ki + 64)] * 2 + [(v, v + 128)])]
        jobs += [job_block(w, [(wi, wi + 4)])]
        jobs += column_jobs(w, gate0, gate0 + 3072)
        jobs += merge_jobs([i["w_branch"][l, n] for n in range(3)], i["w_o"][l])
        jobs += ffn_jobs(i["w_up"][l], i["w_down"][l])
        assert len(jobs) == len(JOBS1)
        for g, job in enumerate(jobs):
            fill(w1[l, g], job)
        table = {"mix_g": i["norm_mix_g"][l], "mu": i["a_mu"][l], "w0": i["a_w0"][l],
                 "a0": i["a_a0"][l], "k_k": i["a_k_k"][l], "k_a": i["a_k_a"][l],
                 "r_k": i["a_r_k"][l].reshape(-1), "gn_g": i["a_gn_g"][l], "gn_b": i["a_gn_b"][l],
                 "lb0": i["b_lb_logits"][0], "lb1": i["b_lb_logits"][1], "b_gn_g": i["b_gn_g"][l],
                 "ffn_g": i["norm_ffn_g"][l], "conv_w": i["conv_w"][l].reshape(-1),
                 "conv_b": i["conv_b"][l], "fin_g": i["norm_final_g"]}
        for name, v in table.items():
            fill(par[l, :, C1[name]:], cols_of(v))
        par[l, :, C1["layer"]] = float(l)
        small[l, 0:HD, 0:MIX] = i["a_w_up"][l]
        small[l, HD:P, 0:MIX] = i["a_a_up"][l]
        small[l, :, MIX:] = i["a_g_up"][l]
    return w1, par, small


def pack_block2(i):
    w2 = np.zeros((DEPTH, len(JOBS2), P, SLOT), np.float32)
    par = np.zeros((DEPTH, P, N_PAR2), np.float32)
    small = np.zeros((DEPTH, P, 2560), np.float32)
    for l in range(DEPTH):
        w = i["w_in_2"][l]
        jobs = ffn_jobs(i["ffn1_w_gu_2"][l], i["ffn1_w_down_2"][l])
        jobs += [job_block(w, [(1536, 1544), (4008, 4024)])]
        jobs += column_jobs(w, 1960, 3496)
        jobs += column_jobs(w, 0, 1536)
        jobs += [job_block(w, [(1544, 1800)]), job_block(w, [(1800, 1960)])]
        jobs += column_jobs(w, 3496, 4008)
        jobs += column_jobs(w, 4024, 7096)
        jobs += merge_jobs([i[n][l] for n in ("w_br_fox_2", "w_br_mla_2", "w_br_dn_2")],
                           i["w_out_2"][l])
        jobs += ffn_jobs(i["ffn2_w_gu_2"][l], i["ffn2_w_down_2"][l])
        assert len(jobs) == len(JOBS2)
        for g, job in enumerate(jobs):
            fill(w2[l, g], job)
        table = {"ffn1_g": i["ffn1_norm_2"][l], "mix_g": i["mix_norm_2"][l],
                 "ffn2_g": i["ffn2_norm_2"][l], "fin_g": i["final_norm_2"],
                 "b_gate": i["b_gate_2"][l], "q_norm": i["mla_q_norm_2"][l],
                 "kv_norm": i["mla_kv_norm_2"][l], "dn_conv": i["dn_conv_w_2"][l].reshape(-1)}
        for name, v in table.items():
            fill(par[l, :, C2[name]:], cols_of(v))
        par[l, 0:HD, C2["o_norm"]] = i["dn_o_norm_2"][l]
        par[l, HD:P, C2["o_norm"]] = i["dn_o_norm_2"][l]
        par[l, 0:HEADS, C2["fox_b"]] = i["fox_b_f_2"][l]
        par[l, 0:HEADS, C2["a_log"]] = i["dn_a_log_2"][l]
        par[l, 0:HEADS, C2["dt_bias"]] = i["dn_dt_bias_2"][l]
        fill(small[l], job_block(i["mla_w_uq_2"][l]))
        small[l, :, 1536:] = i["mla_w_ukv_2"][l]
    return w2, par, small


def kernel(**inputs):
    import concourse.bacc as bacc
    from concourse.bass_utils import run_bass_kernel_spmd as run

    i = {k: np.asarray(v) for k, v in inputs.items()}
    w1, par1, small1 = pack_block1(i)
    w2, par2, small2 = pack_block2(i)
    xt = np.ascontiguousarray(i["x"][0].T.reshape(KT, P, T).transpose(1, 0, 2))
    pos = np.ascontiguousarray(i["positions_2"].astype(np.int32))
    arrays = {"w1": w1, "w2": w2, "par1": par1, "par2": par2, "small1": small1, "small2": small2,
              "xt": xt, "const": const_array(), "pos": pos}
    nc = bacc.Bacc("TRN2", target_bir_lowering=False, num_devices=1)
    aps = [nc.dram_tensor(n, a.shape, mybir.dt.from_np(a.dtype), kind="ExternalInput").ap()
           for n, a in arrays.items()]
    out = nc.dram_tensor("out", (P, KT, T), F32, kind="ExternalOutput").ap()
    hybrid_blocks(nc, *aps, out)
    got = run(nc, [arrays], core_ids=[0]).results[0]["out"]
    return np.ascontiguousarray(got.transpose(1, 0, 2).reshape(D, T).T)[None]
```
